# Optimizing a Trainium2 kernel written in Bass

```python
import math
import jax, jax.numpy as jnp
from jax import lax
import numpy as np
import jax
import jax.numpy as jnp

D_MODEL = 1024
BATCH = 1
SEQ = 256
DEPTH = 1

HEAD_DIM = 64
ATTN_HEADS_PER_GROUP = 8
DILATED_GROUPS = ((128, 1), (512, 4), (2048, 16))
N_GROUPS = 3
ATTN_WIDTH = ATTN_HEADS_PER_GROUP * HEAD_DIM
N_ATTN_HEADS = N_GROUPS * ATTN_HEADS_PER_GROUP
QBLOCK = 128
N_BUCKETS = 32
MAX_DISTANCE = 2048
RWKV_HEADS = 8
RWKV_HEAD_SIZE = 64
RWKV_WIDTH = RWKV_HEADS * RWKV_HEAD_SIZE
DECAY_LORA = 64
AAA_LORA = 64
GN_EPS = 64e-5
RMS_EPS = 1e-6

QKV_COLS = 3 * N_GROUPS * ATTN_WIDTH
OFF_ATTN_GATE = QKV_COLS
OFF_RWKV = OFF_ATTN_GATE + ATTN_WIDTH
RWKV_SHIFT_COLS = 3 * RWKV_WIDTH + DECAY_LORA + AAA_LORA
OFF_RWKV_GATE = OFF_RWKV + RWKV_SHIFT_COLS
OFF_MERGE = OFF_RWKV_GATE + RWKV_WIDTH
IN_COLS = OFF_MERGE + 2 * D_MODEL


def rms_norm(x, g):
    xf = x.astype(jnp.float32)
    y = xf * lax.rsqrt(jnp.mean(xf * xf, axis=-1, keepdims=True) + RMS_EPS) * g.astype(jnp.float32)
    return y.astype(x.dtype)

def t5_causal_bucket(dist):
    d = np.maximum(np.asarray(dist), 0)
    max_exact = N_BUCKETS // 2
    ratio = np.log(np.maximum(d, 1).astype(np.float32) / max_exact) / np.float32(math.log(MAX_DISTANCE / max_exact))
    large = max_exact + (ratio * (N_BUCKETS - max_exact)).astype(np.int32)
    large = np.minimum(large, N_BUCKETS - 1)
    return np.where(d < max_exact, d, large).astype(np.int32)

def dilated_group_attention(q, k, v, bias_table_g, window, dilation):
    B, S, H, Dh = q.shape
    L = S // dilation
    steps = window // dilation
    nb = -(-L // QBLOCK)
    Lp = nb * QBLOCK

    def to_blocks(t):
        t = t.reshape(B, L, dilation, H, Dh).transpose(0, 2, 3, 1, 4)
        t = jnp.pad(t, ((0, 0), (0, 0), (0, 0), (0, Lp - L), (0, 0)))
        return t.reshape(B, dilation, H, nb, QBLOCK, Dh)

    def with_prev(t):
        prev = jnp.pad(t, ((0, 0), (0, 0), (0, 0), (1, 0), (0, 0), (0, 0)))[:, :, :, :-1]
        return jnp.concatenate([prev, t], axis=4)

    qb = to_blocks(q)
    kb = with_prev(to_blocks(k))
    vb = with_prev(to_blocks(v))

    qi = np.arange(QBLOCK)[:, None] + QBLOCK
    ki = np.arange(2 * QBLOCK)[None, :]
    rel = qi - ki
    band = (rel >= 0) & (rel <= steps)
    has_prev = (np.arange(nb)[:, None, None] > 0) | (ki >= QBLOCK)[None]
    valid = band[None] & has_prev
    bucket = t5_causal_bucket(np.maximum(rel, 0) * dilation)
    bias = bias_table_g.astype(jnp.float32)[bucket].transpose(2, 0, 1)

    scale = 1.0 / math.sqrt(Dh)
    logits = jnp.einsum('bdhnqc,bdhnkc->bdhnqk', qb, kb) * scale + bias[None, None, :, None]
    logits = jnp.where(valid, logits, -jnp.inf)
    m = jnp.max(logits, axis=-1)
    p = jnp.exp(logits - m[..., None])
    s = jnp.sum(p, axis=-1)
    num = jnp.einsum('bdhnqk,bdhnkc->bdhnqc', p, vb)

    def unblock(t):
        C = t.shape[-1]
        t = t.reshape(B, dilation, H, Lp, C)[:, :, :, :L]
        return t.transpose(0, 3, 1, 2, 4).reshape(B, S, H, C)

    return unblock(num), unblock(s[..., None])[..., 0], unblock(m[..., None])[..., 0]

def rwkv7_scan(r, decay, k, v, a_in, b_in):
    B, S, H, N = r.shape
    xs = tuple(t.transpose(1, 0, 2, 3) for t in (r, decay, k, v, a_in, b_in))

    def step(state, inp):
        r_t, w_t, k_t, v_t, a_t, b_t = inp
        sa = jnp.einsum('bhvk,bhk->bhv', state, a_t)
        state = (state * w_t[:, :, None, :] + sa[..., None] * b_t[:, :, None, :]
                 + v_t[..., None] * k_t[:, :, None, :])
        y = jnp.einsum('bhvk,bhk->bhv', state, r_t)
        return state, y

    s0 = jnp.zeros((B, H, N, N), jnp.float32)
    _, ys = lax.scan(step, s0, xs)
    return ys.transpose(1, 0, 2, 3)

def first_inputs(seed: int = 0) -> dict:
    key = jax.random.key(seed)
    ks = jax.random.split(key, 20)
    f32 = jnp.float32
    nrm = lambda k, shape: jax.random.normal(k, shape, f32)
    L = DEPTH
    return {
        "x": nrm(ks[0], (BATCH, SEQ, D_MODEL)),
        "pre_norm_gain": 1.0 + 0.05 * nrm(ks[1], (L, D_MODEL)),
        "w_in": nrm(ks[2], (L, D_MODEL, IN_COLS)) * D_MODEL ** -0.5,
        "rel_bias": 0.5 * nrm(ks[3], (N_BUCKETS, N_ATTN_HEADS)),
        "rwkv_shift_mix": jax.random.uniform(ks[4], (L, RWKV_SHIFT_COLS), f32),
        "rwkv_w0": jax.random.uniform(ks[5], (L, RWKV_WIDTH), f32, -6.0, 1.0),
        "rwkv_w_up": nrm(ks[6], (L, DECAY_LORA, RWKV_WIDTH)) * 0.5 * DECAY_LORA ** -0.5,
        "rwkv_a0": 0.5 * nrm(ks[7], (L, RWKV_WIDTH)),
        "rwkv_a_up": nrm(ks[8], (L, AAA_LORA, RWKV_WIDTH)) * 0.5 * AAA_LORA ** -0.5,
        "rwkv_k_k": 0.85 + 0.05 * nrm(ks[9], (L, RWKV_WIDTH)),
        "rwkv_k_a": 1.0 + 0.05 * nrm(ks[10], (L, RWKV_WIDTH)),
        "rwkv_r_k": 0.1 * nrm(ks[11], (L, RWKV_HEADS, RWKV_HEAD_SIZE)),
        "rwkv_ln_w": 1.0 + 0.05 * nrm(ks[12], (L, RWKV_WIDTH)),
        "rwkv_ln_b": 0.01 * nrm(ks[13], (L, RWKV_WIDTH)),
        "w_up_attn": nrm(ks[14], (L, ATTN_WIDTH, D_MODEL)) * ATTN_WIDTH ** -0.5,
        "w_up_rwkv": nrm(ks[15], (L, RWKV_WIDTH, D_MODEL)) * RWKV_WIDTH ** -0.5,
        "w_out": nrm(ks[16], (L, D_MODEL, D_MODEL)) * D_MODEL ** -0.5,
        "post_norm_gain": 1.0 + 0.05 * nrm(ks[17], (L, D_MODEL)),
    }

def first_block(x, pre_norm_gain, w_in, rel_bias, rwkv_shift_mix, rwkv_w0, rwkv_w_up,
              rwkv_a0, rwkv_a_up, rwkv_k_k, rwkv_k_a, rwkv_r_k, rwkv_ln_w, rwkv_ln_b,
              w_up_attn, w_up_rwkv, w_out, post_norm_gain):
    B, S, D = x.shape
    f32 = jnp.float32
    for l in range(DEPTH):
        h = rms_norm(x, pre_norm_gain[l])
        proj = h @ w_in[l]

        qkv = proj[..., :QKV_COLS].astype(f32).reshape(
            B, S, 3, N_GROUPS, ATTN_HEADS_PER_GROUP, HEAD_DIM)
        nums, dens, maxes = [], [], []
        for g, (window, dilation) in enumerate(DILATED_GROUPS):
            table_g = rel_bias[:, g * ATTN_HEADS_PER_GROUP:(g + 1) * ATTN_HEADS_PER_GROUP]
            num, den, mx = dilated_group_attention(
                qkv[:, :, 0, g], qkv[:, :, 1, g], qkv[:, :, 2, g], table_g, window, dilation)
            nums.append(num); dens.append(den); maxes.append(mx)
        m_all = jnp.max(jnp.stack(maxes), axis=0)
        wts = [jnp.exp(mx - m_all) for mx in maxes]
        num_tot = sum(w[..., None] * n for w, n in zip(wts, nums))
        den_tot = sum(w * d for w, d in zip(wts, dens))
        o_attn = (num_tot / den_tot[..., None]).reshape(B, S, ATTN_WIDTH).astype(x.dtype)
        z_attn = proj[..., OFF_ATTN_GATE:OFF_RWKV]
        y_attn = (o_attn * jax.nn.silu(z_attn)) @ w_up_attn[l]

        pr = proj[..., OFF_RWKV:OFF_RWKV_GATE].astype(f32)
        pr_prev = jnp.pad(pr, ((0, 0), (1, 0), (0, 0)))[:, :-1]
        pr = pr + (pr_prev - pr) * rwkv_shift_mix[l].astype(f32)
        r = pr[..., :RWKV_WIDTH]
        k = pr[..., RWKV_WIDTH:2 * RWKV_WIDTH]
        v = pr[..., 2 * RWKV_WIDTH:3 * RWKV_WIDTH]
        w_low = pr[..., 3 * RWKV_WIDTH:3 * RWKV_WIDTH + DECAY_LORA]
        a_low = pr[..., 3 * RWKV_WIDTH + DECAY_LORA:]
        w_log = -jax.nn.softplus(-(rwkv_w0[l].astype(f32) + jnp.tanh(w_low) @ rwkv_w_up[l].astype(f32))) - 0.5
        decay = jnp.exp(-jnp.exp(w_log))
        a = jax.nn.sigmoid(rwkv_a0[l].astype(f32) + a_low @ rwkv_a_up[l].astype(f32))
        hs = (B, S, RWKV_HEADS, RWKV_HEAD_SIZE)
        kk = (k * rwkv_k_k[l].astype(f32)).reshape(hs)
        kk = kk / jnp.maximum(jnp.linalg.norm(kk, axis=-1, keepdims=True), 1e-12)
        k = k * (1.0 + (a - 1.0) * rwkv_k_a[l].astype(f32))
        r4, k4, v4 = r.reshape(hs), k.reshape(hs), v.reshape(hs)
        y = rwkv7_scan(r4, decay.reshape(hs), k4, v4, -kk, kk * a.reshape(hs))
        mu = jnp.mean(y, axis=-1, keepdims=True)
        var = jnp.mean(jnp.square(y - mu), axis=-1, keepdims=True)
        y = ((y - mu) * lax.rsqrt(var + GN_EPS)).reshape(B, S, RWKV_WIDTH)
        y = y * rwkv_ln_w[l].astype(f32) + rwkv_ln_b[l].astype(f32)
        bonus = jnp.sum(r4 * k4 * rwkv_r_k[l].astype(f32), axis=-1, keepdims=True) * v4
        o_rwkv = (y + bonus.reshape(B, S, RWKV_WIDTH)).astype(x.dtype)
        z_rwkv = proj[..., OFF_RWKV_GATE:OFF_MERGE]
        y_rwkv = (o_rwkv * jax.nn.silu(z_rwkv)) @ w_up_rwkv[l]

        g_attn = proj[..., OFF_MERGE:OFF_MERGE + D_MODEL]
        g_rwkv = proj[..., OFF_MERGE + D_MODEL:]
        merged = jax.nn.sigmoid(g_attn) * y_attn + jax.nn.sigmoid(g_rwkv) * y_rwkv
        out = merged @ w_out[l]
        x = x + rms_norm(out, post_norm_gain[l])
    return x


MIX_WIDTH = D_MODEL
HYENA_WIDTH = MIX_WIDTH // 2
HYENA_ORDER = 2
HYENA_GROUPS = 8
SHORT_CONV_WIDTH = 3
FILTER_EMB_DIM = 33
FILTER_BANDS = (FILTER_EMB_DIM - 1) // 2
FILTER_HIDDEN = 64
DECAY_TARGET = 1e-2
FAST_DECAY_PCT = 0.3
SLOW_DECAY_PCT = 1.5
ATTN_WIDTH_2 = MIX_WIDTH - HYENA_WIDTH
ATTN_HEADS = 4
ATTN_HEAD_DIM = ATTN_WIDTH_2 // (2 * ATTN_HEADS)
Q_BLOCK = 128
HYENA_COLS = (HYENA_ORDER + 1) * HYENA_WIDTH
IN_COLS_2 = HYENA_COLS + 3 * ATTN_WIDTH_2
N_EXPERTS = 16
EC_CAPACITY_FACTOR = 2
EXPERT_FF = 2816
NORM_EPS = 1e-6


def _rmsnorm(x, g):
    xf = x.astype(jnp.float32)
    y = xf * lax.rsqrt(jnp.mean(xf * xf, axis=-1, keepdims=True) + NORM_EPS)
    return (y * g.astype(jnp.float32)).astype(x.dtype)

def _alibi_slopes(n):
    return jnp.asarray([2.0 ** (-8.0 * (i + 1) / n) for i in range(n)], dtype=jnp.float32)

def _hyena_filters(L, w1, b1, w2, b2, w3, freq):
    f32 = jnp.float32
    t = jnp.linspace(0.0, 1.0, L, dtype=f32)[:, None]
    w = 2.0 * math.pi * jnp.arange(L, dtype=f32)[:, None] / L
    bands = jnp.linspace(1e-4, FILTER_BANDS - 1, FILTER_BANDS, dtype=f32)[None, :]
    z = jnp.concatenate([t, jnp.cos(bands * w), -jnp.sin(bands * w)], axis=-1)
    fr = freq.astype(f32)
    hid = jnp.sin(fr * (z @ w1.astype(f32) + b1.astype(f32)))
    hid = jnp.sin(fr * (hid @ w2.astype(f32) + b2.astype(f32)))
    h = (hid @ w3.astype(f32)).reshape(L, 2, HYENA_ORDER, HYENA_WIDTH)
    min_decay = math.log(DECAY_TARGET) / SLOW_DECAY_PCT
    max_decay = math.log(DECAY_TARGET) / FAST_DECAY_PCT
    deltas = jnp.abs(jnp.linspace(min_decay, max_decay, HYENA_WIDTH, dtype=f32))
    h = h * jnp.exp(-t[:, :, None, None] * deltas)
    fwd, bwd = h[:, 0], h[:, 1]
    k = jnp.concatenate([fwd, jnp.zeros((1, HYENA_ORDER, HYENA_WIDTH), f32), bwd[:0:-1]], axis=0)
    return k / jnp.sum(jnp.abs(k), axis=0, keepdims=True)

def _fft_conv(u, k_freq, L):
    uf = jnp.fft.rfft(u, n=2 * L, axis=1)
    return jnp.fft.irfft(uf * k_freq[None], n=2 * L, axis=1)[:, :L]

def _hyena_mixer(proj, conv_w, conv_b, w1, b1, w2, b2, w3, freq, skip, norm_g):
    B, L, _ = proj.shape
    pad = SHORT_CONV_WIDTH // 2
    up = jnp.pad(proj, ((0, 0), (pad, pad), (0, 0)))
    u = conv_b
    for j in range(SHORT_CONV_WIDTH):
        u = u + up[:, j:j + L] * conv_w[j]
    x1, x2, v = jnp.split(u, HYENA_ORDER + 1, axis=-1)
    k_freq = jnp.fft.rfft(_hyena_filters(L, w1, b1, w2, b2, w3, freq), axis=0)
    skip = skip.astype(jnp.float32)
    z = v.astype(jnp.float32)
    for n, gate in enumerate((x1, x2)):
        z = gate.astype(jnp.float32) * (_fft_conv(z, k_freq[:, n], L) + skip[n] * z)
    z = z.reshape(B, L, HYENA_GROUPS, HYENA_WIDTH // HYENA_GROUPS)
    z = _rmsnorm(z, norm_g.reshape(HYENA_GROUPS, HYENA_WIDTH // HYENA_GROUPS))
    return z.reshape(B, L, HYENA_WIDTH).astype(proj.dtype)

def _diff_attention(q, k, v, lam, lam_init, subln_g):
    B, L, _ = q.shape
    H, Dh = ATTN_HEADS, ATTN_HEAD_DIM
    q = q.reshape(B, L, H, 2, Dh)
    k = k.reshape(B, L, H, 2, Dh)
    v = v.reshape(B, L, H, 2 * Dh)
    scale = Dh ** -0.5
    slopes = _alibi_slopes(H)
    nb = L // Q_BLOCK
    qb = q.reshape(B, nb, Q_BLOCK, H, 2, Dh).transpose(1, 0, 2, 3, 4, 5)
    starts = jnp.arange(nb, dtype=jnp.int32) * Q_BLOCK
    kpos = jnp.arange(L, dtype=jnp.float32)

    def block(args):
        qblk, s0 = args
        qpos = (s0 + jnp.arange(Q_BLOCK, dtype=jnp.int32)).astype(jnp.float32)
        dist = jnp.abs(qpos[:, None] - kpos[None, :])
        s = jnp.einsum('bqhcd,bkhcd->bhcqk', qblk, k).astype(jnp.float32) * scale
        s = s - slopes[None, :, None, None, None] * dist
        p = jax.nn.softmax(s, axis=-1)
        a = p[:, :, 0] - lam * p[:, :, 1]
        return jnp.einsum('bhqk,bkhe->bqhe', a.astype(v.dtype), v)

    o = lax.map(block, (qb, starts))
    o = o.transpose(1, 0, 2, 3, 4).reshape(B, L, H, 2 * Dh)
    o = _rmsnorm(o, subln_g) * (1.0 - lam_init)
    return o.reshape(B, L, H * 2 * Dh).astype(q.dtype)

def _expert_choice_ffn(h, w_router, w_gate, w_up, w_down):
    B, L, _ = h.shape
    cap = EC_CAPACITY_FACTOR * L // N_EXPERTS
    logits = jnp.einsum('bsd,de->bse', h, w_router).astype(jnp.float32)
    aff = jax.nn.softmax(logits, axis=-1)
    g, idx = lax.top_k(aff.transpose(2, 0, 1), cap)
    bi = jnp.arange(B, dtype=jnp.int32)[None, :, None]
    xin = h[bi, idx]

    def expert(args):
        xe, wg, wu, wd = args
        a = jnp.einsum('bcd,df->bcf', xe, wg)
        u = jnp.einsum('bcd,df->bcf', xe, wu)
        return jnp.einsum('bcf,fd->bcd', jax.nn.silu(a) * u, wd)

    out = lax.map(expert, (xin, w_gate, w_up, w_down))
    out = out * g[..., None].astype(out.dtype)
    return jnp.zeros_like(h).at[bi, idx].add(out)

def second_inputs(seed: int = 0) -> dict:
    key = jax.random.key(seed)
    ks = jax.random.split(key, 25)
    f32 = jnp.float32

    def nrm(k, shape, scale):
        return jax.random.normal(k, shape, f32) * scale

    D, E, F = D_MODEL, N_EXPERTS, EXPERT_FF
    return {
        'x': nrm(ks[0], (BATCH, SEQ, D), 1.0),
        'attn_norm_g': 1.0 + nrm(ks[1], (DEPTH, D), 0.02),
        'w_in': nrm(ks[2], (DEPTH, D, IN_COLS_2), D ** -0.5),
        'conv_w': nrm(ks[3], (DEPTH, SHORT_CONV_WIDTH, HYENA_COLS), SHORT_CONV_WIDTH ** -0.5),
        'conv_b': nrm(ks[4], (DEPTH, HYENA_COLS), 0.02),
        'filt_w1': nrm(ks[5], (DEPTH, FILTER_EMB_DIM, FILTER_HIDDEN), FILTER_EMB_DIM ** -0.5),
        'filt_b1': nrm(ks[6], (DEPTH, FILTER_HIDDEN), 0.1),
        'filt_w2': nrm(ks[7], (DEPTH, FILTER_HIDDEN, FILTER_HIDDEN), FILTER_HIDDEN ** -0.5),
        'filt_b2': nrm(ks[8], (DEPTH, FILTER_HIDDEN), 0.1),
        'filt_w3': nrm(ks[9], (DEPTH, FILTER_HIDDEN, 2 * HYENA_ORDER * HYENA_WIDTH), FILTER_HIDDEN ** -0.5),
        'filt_freq': 1.0 + nrm(ks[10], (DEPTH, FILTER_HIDDEN), 0.1),
        'hyena_skip': nrm(ks[11], (DEPTH, HYENA_ORDER, HYENA_WIDTH), 1.0),
        'hyena_norm_g': 1.0 + nrm(ks[12], (DEPTH, HYENA_WIDTH), 0.02),
        'lambda_q1': nrm(ks[13], (DEPTH, ATTN_HEAD_DIM), 0.1),
        'lambda_k1': nrm(ks[14], (DEPTH, ATTN_HEAD_DIM), 0.1),
        'lambda_q2': nrm(ks[15], (DEPTH, ATTN_HEAD_DIM), 0.1),
        'lambda_k2': nrm(ks[16], (DEPTH, ATTN_HEAD_DIM), 0.1),
        'subln_g': 1.0 + nrm(ks[17], (DEPTH, 2 * ATTN_HEAD_DIM), 0.02),
        'w_out': nrm(ks[18], (DEPTH, MIX_WIDTH, D), MIX_WIDTH ** -0.5),
        'ffn_norm_g': 1.0 + nrm(ks[19], (DEPTH, D), 0.02),
        'w_router': nrm(ks[20], (DEPTH, D, E), D ** -0.5),
        'w_gate': nrm(ks[21], (DEPTH, E, D, F), D ** -0.5),
        'w_up': nrm(ks[22], (DEPTH, E, D, F), D ** -0.5),
        'w_down': nrm(ks[23], (DEPTH, E, F, D), F ** -0.5),
        'final_norm_g': 1.0 + nrm(ks[24], (D,), 0.02),
    }

def second_block(x, attn_norm_g, w_in, conv_w, conv_b, filt_w1, filt_b1, filt_w2, filt_b2,
              filt_w3, filt_freq, hyena_skip, hyena_norm_g, lambda_q1, lambda_k1,
              lambda_q2, lambda_k2, subln_g, w_out, ffn_norm_g, w_router, w_gate, w_up,
              w_down, final_norm_g):
    f32 = jnp.float32
    for l in range(DEPTH):
        hn = _rmsnorm(x, attn_norm_g[l])
        proj = jnp.einsum('bsd,dn->bsn', hn, w_in[l])
        hy = _hyena_mixer(proj[..., :HYENA_COLS], conv_w[l], conv_b[l], filt_w1[l], filt_b1[l],
                          filt_w2[l], filt_b2[l], filt_w3[l], filt_freq[l], hyena_skip[l],
                          hyena_norm_g[l])
        q, k, v = jnp.split(proj[..., HYENA_COLS:], 3, axis=-1)
        lam_init = 0.8 - 0.6 * math.exp(-0.3 * l)
        lam = (jnp.exp(jnp.sum(lambda_q1[l].astype(f32) * lambda_k1[l].astype(f32)))
               - jnp.exp(jnp.sum(lambda_q2[l].astype(f32) * lambda_k2[l].astype(f32)))
               + lam_init)
        at = _diff_attention(q, k, v, lam, lam_init, subln_g[l])
        mix = jnp.concatenate([hy, at], axis=-1)
        x = x + jnp.einsum('bsm,md->bsd', mix, w_out[l])
        x = x + _expert_choice_ffn(_rmsnorm(x, ffn_norm_g[l]), w_router[l], w_gate[l],
                                   w_up[l], w_down[l])
    return _rmsnorm(x, final_norm_g)


def setup_inputs(seed=0):
    out = dict(first_inputs(seed))
    for name, value in second_inputs(seed + 1).items():
        if name != "x":
            out[name + "_2"] = value
    return out


def reference(
    x, pre_norm_gain, w_in, rel_bias, rwkv_shift_mix, rwkv_w0, rwkv_w_up, rwkv_a0, rwkv_a_up,
    rwkv_k_k, rwkv_k_a, rwkv_r_k, rwkv_ln_w, rwkv_ln_b, w_up_attn, w_up_rwkv, w_out,
    post_norm_gain, attn_norm_g_2, w_in_2, conv_w_2, conv_b_2, filt_w1_2, filt_b1_2, filt_w2_2,
    filt_b2_2, filt_w3_2, filt_freq_2, hyena_skip_2, hyena_norm_g_2, lambda_q1_2, lambda_k1_2,
    lambda_q2_2, lambda_k2_2, subln_g_2, w_out_2, ffn_norm_g_2, w_router_2, w_gate_2, w_up_2,
    w_down_2, final_norm_g_2,
):
    x = first_block(
        x, pre_norm_gain, w_in, rel_bias, rwkv_shift_mix, rwkv_w0, rwkv_w_up, rwkv_a0,
        rwkv_a_up, rwkv_k_k, rwkv_k_a, rwkv_r_k, rwkv_ln_w, rwkv_ln_b, w_up_attn, w_up_rwkv,
        w_out, post_norm_gain,
    )
    return second_block(
        x, attn_norm_g_2, w_in_2, conv_w_2, conv_b_2, filt_w1_2, filt_b1_2, filt_w2_2,
        filt_b2_2, filt_w3_2, filt_freq_2, hyena_skip_2, hyena_norm_g_2, lambda_q1_2,
        lambda_k1_2, lambda_q2_2, lambda_k2_2, subln_g_2, w_out_2, ffn_norm_g_2, w_router_2,
        w_gate_2, w_up_2, w_down_2, final_norm_g_2,
    )


_drawn_inputs = setup_inputs


def setup_inputs(seed=0):
    import zlib

    import numpy as np

    out = dict(_drawn_inputs(seed))
    spreads = {}
    factors = {'rwkv_ln_b': 5.019,
     'conv_b_2': 2.732,
     'filt_b1_2': 3.309,
     'filt_b2_2': 3.254,
     'filt_freq_2': 5.897,
     'hyena_norm_g_2': 5.452,
     'lambda_q2_2': 8.0,
     'lambda_k2_2': 8.0,
     'subln_g_2': 6.777,
     'ffn_norm_g_2': 5.143,
     'final_norm_g_2': 2.839}
    for name, (base, spread) in spreads.items():
        noise = np.random.default_rng([zlib.crc32(name.encode()), seed]).standard_normal(out[name].shape)
        drawn = base * np.exp(spread * noise) if base else spread * noise
        out[name] = jnp.asarray(drawn.astype(out[name].dtype))
    for name, factor in factors.items():
        out[name] = (out[name] * factor).astype(out[name].dtype)
    return out
```

```python
from contextlib import ExitStack

import concourse.bass as bass
from concourse import mybir

F32 = mybir.dt.float32
ALU = mybir.AluOpType
ACT = mybir.ActivationFunctionType
AX = mybir.AxisListType

P = 128
T = 256
TT = T // P
D = 1024
KC = D // P
HD = 64
NG, NH = 3, 8
CH = 64
NCH = T // CH
AW = NH * HD
FT = AW // P
OFF_GATE = 3 * NG * AW
OFF_RWKV = OFF_GATE + AW
OFF_LOW = OFF_RWKV + 3 * AW
OFF_RGATE = OFF_LOW + P
OFF_MERGE = OFF_RGATE + AW
NEG = -1.0e30
E_HALF = 0.6065306597126334

COLS = {}
def _cols():
    at = 0
    for name, n in [("pre_g", 8), ("mix", 13), ("w0", 4), ("a0", 4), ("k_k", 4), ("k_a", 4), ("r_k", 4),
                    ("attn_g", 8), ("conv_w", 36), ("conv_b", 12), ("subln", 1), ("ffn_g", 8),
                    ("hy_g", 4), ("filt_b1", 1), ("filt_b2", 1), ("filt_freq", 1)]:
        COLS[name] = (at, at + n)
        at += n
    return at
NCOLS = _cols()
ROWS = {}
def _rows():
    at = 0
    for name, n in [("post_g", 1024), ("ln_w", 512), ("ln_b", 512), ("skip", 1024), ("final_g", 1024), ("lam", 256)]:
        ROWS[name] = (at, at + n)
        at += n
    return at
NROWS = _rows()


def spread(x, axis, n):
    dims = [list(d) for d in x.ap]
    dims.insert(axis, [0, n])
    return bass.AP(x.tensor, x.offset, dims)


MAGIC = 12582912.0
INV_2PI = 0.15915494309189535
PI2_HI = 6.28125
PI2_LO = 0.0019353071795864769


def constants():
    import numpy as np
    import math
    c = {}
    i = np.arange(128)
    eye = np.eye(128, dtype=np.float32)
    half = np.arange(64)
    par = i % 64
    us = (par[:, None] < half[None, :]).astype(np.float32)
    ui = (par[:, None] <= half[None, :]).astype(np.float32)
    ls = (half[None, :] < par[:, None]).astype(np.float32)
    same2 = (par[:, None] // 2 == half[None, :] // 2).astype(np.float32)
    i64 = (par[:, None] == half[None, :]).astype(np.float32)
    offs = []
    for b in (2, 4, 8, 16, 32):
        offs.append(((par[:, None] // (2 * b) == half[None, :] // (2 * b)) & (par[:, None] % (2 * b) >= b)
                     & (half[None, :] % (2 * b) < b)).astype(np.float32))
    blockones = (i[:, None] // 64 == i[None, :] // 64).astype(np.float32)
    two = (i[:, None] // 64 == np.arange(2)[None, :]).astype(np.float32)
    chunkstart = np.tile((np.arange(256) % 64 != 0).astype(np.float32)[None], (128, 1))
    c["c_square"] = np.concatenate([eye, eye[:, ::-1], us, ui, ls, us * same2, ls * same2, i64] + offs
                                   + [blockones, two, chunkstart], axis=1).astype(np.float32)
    j = np.arange(384) - 127
    d = np.maximum(j, 0)
    ratio = np.log(np.maximum(d, 1).astype(np.float32) / 16) / np.float32(math.log(2048 / 16))
    large = np.minimum(16 + (ratio * 16).astype(np.int32), 31)
    bucket = np.where(d < 16, d, large).astype(np.int32)
    c["c_bucket"] = (np.arange(32)[:, None] == bucket[None]).astype(np.float32)
    rows = []
    for window, dil in ((128, 1), (512, 4), (2048, 16)):
        ok = (j >= 0) & (j % dil == 0) & (j // dil <= window // dil) & (j <= 255)
        rows += [np.where(ok, 0.0, -1.0e30)] * 8
    c["c_mask"] = np.stack(rows).astype(np.float32)
    t = np.arange(256)
    f = np.arange(256)
    ang = 2 * np.pi * ((t[:, None] * f[None]) % 512) / 512
    alt = np.where(t % 2 == 0, 1.0, -1.0)
    cos, sin = np.cos(ang), np.sin(ang)
    cosp = cos[:, 0:128].copy()
    cosp[:, 0] = alt
    sinp = -sin[:, 0:128]
    sinp[:, 0] = alt
    fwd = np.concatenate([cos, -sin, cosp, sinp], axis=1)
    c["c_fwd"] = fwd.reshape(2, 128, 768).transpose(1, 0, 2).reshape(128, 1536)
    wt = np.where(f == 0, 1.0, 2.0) / 512
    re = wt[:, None] * cos.T
    im = -wt[:, None] * sin.T
    im[0] = alt / 512
    inv = np.concatenate([re, im], axis=0).reshape(4, 128, 256)
    c["c_inv"] = inv.transpose(1, 0, 2).reshape(128, 1024)
    ts = np.linspace(0.0, 1.0, 256, dtype=np.float32)
    lo, hi = math.log(1e-2) / 1.5, math.log(1e-2) / 0.3
    deltas = np.abs(np.linspace(lo, hi, 512, dtype=np.float32))
    dec = np.exp(-ts[:, None] * deltas)
    c["c_decay"] = dec.reshape(2, 128, 512).transpose(1, 0, 2).reshape(128, 1024)
    w = np.float32(2 * math.pi) * np.arange(256, dtype=np.float32)[:, None] / np.float32(256)
    bands = np.linspace(1e-4, 15, 16, dtype=np.float32)[None]
    z = np.concatenate([ts[:, None], np.cos(bands * w), -np.sin(bands * w)], axis=-1)
    c["c_emb"] = z.T
    dist = np.abs(t[:, None] - t[None]).astype(np.float32)
    first = (np.arange(128) > 0).astype(np.float32)[:, None]
    c["c_dist"] = np.concatenate([dist.reshape(2, 128, 256).transpose(1, 0, 2).reshape(128, 512), first], axis=1)
    c["c_slots"] = np.tile(np.arange(1, 33)[None], (128, 1))
    return {k: np.ascontiguousarray(v, dtype=np.float32) for k, v in c.items()}


def program(nc, A, out):
    ctx = ExitStack()
    with ctx:
        def sem(name):
            return ctx.enter_context(nc.semaphore(name))

        ARENA = 52992
        arena = ctx.enter_context(nc.sbuf_tensor("arena", [P, ARENA], F32))
        psum = ctx.enter_context(nc.psum_tensor("psum", [P, 8, 512], F32))
        bias_rows = nc.dram_tensor("bias_rows", (NG * NH, 384), F32, kind="Internal").ap()

        def region(off, *shape):
            n = 1
            for s in shape:
                n *= s
            x = arena[:, off:off + n]
            if len(shape) == 2:
                x = x.rearrange("p (a b) -> p a b", a=shape[0])
            elif len(shape) == 3:
                x = x.rearrange("p (a b c) -> p a b c", a=shape[0], b=shape[1])
            elif len(shape) == 4:
                x = x.rearrange("p (a b c d) -> p a b c d", a=shape[0], b=shape[1], c=shape[2])
            return x

        RING = 12 * 2816
        wb = [region(4096 * i, 8, 512) for i in range(4)]
        wb_up = [region(4096 * i, 4, 1024) for i in range(4)]
        S0 = 16896
        qT = region(S0, 12, T)
        kT = region(S0 + 3072, 12, T)
        vR = region(S0 + 6144, TT, 1536)
        bias = region(S0 + 9216, NH, NG, T)
        F0 = RING
        xres = region(F0, TT, D)
        hT = region(F0 + 2048, KC, T)
        hR = region(F0 + 4096, KC, T)
        hn = region(F0 + 12000, TT, D)
        prT = region(F0 + 6144, 13, T)
        oaT = region(F0 + 9472, FT, T)
        zaT = region(F0 + 10496, FT, T)
        zrT = region(F0 + 11520, FT, T)
        LG = region(F0 + 12544, 2, NG * T)
        PT = region(F0 + 14080, 2, 2, 3, P)
        C0 = F0 + 15616
        cols = region(C0, NCOLS)
        csq = region(C0 + 128, 1346)
        small = region(C0 + 128 + 1346, 256)
        bucketT = region(S0, 384)
        maskT = region(S0 + 384, 384)
        relb = region(S0 + 768, 32)
        brow = region(S0 + 800, 384)
        lowW = region(C0 + 1730, 512)
        assert C0 + 1730 + 512 <= ARENA and NCOLS <= 128

        ident, anti = csq[:, 0:128], csq[:, 128:256]
        US, UI, LS = csq[:, 256:320], csq[:, 320:384], csq[:, 384:448]
        US2, LS2, I64 = csq[:, 448:512], csq[:, 512:576], csq[:, 576:640]
        OFFB = [csq[:, 640 + 64 * i:704 + 64 * i] for i in range(5)]
        BLK1, TWO, CSTART = csq[:, 960:1088], csq[:, 1088:1090], csq[:, 1090:1346]

        def col(name, i=0, n=1):
            a = COLS[name][0] + i
            return cols[:, a:a + n]

        AR = region(S0, FT, NCH, 2, CH)
        BT = region(S0 + 2048, FT, T)
        KT = region(S0 + 3072, FT, T)
        TB, TK, TV = (region(S0 + 4096 + 1024 * i, TT, AW) for i in range(3))
        MATS = [region(S0 + 7168 + 1024 * i, 2, NH, CH) for i in range(9)]
        mN, mA, mMT, mM, mT1, mAk, mRb, mRk, mOff = MATS
        ST = region(S0 + 16384, FT, CH)
        LD = region(F0 + 2048 + 2048, FT, T)
        CS = region(F0 + 2048 + 3072, FT, T)
        KK = region(F0 + 12544, FT, T)
        AA = region(F0 + 13568, FT, T)
        TMP = region(F0 + 14592, FT, T)
        EX1 = region(S0 + 7168, FT, T)
        EX2 = region(S0 + 8192, FT, T)
        XV = region(S0 + 2048, 2, NH, CH)
        XS = region(S0 + 3072, NH, CH)
        USB = region(S0 + 3584, NH, CH)
        Y = region(F0 + 4096, TT, AW)
        Y1 = region(F0 + 5120, TT, AW)
        YT = region(F0 + 13568, TT, AW)
        rows = region(F0 + 6144, 1024)
        orT = region(F0 + 12544, FT, T)
        YA = region(S0, KC, T)
        YR = region(S0 + 2048, KC, T)
        EG = region(S0 + 4096, KC, T)
        MG = region(S0 + 6144, KC, T)
        OUT1 = region(S0 + 8192, TT, D)
        postg = region(S0 + 10240, D)

        h2T = region(F0 + 2048, KC, T)
        Kr = region(S0, 2, 2, 512)
        Ki = region(S0 + 2048, 2, 2, 512)
        KrP = region(S0 + 4096, 2, 512)
        fwd = region(S0 + 5120, TT, 768)
        inv = region(S0 + 6656, 4, T)
        decay = region(S0 + 7680, TT, 512)
        skip = region(S0 + 8704, 2, 512)
        XU = region(S0 + 9728, 3, TT, 512)
        SPY = region(S0 + 12800, 2, 2, 512)
        M1 = region(S0 + 14848, 2, 512)
        M2 = region(S0 + 15872, 2, 512)
        UPR = region(F0 + 4096, 12, T + 2)
        UC = region(F0 + 7200, 12, T)
        q2T = region(F0 + 10272, 4, T)
        k2T = region(F0 + 11296, 4, T)
        v2 = region(F0 + 12320, TT, 512)
        LG2 = region(F0 + 13344, 2, 2, T)
        PT2 = region(F0 + 14368, 2, TT, P)
        dist = region(F0 + 14880, 513)
        first = region(F0 + 14880 + 512, 1)
        fS = region(F0 + 4096, TT, 2, 512)
        fD = region(F0 + 6144, TT, 2, 512)
        w3 = region(F0 + 8192, 2048)
        emb = region(F0 + 10272, T)
        fw1 = region(F0 + 10528, 64)
        fw2 = region(F0 + 10592, 64)
        hid = region(F0 + 10656, T)
        harg = region(F0 + 10912, T)
        hrnd = region(F0 + 11168, T)
        lamr = region(F0 + 11424, 4, 64)
        fF = region(F0 + 11680, 512)
        fB = region(F0 + 12192, 512)
        fFa = region(F0 + 12704, 512)
        fBa = region(F0 + 13216, 512)
        rnorm = region(F0 + 13728, 2, 512)
        ones = region(C0 + 1730, 128)
        hn2 = region(S0 + 12800, TT, D)
        OA = region(F0 + 7200, TT, 4, P)
        OSQ = region(F0 + 8224, TT, 4, P)
        mixT = region(F0 + 4096, KC, T)
        ZN = region(S0 + 14848, TT, 512)
        E, CAP, FF = 16, 32, 2816
        SLOTS = 12
        PIECE = 2816
        FPP = FF // P
        QUARTER = FF // 4
        HALFQ = QUARTER // 2

        def slot(n):
            return region(PIECE * n, PIECE)
        XE = region(F0 + 2048, E * KC * CAP)
        OT = region(F0 + 6144, E * TT * P)
        XC = region(F0 + 10240, KC, CAP)
        OC = region(F0 + 10496, TT, P)
        GE = region(F0 + 10752, QUARTER)
        HP = region(F0 + 11456, FPP, CAP)
        HT = region(F0 + 12160, FPP, CAP)
        YS = region(F0 + 12864, 2, 512)
        finalg = region(F0 + 13888, D)
        hf = region(F0 + 2048 + 8192, TT, D)
        hfT = region(F0 + 6144, KC, T)
        ohot = region(F0 + 12288, TT, E, CAP)
        og4 = region(F0 + 13312, 4, 2, 4 * CAP)
        wr = region(F0 + 8192, KC, 16)
        affT = region(F0 + 8320, T)
        work = [region(F0 + 8576 + 256 * i, T) for i in range(2)]
        onesT = region(F0 + 9088, T)
        slotsr = region(F0 + 14912, CAP)
        top8 = region(F0 + 14944, 8)
        aff = region(F0 + 14952, TT, E)
        rank = region(F0 + 14984, TT, E)
        stat = region(F0 + 15016, 16)
        S = {}
        for name in ["params", "xin", "brow_out", "bias_in", "rows_in", "postg_in",
                     "w_used", "proj_ready", "proj_evac", "hn_ready", "sq_sum", "mean_in", "root_in", "hT_ready", "hT_evac", "hR_evac", "low_in",                      "bias_mm", "bias_row", "logit_ready", "prob_ready", "pt_ready", "pt_done",
                     "o_ready", "o_done", "neg_max", "expd",
                     "low_t", "low_mm", "lowexp", "sq_ready", "norm_mm", "norm_sqrt", "cs_ready", "exps",
                     "ab_ready", "tok_tr", "tok_done", "gram_mm", "gram_done", "T1_mm", "T1_done", "MM_mm", "MM_done", "xv_mm", "xv_done",
                     "x_mm", "x_done", "u_mm", "u_done", "s_mm", "s_done", "y_mm", "y1_done", "bonus_mm",                      "gn_done", "or_mm", "or_done", "za_exp", "zr_exp", "up_mm", "up_done", "g_mm", "g_exp", "g_done",
                     "out1_mm", "out1_sb", "x1_ready", "store",
                     "dve_line"]:
            S[name] = sem(name)
        for name in ["f_in", "f_mm", "lam_sum", "ones_set", "n2_evac2", "f_hid", "f_arg", "f_w3mm", "f_abs_in", "f_abs", "f_norm", "f_sd", "f_kmm", "f_kdone",
                     "n2_tr", "n2_evac", "p2_ready", "p2_evac", "u_conv", "u_tr", "u_evac",
                     "z_mm", "spec", "i_mm", "z_done", "hy_norm", "m_tr", "m_evac",
                     "l2_mm", "l2_neg", "l2_exp", "l2_prob", "l2_tr", "l2_turned", "o2_mm", "o2_sb", "o2_sq", "o2_norm",
                     "lam_exp", "m2_tr", "m2_evac", "x2_mm", "x2_ready", "skip_in"]:
            S[name] = sem(name)
        for name in ["r_in", "n3_tr", "n3_evac", "r_mm", "r_neg", "r_exp", "aff_ready", "aff_tr", "rank_ready",
                     "rank_tr", "ohot_ready", "og_ready", "x_gather", "x_evac", "o_tr", "o_evac", "xc_ready", "oc_ready", "piece_used", 
                     "g_expd", "h_ready", "y3_sb", "sc_mm", "acc_done", "out_ready", "fg_in",
                     "dve_loop"]:
            S[name] = sem(name)
        arrived = [sem(f"piece{i}_in") for i in range(SLOTS)]
        wload = [sem(f"wload{i}") for i in range(4)]

        class Line:
            def __init__(self, eng, s):
                self.eng, self.s, self.n = eng, s, 0

            def __call__(self, ins):
                self.n += 1
                ins.then_inc(self.s, 1)
                self.eng.wait_ge(self.s, self.n)

        def in_cols(w, c0, n=512):
            return w[:, c0:c0 + n].rearrange("(k p) n -> p k n", p=P)
        w_in = A["w_in"]
        blocks = [("low", in_cols(w_in, OFF_LOW, P))]
        blocks += [(f"rkv{i}", in_cols(w_in, OFF_RWKV + 512 * i)) for i in range(3)]
        blocks += [("rgate", in_cols(w_in, OFF_RGATE))]
        blocks += [(f"q{i}", in_cols(w_in, 512 * i)) for i in range(3)]
        blocks += [(f"k{i}", in_cols(w_in, 1536 + 512 * i)) for i in range(3)]
        blocks += [(f"v{i}", in_cols(w_in, 3072 + 512 * i)) for i in range(3)]
        blocks += [("agate", in_cols(w_in, OFF_GATE))]
        blocks += [("upa", A["w_up_attn"].rearrange("(k p) n -> p k n", p=P)),
                   ("upr", A["w_up_rwkv"].rearrange("(k p) n -> p k n", p=P))]
        blocks += [(f"g{i}", in_cols(w_in, OFF_MERGE + 512 * i)) for i in range(4)]
        blocks += [(f"out{i}", in_cols(A["w_out"], 512 * i)) for i in range(2)]
        blocks += [(f"hy{i}", in_cols(A["w_in_2"], 512 * i)) for i in range(3)]
        blocks += [(f"at{i}", in_cols(A["w_in_2"], 1536 + 512 * i)) for i in range(3)]
        blocks += [(f"out2_{i}", in_cols(A["w_out_2"], 512 * i)) for i in range(2)]
        number = {name: n for n, (name, _) in enumerate(blocks)}

        def block_of(name):
            return wb[number[name] % 4]

        def weights_in(pe, name):
            n = number[name]
            pe.wait_ge(wload[n % 4], 16 * (n // 4 + 1))

        wg, wu = A["w_gate"], A["w_up"]
        wd = A["w_down"].rearrange("e (p i) n -> (e p) (i n)", p=P)

        def piece(e, i):
            if i < 16:
                w = (wg if i < 8 else wu).rearrange("e k n -> (e k) n")
                return w[bass.ds(e * D + (i % 8) * P, P), :]
            return wd[bass.ds(e * P, P), (i - 16) * PIECE:(i - 15) * PIECE]

        tiles = [("low", 0, hT, prT[:, 12, :], 1.0)]
        tiles += [(f"rkv{i}", c, hT, prT[:, 4 * i + c, :], 1.0) for i in range(3) for c in range(4)]
        tiles += [("rgate", c, hT, zrT[:, c, :], 1.0) for c in range(4)]
        tiles += [(f"q{i}", c, hT, qT[:, 4 * i + c, :], 0.125) for i in range(3) for c in range(4)]
        tiles += [(f"k{i}", c, hR, kT[:, 4 * i + c, :], 1.0) for i in range(3) for c in range(4)]
        tiles += [(f"v{i}", u, None, vR[:, u, 512 * i:512 * i + 512], 1.0) for i in range(3) for u in range(TT)]
        tiles += [("agate", c, hT, zaT[:, c, :], 1.0) for c in range(4)]
        LOW_TILES, RWKV_TILES = 1, 13
        NT = len(tiles)
        units = [(h, tile) for h in range(NH) for tile in (1, 0)]
        NU = len(units)

        def hh(h):
            return (h % 2) * 4 + h // 2
        order = [0, 2, 4, 6, 1, 3, 5, 7]

        block = ctx.enter_context(nc.Block())

        @block.sync
        def _(sp):
            sp.dma_start(xres, A["x"].rearrange("(a p) d -> p a d", p=P)).then_inc(S["xin"], 16)
            for n, (name, src) in enumerate(blocks):
                if n >= 4:
                    sp.wait_ge(S["w_used"], n - 3)
                if name[0:2] == "up":
                    dst = wb_up[n % 4]
                else:
                    dst = wb[n % 4][:, :, 0:src.shape[2]]
                sp.dma_start(dst, src).then_inc(wload[n % 4], 16)
            used, last = S["w_used"], len(blocks)
            for i, count, value in ((0, used, last - 2), (5, used, last - 3), (6, S["spec"], 2), (7, S["spec"], 2), (8, S["i_mm"], 2),
                                    (9, S["z_done"], 2), (10, S["hy_norm"], 1), (11, S["m_tr"], 2),
                                    (1, used, last), (2, used, last), (3, used, last), (4, used, last)):
                sp.wait_ge(count, value)
                sp.dma_start(slot(i), piece(0, i)).then_inc(arrived[i], 16)
            with sp.Fori(0, E - 1) as e:
                for i in range(SLOTS, 24):
                    sp.wait_ge(S["piece_used"], e * 24 + (i - 11))
                    sp.dma_start(slot(i - SLOTS), piece(e, i)).then_inc(arrived[i - SLOTS], 16)
                for i in range(SLOTS):
                    sp.wait_ge(S["piece_used"], e * 24 + (i + 13))
                    sp.dma_start(slot(i), piece(e + 1, i)).then_inc(arrived[i], 16)
            for i in range(SLOTS, 24):
                sp.wait_ge(S["piece_used"], (E - 1) * 24 + (i - 11))
                sp.dma_start(slot(i - SLOTS), piece(E - 1, i)).then_inc(arrived[i - SLOTS], 16)
            sp.wait_ge(S["out_ready"], 2)
            sp.dma_start(out.rearrange("(a p) d -> p a d", p=P), xres).then_inc(S["store"], 16)
            sp.wait_ge(S["store"], 16)

        @block.gpsimd
        def _(pool):
            pool.wait_ge(S["bias_row"], 1)
            pool.dma_start(bias_rows, brow[0:24, :]).then_inc(S["brow_out"], 16)
            pool.wait_ge(S["brow_out"], 16)
            for g in range(NG):
                src = bass.AP(bias_rows.tensor, g * NH * 384, [[1, P], [384, NH], [1, T]])
                pool.dma_start(bias[:, :, g, :], src).then_inc(S["bias_in"], 16)
            pool.wait_ge(S["ab_ready"], 1)
            a, b = ROWS["ln_w"][0], ROWS["ln_b"][1]
            pool.dma_start(rows, A["rows"][a:b].partition_broadcast(P)).then_inc(S["rows_in"], 16)
            pool.wait_ge(S["s_done"], NCH)
            pool.wait_ge(S["or_done"], 2)
            a, b = ROWS["post_g"]
            pool.dma_start(postg, A["rows"][a:b].partition_broadcast(P)).then_inc(S["postg_in"], 16)
            pool.wait_ge(S["x1_ready"], 1)
            nc.gpsimd.memset(ones, 1.0).then_inc(S["ones_set"], 1)
            for dst, name in ((fwd, "c_fwd"), (inv, "c_inv"), (decay, "c_decay"), (dist, "c_dist")):
                src = A[name]
                if name == "c_fwd" or name == "c_decay":
                    src = src.rearrange("p (a n) -> p a n", a=2)
                elif name == "c_inv":
                    src = src.rearrange("p (a n) -> p a n", a=4)
                pool.dma_start(dst, src).then_inc(S["f_in"], 16)
            pool.dma_start(emb[0:33, :], A["c_emb"]).then_inc(S["f_in"], 16)
            pool.dma_start(fw1[0:33, :], A["filt_w1"]).then_inc(S["f_in"], 16)
            pool.dma_start(fw2[0:64, :], A["filt_w2"]).then_inc(S["f_in"], 16)
            pool.dma_start(w3[0:64, :], A["filt_w3"]).then_inc(S["f_in"], 16)
            a, b = ROWS["lam"]
            pool.dma_start(lamr, A["rows"][a:b].rearrange("(q d) -> q d", q=4).partition_broadcast(P)).then_inc(S["f_in"], 16)
            a, b = ROWS["skip"]
            pool.dma_start(skip, A["rows"][a:b].rearrange("(q d) -> q d", q=2).partition_broadcast(P)).then_inc(S["f_in"], 16)
            pool.wait_ge(S["x2_ready"], 4)
            pool.dma_start(wr, A["w_router"].rearrange("(k p) e -> p k e", p=P)).then_inc(S["r_in"], 16)
            pool.dma_start(slotsr, A["c_slots"]).then_inc(S["r_in"], 16)
            nc.gpsimd.memset(onesT[0:16, :], 1.0).then_inc(S["ones_set"], 1)
            pool.wait_ge(S["x_evac"], KC)
            pool.wait_ge(S["o_evac"], 8)
            a, b = ROWS["final_g"]
            pool.dma_start(finalg, A["rows"][a:b].partition_broadcast(P)).then_inc(S["fg_in"], 16)
            nc.gpsimd.tensor_copy(XC.rearrange("p k c -> p (k c)"), XE[:, 0:KC * CAP]).then_inc(S["xc_ready"], 1)
            nc.gpsimd.tensor_copy(OC.rearrange("p a t -> p (a t)"), OT[:, 0:T]).then_inc(S["oc_ready"], 1)
            with pool.Fori(1, E) as e:
                pool.wait_ge(S["piece_used"], e * 24 - 8)
                nc.gpsimd.tensor_copy(XC.rearrange("p k c -> p (k c)"), XE[:, bass.ds(e * KC * CAP, KC * CAP)]).then_inc(S["xc_ready"], 1)
                pool.wait_ge(S["sc_mm"], e * 2)
                nc.gpsimd.tensor_copy(OC.rearrange("p a t -> p (a t)"), OT[:, bass.ds(e * T, T)]).then_inc(S["oc_ready"], 1)

        @block.scalar
        def _(act):
            act.dma_start(cols, A["cols"]).then_inc(S["params"], 16)
            act.dma_start(csq, A["c_square"]).then_inc(S["params"], 16)
            act.dma_start(bucketT[0:32, :], A["c_bucket"]).then_inc(S["params"], 16)
            act.dma_start(maskT[0:24, :], A["c_mask"]).then_inc(S["params"], 16)
            act.dma_start(relb[0:32, 0:24], A["rel_bias"]).then_inc(S["params"], 16)
            act.dma_start(lowW, A["low_up"]).then_inc(S["params"], 16)
            act.wait_ge(S["xin"], 16)
            for a in range(TT):
                act.activation(hn[:, a, :], xres[:, a, :], ACT.Square, accum_out=small[:, a:a + 1]).then_inc(S["sq_sum"], 1)
            act.wait_ge(S["mean_in"], 1)
            act.activation(small[:, 2:4], small[:, 2:4], ACT.Sqrt).then_inc(S["root_in"], 1)
            for k in range(KC):
                act.wait_ge(S["hT_ready"], k // 2 + 1)
                act.wait_ge(S["params"], 96)
                act.activation(hT[:, k, :], psum[:, k // 2, (k % 2) * T:(k % 2) * T + T], ACT.Copy, scale=col("pre_g", k)).then_inc(S["hT_evac"], 1)

            def evac(j):
                act.wait_ge(S["proj_ready"], j + 1)
                blk, c, rhs, dst, scale = tiles[j]
                n = T if rhs is not None else 512
                if j == 17:
                    act.wait_ge(S["bias_row"], 1)
                    act.wait_ge(S["brow_out"], 16)
                act.activation(dst, psum[:, j % 4, 0:n], ACT.Copy, scale=scale).then_inc(S["proj_evac"], 1)

            for j in range(NT):
                evac(j)
            act.wait_ge(S["proj_evac"], NT)
            act.activation(oaT, zaT, ACT.Exp, scale=-1.0).then_inc(S["za_exp"], 1)
            for n, (h, tile) in enumerate(units):
                w = NG * P * (tile + 1)
                act.wait_ge(S["neg_max"], n + 1)
                act.activation(LG[:, n % 2, 0:w], LG[:, n % 2, 0:w], ACT.Exp, bias=small[:, 8 + n % 2:9 + n % 2],
                               accum_out=small[:, 10 + n % 2:11 + n % 2]).then_inc(S["expd"], 1)
            act.wait_ge(S["low_in"], 1)
            act.activation(prT[0:64, 12, :], prT[0:64, 12, :], ACT.Tanh).then_inc(S["low_t"], 1)
            act.wait_ge(S["low_mm"], 1)
            for f in range(FT):
                act.activation(LD[:, f, :], psum[:, f // 2, (f % 2) * T:(f % 2) * T + T], ACT.Exp, scale=-1.0,
                               bias=small[:, 16 + f:17 + f])
                last = act.activation(AA[:, f, :], psum[:, 2 + f // 2, (f % 2) * T:(f % 2) * T + T], ACT.Exp, scale=-1.0,
                                      bias=small[:, 20 + f:21 + f])
            last.then_inc(S["lowexp"], 1)
            act.wait_ge(S["cs_ready"], 1)
            act.activation(EX1, CS, ACT.Exp).then_inc(S["exps"], 1)
            act.activation(EX2, CS, ACT.Exp, scale=-1.0).then_inc(S["exps"], 1)
            act.wait_ge(S["cs_ready"], 2)
            act.wait_ge(S["exps"], 2)
            act.activation(CS, LD, ACT.Exp).then_inc(S["exps"], 1)
            act.wait_ge(S["norm_mm"], 1)
            act.activation(TMP, psum[:, 4:6, :].rearrange("p a (b c) -> p (a b) c", b=2), ACT.Sqrt).then_inc(S["norm_sqrt"], 1)
            for w, dst in enumerate((TB, TK, TV)):
                for a in range(TT):
                    act.wait_ge(S["tok_tr"], 2 * w + a + 1)
                    act.activation(dst[:, a, :], psum[:, 2 * w + a, :], ACT.Copy).then_inc(S["tok_done"], 1)
            for c in range(NCH):
                act.wait_ge(S["y_mm"], 2 * c + 1)
                a, p0 = c // 2, 64 * (c % 2)
                if c == 0:
                    continue
                act.activation(Y1[p0:p0 + 64, a, :].rearrange("p (q r v) -> p r q v", q=4, r=2),
                               psum[p0:p0 + 64, 2:4, 0:256].rearrange("p a (b c) -> p a b c", b=4), ACT.Copy).then_inc(S["y1_done"], 1)
            act.activation(KK, zrT, ACT.Exp, scale=-1.0).then_inc(S["zr_exp"], 1)
            act.wait_ge(S["mean_in"], 2)
            act.activation(small[:, 64:80], small[:, 64:80], ACT.Sqrt).then_inc(S["root_in"], 1)
            for j in range(16):
                act.wait_ge(S["up_mm"], j + 1)
                dst = (YA if j < 8 else YR)[:, j % 8, :]
                act.activation(dst, psum[:, j % 4, 0:T], ACT.Copy).then_inc(S["up_done"], 1)
            for j in range(16):
                act.wait_ge(S["g_mm"], j + 1)
                if j >= 8:
                    act.wait_ge(S["g_done"], j - 7)
                act.activation(EG[:, j % 8, :], psum[:, 4 + j % 4, 0:T], ACT.Exp, scale=-1.0).then_inc(S["g_exp"], 1)
            for n in range(2):
                for a in range(TT):
                    act.wait_ge(S["out1_mm"], 2 * n + a + 1)
                    act.activation(OUT1[:, a, 512 * n:512 * n + 512], psum[:, 2 * n + a, :], ACT.Copy).then_inc(S["out1_sb"], 1)
            act.wait_ge(S["out1_sb"], 4)
            for a in range(TT):
                act.activation(EG.rearrange("p a b -> p (a b)")[:, a * D:a * D + D], OUT1[:, a, :], ACT.Square, accum_out=small[:, 96 + a:97 + a]).then_inc(S["sq_sum"], 1)
            act.wait_ge(S["mean_in"], 3)
            act.activation(small[:, 98:100], small[:, 98:100], ACT.Sqrt).then_inc(S["root_in"], 1)
            act.wait_ge(S["x1_ready"], 1)
            for a in range(TT):
                act.activation(hn2[:, a, :], xres[:, a, :], ACT.Square, accum_out=small[:, 128 + a:129 + a]).then_inc(S["sq_sum"], 1)
            act.wait_ge(S["mean_in"], 4)
            act.activation(small[:, 130:132], small[:, 130:132], ACT.Sqrt).then_inc(S["root_in"], 1)
            for i in range(2):
                act.wait_ge(S["f_arg"], i + 1)
                act.activation(hid[0:64, :], harg[0:64, :], ACT.Sin).then_inc(S["f_hid"], 1)
            for k in range(4):
                act.wait_ge(S["n2_tr"], k // 2 + 1)
                act.activation(h2T[:, k, :], psum[:, k // 2, (k % 2) * T:(k % 2) * T + T], ACT.Copy, scale=col("attn_g", k)).then_inc(S["n2_evac"], 1)
            for i in range(4):
                act.wait_ge(S["f_abs_in"], i + 1)
                act.activation(fFa, fF, ACT.Abs).then_inc(S["f_abs"], 1)
                act.activation(fBa, fB, ACT.Abs).then_inc(S["f_abs"], 1)
            for j in range(22):
                act.wait_ge(S["p2_ready"], j + 1)
                if j == 0:
                    act.wait_ge(S["f_kdone"], 5)
                if j < 12:
                    act.activation(UPR[:, j, 1:T + 1], psum[:, j % 4, 0:T], ACT.Copy).then_inc(S["p2_evac"], 1)
                elif j < 20:
                    dst = (q2T if j < 16 else k2T)[:, j % 4, :]
                    act.activation(dst, psum[:, j % 4, 0:T], ACT.Copy, scale=0.125 if j < 16 else 1.0).then_inc(S["p2_evac"], 1)
                else:
                    act.activation(v2[:, j - 20, :], psum[:, j % 4, :], ACT.Copy).then_inc(S["p2_evac"], 1)
            for i in range(6):
                act.wait_ge(S["u_tr"], i + 1)
                act.activation(XU[:, i // 2, i % 2, :], psum[:, 4 + i % 4, :], ACT.Copy).then_inc(S["u_evac"], 1)
            act.wait_ge(S["lam_sum"], 1)
            act.activation(small[:, 140:142], small[:, 138:140], ACT.Exp).then_inc(S["lam_exp"], 1)
            act.wait_ge(S["mean_in"], 5)
            act.activation(small[:, 144:160], small[:, 144:160], ACT.Sqrt).then_inc(S["root_in"], 1)
            for n in range(8):
                act.wait_ge(S["l2_neg"], n + 1)
                for c in range(2):
                    act.activation(LG2[:, n % 2, c, :], LG2[:, n % 2, c, :], ACT.Exp, bias=small[:, 176 + 2 * (n % 2) + c:177 + 2 * (n % 2) + c],
                                   accum_out=small[:, 180 + 2 * (n % 2) + c:181 + 2 * (n % 2) + c]).then_inc(S["l2_exp"], 1)
            act.wait_ge(S["o2_mm"], 8)
            act.activation(OA.rearrange("p a h v -> p a (h v)"), psum[:, 6:8, :], ACT.Copy).then_inc(S["o2_sb"], 1)
            act.wait_ge(S["o2_sb"], 1)
            act.activation(OSQ, OA, ACT.Square).then_inc(S["o2_sq"], 1)
            act.wait_ge(S["mean_in"], 6)
            act.activation(small[:, 192:200], small[:, 192:200], ACT.Sqrt).then_inc(S["root_in"], 1)
            act.wait_ge(S["x2_ready"], 4)
            for a in range(TT):
                act.activation(hf[:, a, :], xres[:, a, :], ACT.Square, accum_out=stat[:, a:a + 1]).then_inc(S["sq_sum"], 1)
            act.wait_ge(S["mean_in"], 7)
            act.activation(stat[:, 2:4], stat[:, 2:4], ACT.Sqrt).then_inc(S["root_in"], 1)
            for k in range(KC):
                act.wait_ge(S["n3_tr"], k // 2 + 1)
                act.activation(hfT[:, k, :], psum[:, k // 2, (k % 2) * T:(k % 2) * T + T], ACT.Copy, scale=col("ffn_g", k)).then_inc(S["n3_evac"], 1)
            for a in range(TT):
                act.wait_ge(S["r_neg"], 1)
                act.activation(aff[:, a, :], psum[:, 4, a * E:a * E + E], ACT.Exp, bias=stat[:, 6 + a:7 + a], accum_out=stat[:, 8 + a:9 + a]).then_inc(S["r_exp"], 1)
            for k in range(KC):
                act.wait_ge(S["x_gather"], k + 1)
                dst = XE.rearrange("p (e k c) -> p e k c", e=E, k=KC)[:, :, k, :]
                act.activation(dst, psum[:, k % 4, :].rearrange("p (e c) -> p e c", e=E), ACT.Copy, scale=col("ffn_g", k)).then_inc(S["x_evac"], 1)
            with act.Fori(0, E) as e:
                act.wait_ge(S["piece_used"], e * 24 + 8)
                act.wait_ge(S["h_ready"], e + 1)
                act.activation(GE.rearrange("p (n x) -> p n x", n=2), psum[:, 0:2, 0:HALFQ], ACT.Exp, scale=-1.0).then_inc(S["g_expd"], 1)
                act.wait_ge(S["piece_used"], e * 24 + 24)
                act.wait_ge(S["acc_done"], e * 2 + 1)
                act.activation(YS, psum[:, 4:6, :], ACT.Copy).then_inc(S["y3_sb"], 1)
            act.wait_ge(S["acc_done"], 2 * E + 1)
            for a in range(TT):
                act.activation(hfT.rearrange("p k t -> p (k t)")[:, a * D:a * D + D], xres[:, a, :], ACT.Square, accum_out=small[:, 224 + a:225 + a]).then_inc(S["sq_sum"], 1)
            act.wait_ge(S["mean_in"], 8)
            act.activation(small[:, 226:228], small[:, 226:228], ACT.Sqrt).then_inc(S["root_in"], 1)

        @block.tensor
        def _(pe):
            mm = nc.tensor.matmul
            pe.wait_ge(S["params"], 96)
            pe.wait_ge(S["params"], 96)
            mm(psum[0:24, 7, 0:384], relb[0:32, 0:24], bucketT[0:32, :], start=True, stop=True).then_inc(S["bias_mm"], 1)
            pe.wait_ge(S["hn_ready"], 1)
            for k in range(KC):
                for a in range(TT):
                    o = (k % 2) * T + a * P
                    last = nc.tensor.transpose(psum[:, k // 2, o:o + P], hn[:, a, k * P:k * P + P], ident)
                if k % 2:
                    last.then_inc(S["hT_ready"], 1)
            pe.wait_ge(S["bias_row"], 1)
            for k in range(KC):
                for a in range(TT):
                    o = (k % 2) * T + (1 - a) * P
                    last = nc.tensor.transpose(psum[:, 4 + k // 2, o:o + P], hn[:, a, k * P:k * P + P], anti)
                if k % 2:
                    last.then_inc(S["hT_ready"], 1)

            pe.wait_ge(S["hT_evac"], KC)
            for j, (blk, c, rhs, dst, scale) in enumerate(tiles):
                n = number[blk]
                pe.wait_ge(wload[n % 4], 16 * (n // 4 + 1))
                if rhs is hR or rhs is None:
                    pe.wait_ge(S["hR_evac"], KC)
                if j >= 4:
                    pe.wait_ge(S["proj_evac"], j - 3)
                for k in range(KC):
                    if rhs is not None:
                        last = mm(psum[:, j % 4, 0:T], block_of(blk)[:, k, c * P:c * P + P], rhs[:, k, :], start=(k == 0), stop=(k == KC - 1))
                    else:
                        last = mm(psum[:, j % 4, :], hR[:, k, c * P:c * P + P], block_of(blk)[:, k, :], start=(k == 0), stop=(k == KC - 1))
                last.then_inc(S["proj_ready"], 1)
                if j == NT - 1 or tiles[j + 1][0] != blk:
                    pe.wait_ge(S["proj_ready"], j + 1)
                    pe.nop().then_inc(S["w_used"], 1)

            def logits(n):
                h, tile = units[n]
                b = 2 * (n % 2)
                w = P * (tile + 1)
                if n >= 2:
                    pe.wait_ge(S["neg_max"], n - 1)
                r = 64 * (h % 2)
                for g in range(NG):
                    t = 4 * g + h // 2
                    last = mm(psum[:, b + g * w // 512, (g * w) % 512:(g * w) % 512 + w],
                              qT[r:r + 64, t, tile * P:tile * P + P], kT[r:r + 64, t, T - w:T] if tile == 0 else kT[r:r + 64, t, :],
                              start=True, stop=True)
                last.then_inc(S["logit_ready"], 1)

            def turned(n):
                h, tile = units[n]
                pe.wait_ge(S["prob_ready"], n + 1)
                for half in range(tile + 1):
                    m = 0
                    i = (n // 2) * 3 + (n % 2) * 2 + half
                    if i >= 2:
                        pe.wait_ge(S["pt_done"], i - 1)
                    for g in range(NG):
                        o = (g * (tile + 1) + half) * P
                        last = nc.tensor.transpose(psum[:, 4 + i % 2, g * P:g * P + P], LG[:, n % 2, o:o + P], ident)
                    last.then_inc(S["pt_ready"], 1)

            def values(n):
                h, tile = units[n]
                r = 64 * (h % 2)
                ob = 6 + h % 2
                if tile == 1 and h >= 2:
                    pe.wait_ge(S["o_done"], h - 1)
                for half in range(tile + 1):
                    i = (n // 2) * 3 + (n % 2) * 2 + half
                    pe.wait_ge(S["pt_done"], i + 1)
                    for g in range(NG):
                        u = half if tile else 1
                        last = mm(psum[r:r + 64, ob, tile * P:tile * P + P], vR[:, u, g * AW + h * HD:g * AW + h * HD + HD],
                                  PT[:, i % 2, 0, g, :], start=(g == 0 and half == 0), stop=(g == NG - 1 and half == tile))
                if tile == 0:
                    last.then_inc(S["o_ready"], 1)

            pe.wait_ge(S["proj_evac"], NT)
            pe.wait_ge(S["bias_in"], 48)
            logits(0)
            for n in range(NU):
                if n + 1 < NU:
                    logits(n + 1)
                turned(n)
                values(n)

            pe.wait_ge(S["params"], 96)
            pe.wait_ge(S["low_t"], 1)
            for f in range(FT):
                mm(psum[:, f // 2, (f % 2) * T:(f % 2) * T + T], lowW[0:64, f * P:f * P + P], prT[0:64, 12, :], start=True, stop=True)
            for f in range(FT):
                last = mm(psum[:, 2 + f // 2, (f % 2) * T:(f % 2) * T + T], lowW[64:128, f * P:f * P + P], prT[64:128, 12, :], start=True, stop=True)
            last.then_inc(S["low_mm"], 1)
            pe.wait_ge(S["sq_ready"], 1)
            pe.wait_ge(S["pt_done"], 24)
            for f in range(FT):
                last = mm(psum[:, 4 + f // 2, (f % 2) * T:(f % 2) * T + T], BLK1, TMP[:, f, :], start=True, stop=True)
            last.then_inc(S["norm_mm"], 1)
            pe.wait_ge(S["sq_ready"], 2)
            pe.wait_ge(S["o_done"], NH)
            for a in range(TT):
                for f in range(FT):
                    last = mm(psum[:, 6, a * 8 + 2 * f:a * 8 + 2 * f + 2], CS[:, f, a * P:a * P + P], small[:, 24 + 2 * f:26 + 2 * f], start=True, stop=True)
            last.then_inc(S["bonus_mm"], 1)
            pe.wait_ge(S["ab_ready"], 1)
            pe.wait_ge(S["norm_sqrt"], 1)
            for w, src in enumerate((BT, KT, prT[:, 8:12, :])):
                for a in range(TT):
                    if w == 2:
                        pe.wait_ge(S["tok_done"], 1)
                    for f in range(FT):
                        last = nc.tensor.transpose(psum[:, 2 * w + a, f * P:f * P + P], src[:, f, a * P:a * P + P], ident)
                    last.then_inc(S["tok_tr"], 1)
            pe.wait_ge(S["tok_done"], 6)
            for cp in range(2):
                if cp:
                    pe.wait_ge(S["gram_done"], 5)
                for h in order:
                    r, f = 64 * (h % 2), h // 2
                    for c in (2 * cp, 2 * cp + 1):
                        o = 64 * (c % 2)
                        ar = AR[r:r + 64, f, c, :, :].rearrange("p a b -> p (a b)")
                        q = (h // 2) * 128
                        mm(psum[o:o + 64, h % 2, q:q + 128], BT[r:r + 64, f, c * CH:c * CH + CH], ar, start=True, stop=True)
                        last = mm(psum[o:o + 64, 2 + h % 2, q:q + 128], KT[r:r + 64, f, c * CH:c * CH + CH], ar, start=True, stop=True)
                last.then_inc(S["gram_mm"], 1)
                for h in order:
                    r, f = 64 * (h % 2), h // 2
                    for c in (2 * cp, 2 * cp + 1):
                        o = 64 * (c % 2)
                        last = mm(psum[o:o + 64, 4 + h % 2, (h // 2) * 64:(h // 2) * 64 + 64], AR[r:r + 64, f, c, 0, :],
                                  BT[r:r + 64, f, c * CH:c * CH + CH], start=True, stop=True)
                last.then_inc(S["gram_mm"], 1)

            def pairs(bank, lhs, rhs):
                for par in range(2):
                    for cp in range(2):
                        p0 = 64 * par
                        for i in range(NH):
                            last = mm(psum[p0:p0 + 64, bank + cp, i * CH:i * CH + CH], lhs[p0:p0 + 64, cp, i, :], rhs[p0:p0 + 64, cp, i, :],
                                      start=True, stop=True)
                return last

            pe.wait_ge(S["gram_done"], 10)
            for lev in range(5):
                pe.wait_ge(S["MM_done"], 2 * lev + 3)
                pairs(0, mOff, mMT).then_inc(S["T1_mm"], 1)
                pe.wait_ge(S["T1_done"], lev + 1)
                pairs(2, mM, mT1).then_inc(S["MM_mm"], 1)
                pairs(4, mT1, mM).then_inc(S["MM_mm"], 1)
            for par in range(2):
                for cp in range(2):
                    p0 = 64 * par
                    for h in range(NH):
                        last = mm(psum[p0:p0 + 64, 6 + cp, hh(h) * CH:hh(h) * CH + CH], mAk[p0:p0 + 64, cp, hh(h), :],
                                  TV[p0:p0 + 64, cp, h * CH:h * CH + CH], start=True, stop=True)
            last.then_inc(S["xv_mm"], 1)
            pe.wait_ge(S["MM_done"], 13)
            pe.wait_ge(S["xv_done"], 1)
            for c in range(NCH):
                cp, p0 = c // 2, 64 * (c % 2)
                if c:
                    pe.wait_ge(S["s_done"], c)
                    for h in order:
                        r, f = 64 * (h % 2), h // 2
                        last = mm(psum[p0:p0 + 64, h % 2, f * CH:f * CH + CH], AR[r:r + 64, f, c, 0, :], ST[r:r + 64, f, :], start=True, stop=True)
                    last.then_inc(S["x_mm"], 1)
                    if c >= 2:
                        pe.wait_ge(S["y1_done"], c - 1)
                    for h in order:
                        r, f = 64 * (h % 2), h // 2
                        last = mm(psum[p0:p0 + 64, 2 + h % 2, f * CH:f * CH + CH], AR[r:r + 64, f, c, 1, :], ST[r:r + 64, f, :], start=True, stop=True)
                    last.then_inc(S["y_mm"], 1)
                    pe.wait_ge(S["x_done"], c)
                else:
                    pe.nop().then_inc(S["y_mm"], 1)
                for h in range(NH):
                    rhs = XS[p0:p0 + 64, hh(h), :] if c else XV[p0:p0 + 64, 0, hh(h), :]
                    last = mm(psum[p0:p0 + 64, 4, hh(h) * CH:hh(h) * CH + CH], mMT[p0:p0 + 64, cp, hh(h), :], rhs, start=True, stop=True)
                last.then_inc(S["u_mm"], 1)
                pe.wait_ge(S["u_done"], c + 1)
                for h in range(NH):
                    r, f = 64 * (h % 2), h // 2
                    mm(psum[r:r + 64, 5, f * CH:f * CH + CH], TB[p0:p0 + 64, cp, h * CH:h * CH + CH], USB[p0:p0 + 64, hh(h), :], start=True, stop=False)
                    last = mm(psum[r:r + 64, 5, f * CH:f * CH + CH], TK[p0:p0 + 64, cp, h * CH:h * CH + CH], TV[p0:p0 + 64, cp, h * CH:h * CH + CH],
                              start=False, stop=True)
                last.then_inc(S["s_mm"], 1)
                if c == 1:
                    pe.wait_ge(S["xv_done"], 1)
                for h in range(NH):
                    o = psum[p0:p0 + 64, 6 + cp, hh(h) * CH:hh(h) * CH + CH]
                    mm(o, mRb[p0:p0 + 64, cp, hh(h), :], USB[p0:p0 + 64, hh(h), :], start=True, stop=False)
                    last = mm(o, mRk[p0:p0 + 64, cp, hh(h), :], TV[p0:p0 + 64, cp, h * CH:h * CH + CH], start=False, stop=True)
                last.then_inc(S["y_mm"], 1)
            for a in range(TT):
                pe.wait_ge(S["gn_done"], 1)
                for f in range(FT):
                    last = nc.tensor.transpose(psum[:, a, f * P:f * P + P], Y[:, a, f * P:f * P + P], ident)
                last.then_inc(S["or_mm"], 1)
            for j in range(16):
                name, src = ("upa", oaT) if j < 8 else ("upr", orT)
                pe.wait_ge(wload[number[name] % 4], 16 * (number[name] // 4 + 1))
                if j == 0:
                    pe.wait_ge(S["o_done"], NH)
                    pe.wait_ge(S["or_done"], 2)
                if j >= 4:
                    pe.wait_ge(S["up_done"], j - 3)
                for f in range(FT):
                    last = mm(psum[:, j % 4, 0:T], wb_up[number[name] % 4][:, f, (j % 8) * P:(j % 8) * P + P], src[:, f, :], start=(f == 0), stop=(f == FT - 1))
                last.then_inc(S["up_mm"], 1)
                if j % 8 == 7:
                    pe.wait_ge(S["up_mm"], j + 1)
                    pe.nop().then_inc(S["w_used"], 1)
            for j in range(16):
                name = f"g{j // 4}"
                pe.wait_ge(wload[number[name] % 4], 16 * (number[name] // 4 + 1))
                if j >= 4:
                    pe.wait_ge(S["g_exp"], j - 3)
                for k in range(KC):
                    last = mm(psum[:, 4 + j % 4, 0:T], block_of(name)[:, k, (j % 4) * P:(j % 4) * P + P], hT[:, k, :], start=(k == 0), stop=(k == KC - 1))
                last.then_inc(S["g_mm"], 1)
                if j % 4 == 3:
                    pe.wait_ge(S["g_mm"], j + 1)
                    pe.nop().then_inc(S["w_used"], 1)
            pe.wait_ge(S["g_done"], 16)
            pe.wait_ge(S["up_done"], 16)
            for n in range(2):
                name = f"out{n}"
                pe.wait_ge(wload[number[name] % 4], 16 * (number[name] // 4 + 1))
                for a in range(TT):
                    for k in range(KC):
                        last = mm(psum[:, 2 * n + a, :], MG[:, k, a * P:a * P + P], block_of(name)[:, k, :], start=(k == 0), stop=(k == KC - 1))
                    last.then_inc(S["out1_mm"], 1)
                pe.wait_ge(S["out1_mm"], 2 * n + 2)
                pe.nop().then_inc(S["w_used"], 1)
            pe.wait_ge(S["f_in"], 160)
            mm(psum[0:64, 7, 0:T], fw1[0:33, :], emb[0:33, :], start=True, stop=True).then_inc(S["f_mm"], 1)
            pe.wait_ge(S["f_hid"], 1)
            mm(psum[0:64, 7, 0:T], fw2[0:64, :], hid[0:64, :], start=True, stop=True).then_inc(S["f_mm"], 1)
            pe.wait_ge(S["hn_ready"], 2)
            for k in range(KC):
                for a in range(TT):
                    o = (k % 2) * T + a * P
                    last = nc.tensor.transpose(psum[:, k // 2, o:o + P], hn2[:, a, k * P:k * P + P], ident)
                if k % 2:
                    last.then_inc(S["n2_tr"], 1)
            pe.wait_ge(S["f_hid"], 2)
            pe.wait_ge(S["ones_set"], 1)
            for i in range(4):
                a, o = i // 2, i % 2
                if i:
                    pe.wait_ge(S["f_abs_in"], i)
                for w in range(2):
                    c0 = (2 * w + o) * 512
                    last = mm(psum[:, 4 + w, :], hid[0:64, a * P:a * P + P], w3[0:64, c0:c0 + 512], start=True, stop=True)
                last.then_inc(S["f_w3mm"], 1)
                pe.wait_ge(S["f_abs"], 2 * i + 2)
                mm(psum[:, 6 + o, :], ones, fFa, start=(a == 0), stop=False)
                mm(psum[:, 6 + o, :], ones, fBa, start=False, stop=(a == 1)).then_inc(S["f_norm"], 1)
            pe.wait_ge(S["f_sd"], 4)
            pe.wait_ge(S["n2_evac"], 4)
            pe.wait_ge(S["n2_evac2"], 4)
            for i, (c0, src) in enumerate(((0, fS), (P, fS), (2 * P, fD), (3 * P, fD), (4 * P, fS))):
                if i >= 2:
                    pe.wait_ge(S["f_kdone"], i - 1)
                for o in range(2):
                    for a in range(TT):
                        last = mm(psum[:, 2 * (i % 2) + o, :], fwd[:, a, c0:c0 + P], src[:, a, o, :], start=(a == 0), stop=(a == 1))
                last.then_inc(S["f_kmm"], 1)
            pe.wait_ge(S["f_kdone"], 5)
            for j in range(22):
                b = j // 4 if j < 20 else 5
                name = f"hy{b}" if b < 3 else f"at{b - 3}"
                weights_in(pe, name)
                if j >= 4:
                    pe.wait_ge(S["p2_evac"], j - 3)
                for k in range(KC):
                    if j < 20:
                        last = mm(psum[:, j % 4, 0:T], block_of(name)[:, k, (j % 4) * P:(j % 4) * P + P], h2T[:, k, :], start=(k == 0), stop=(k == KC - 1))
                    else:
                        last = mm(psum[:, j % 4, :], h2T[:, k, (j - 20) * P:(j - 20) * P + P], block_of(name)[:, k, :], start=(k == 0), stop=(k == KC - 1))
                last.then_inc(S["p2_ready"], 1)
                if j in (3, 7, 11, 15, 19, 21):
                    pe.wait_ge(S["p2_ready"], j + 1)
                    pe.nop().then_inc(S["w_used"], 1)
            for i in range(6):
                pe.wait_ge(S["u_conv"], i // 2 + 1)
                if i >= 4:
                    pe.wait_ge(S["u_evac"], i - 3)
                for f in range(4):
                    last = nc.tensor.transpose(psum[:, 4 + i % 4, f * P:f * P + P], UC[:, 4 * (i // 2) + f, (i % 2) * P:(i % 2) * P + P], ident)
                last.then_inc(S["u_tr"], 1)
            for n in range(2):
                z = XU[:, 2, :, :]
                if n == 0:
                    pe.wait_ge(S["u_evac"], 6)
                    pe.wait_ge(S["p2_evac"], 22)
                else:
                    pe.wait_ge(S["z_done"], 1)
                for j, c0 in enumerate((0, P, 5 * P, 3 * P)):
                    for a in range(TT):
                        last = mm(psum[:, j, :], fwd[:, a, c0:c0 + P], z[:, a, :], start=(a == 0), stop=(a == 1))
                last.then_inc(S["z_mm"], 1)
                pe.wait_ge(S["spec"], n + 1)
                for a in range(TT):
                    for j in range(4):
                        last = mm(psum[:, 4 + a, :], inv[:, j, a * P:a * P + P], SPY[:, j // 2, j % 2, :], start=(j == 0), stop=(j == 3))
                last.then_inc(S["i_mm"], 1)
            pe.wait_ge(S["hy_norm"], 1)
            for f in range(4):
                for a in range(TT):
                    o = (f % 2) * T + a * P
                    last = nc.tensor.transpose(psum[:, 4 + f // 2, o:o + P], ZN[:, a, f * P:f * P + P], ident)
                if f % 2:
                    last.then_inc(S["m_tr"], 1)
            def logits2(n):
                h, tile = n // 2, n % 2
                if n >= 2:
                    pe.wait_ge(S["l2_neg"], n - 1)
                for c in range(2):
                    r = 64 * c
                    last = mm(psum[:, 2 * (n % 2) + c, 0:T], q2T[r:r + 64, h, tile * P:tile * P + P], k2T[r:r + 64, h, :], start=True, stop=True)
                last.then_inc(S["l2_mm"], 1)
            pe.wait_ge(S["m_evac"], 4)
            logits2(0)
            for n in range(8):
                if n < 7:
                    logits2(n + 1)
                h, tile = n // 2, n % 2
                pe.wait_ge(S["l2_prob"], n + 1)
                if n >= 2:
                    pe.wait_ge(S["l2_turned"], n - 1)
                for s in range(TT):
                    last = nc.tensor.transpose(psum[:, 4 + n % 2, s * P:s * P + P], LG2[:, n % 2, 0, s * P:s * P + P], ident)
                last.then_inc(S["l2_tr"], 1)
                pe.wait_ge(S["l2_turned"], n + 1)
                for s in range(TT):
                    last = mm(psum[:, 6 + tile, h * P:h * P + P], PT2[:, n % 2, s, :], v2[:, s, h * P:h * P + P], start=(s == 0), stop=(s == 1))
                last.then_inc(S["o2_mm"], 1)
            pe.wait_ge(S["o2_norm"], 1)
            for f in range(4):
                for a in range(TT):
                    o = (f % 2) * T + a * P
                    last = nc.tensor.transpose(psum[:, f // 2, o:o + P], OA[:, a, f, :], ident)
                if f % 2:
                    last.then_inc(S["m2_tr"], 1)
            pe.wait_ge(S["m2_evac"], 4)
            for n in range(2):
                name = f"out2_{n}"
                weights_in(pe, name)
                for a in range(TT):
                    for k in range(KC):
                        last = mm(psum[:, 2 + 2 * n + a, :], mixT[:, k, a * P:a * P + P], block_of(name)[:, k, :], start=(k == 0), stop=(k == KC - 1))
                    last.then_inc(S["x2_mm"], 1)
                pe.wait_ge(S["x2_mm"], 2 * n + 2)
                pe.nop().then_inc(S["w_used"], 1)
            pe.wait_ge(S["hn_ready"], 3)
            for k in range(KC):
                for a in range(TT):
                    o = (k % 2) * T + a * P
                    last = nc.tensor.transpose(psum[:, k // 2, o:o + P], hf[:, a, k * P:k * P + P], ident)
                if k % 2:
                    last.then_inc(S["n3_tr"], 1)
            pe.wait_ge(S["r_in"], 32)
            for a in range(TT):
                for k in range(KC):
                    pe.wait_ge(S["n3_evac"], k + 1)
                    last = mm(psum[:, 4, a * E:a * E + E], hfT[:, k, a * P:a * P + P], wr[:, k, :], start=(k == 0), stop=(k == KC - 1))
            last.then_inc(S["r_mm"], 1)
            pe.wait_ge(S["aff_ready"], 1)
            for a in range(TT):
                last = nc.tensor.transpose(psum[0:E, 5, a * P:a * P + P], aff[:, a, :], ident)
            last.then_inc(S["aff_tr"], 1)
            pe.wait_ge(S["rank_ready"], 1)
            for a in range(TT):
                last = nc.tensor.transpose(psum[:, 6, a * E:a * E + E], work[0][0:E, a * P:a * P + P], ident[0:E, 0:E])
            last.then_inc(S["rank_tr"], 1)
            pe.wait_ge(S["ohot_ready"], 1)
            for k in range(KC):
                if k >= 4:
                    pe.wait_ge(S["x_evac"], k - 3)
                for a in range(TT):
                    last = mm(psum[:, k % 4, :], hf[:, a, k * P:k * P + P], ohot[:, a, :, :].rearrange("p e c -> p (e c)"), start=(a == 0), stop=(a == 1))
                last.then_inc(S["x_gather"], 1)
            for q in range(8):
                pe.wait_ge(S["og_ready"], q + 1)
                if q >= 4:
                    pe.wait_ge(S["o_evac"], q - 3)
                for i in range(4):
                    e, a = (4 * q + i) // 2, i % 2
                    last = nc.tensor.transpose(psum[:, 4 + q % 4, i * P:i * P + P], og4[:, 2 * (q % 2) + a, e % 2, :], ident)
                last.then_inc(S["o_tr"], 1)
            with pe.Fori(0, E) as e:
                pe.wait_ge(S["xc_ready"], e + 1)
                pe.wait_ge(S["x_evac"], KC)
                pe.wait_ge(S["h_ready"], e + 1)
                for i in range(16):
                    pe.wait_ge(arrived[i % SLOTS], e * 32 + 16 * (i // SLOTS + 1))
                    w = slot(i % SLOTS)
                    k, b = i % 8, 2 * (i // 8)
                    for n in range(2):
                        for j in range(4):
                            c0 = j * QUARTER + n * HALFQ
                            last = mm(psum[32 * j:32 * j + CAP, b + n, 0:HALFQ], XC[:, k, :], w[:, c0:c0 + HALFQ], start=(k == 0), stop=(k == KC - 1))
                    last.then_inc(S["piece_used"], 1)
                pe.wait_ge(S["h_ready"], e + 2)
                pe.wait_ge(S["acc_done"], e * 2 + 1)
                seen = 0
                for i in range(FPP):
                    need = -(-(i + 1) * D // PIECE)
                    while seen < need:
                        pe.wait_ge(arrived[4 + seen], e * 32 + 32)
                        seen += 1
                    g = i % 4
                    for n in range(2):
                        o = 4 * PIECE + i * D + n * 512
                        last = mm(psum[32 * g:32 * g + CAP, 4 + n, :], HT[:, i, :], region(o, 512), start=(i < 4), stop=(i >= FPP - 4))
                    if (i + 1) * D // PIECE > i * D // PIECE:
                        last.then_inc(S["piece_used"], 1)
                pe.wait_ge(S["y3_sb"], e + 1)
                pe.wait_ge(S["oc_ready"], e + 1)
                for a in range(TT):
                    for n in range(2):
                        last = mm(psum[:, (6 if a == 0 else 4) + n, :], OC[:, a, :], YS[:, n, :], start=True, stop=True)
                    last.then_inc(S["sc_mm"], 1)

        @block.vector
        def _(dve):
            V = nc.vector
            link = Line(dve, S["dve_line"])
            dve.wait_ge(S["sq_sum"], 2)
            V.tensor_scalar(small[:, 2:4], small[:, 0:2], 1.0 / D, 1e-6, ALU.mult, ALU.add).then_inc(S["mean_in"], 1)
            dve.wait_ge(S["root_in"], 1)
            link(V.reciprocal(small[:, 4:6], small[:, 2:4]))
            for a in range(TT):
                last = V.tensor_scalar(hn[:, a, :], xres[:, a, :], small[:, 4 + a:5 + a], None, ALU.mult)
            last.then_inc(S["hn_ready"], 1)
            dve.wait_ge(S["params"], 96)
            dve.wait_ge(S["params"], 96)
            dve.wait_ge(S["bias_mm"], 1)
            V.tensor_tensor(brow[0:24, :], psum[0:24, 7, 0:384], maskT[0:24, :], ALU.add).then_inc(S["bias_row"], 1)
            V.tensor_scalar(small[:, 16:24], cols[:, COLS["w0"][0]:COLS["a0"][1]], -1.0, None, ALU.mult)
            dve.wait_ge(S["params"], 96)
            for f in range(FT):
                V.tensor_scalar(small[:, 24 + 2 * f:26 + 2 * f], TWO, col("r_k", f), None, ALU.mult)
            for k in range(KC):
                dve.wait_ge(S["hT_ready"], 5 + k // 2)
                V.tensor_scalar(hR[:, k, :], psum[:, 4 + k // 2, (k % 2) * T:(k % 2) * T + T], col("pre_g", k), None, ALU.mult).then_inc(S["hR_evac"], 1)

            for i in range(4):
                n = 4 if i < 3 else 1
                dve.wait_ge(S["proj_evac"], min(1 + 4 * (i + 1), 13))
                src = prT[:, 4 * i:4 * i + n, :]
                V.tensor_scalar(TMP[:, 0:n, 0:1], src[:, :, 0:1], -1.0, None, ALU.mult)
                link(V.tensor_tensor(TMP[:, 0:n, 1:T], src[:, :, 0:T - 1], src[:, :, 1:T], ALU.subtract))
                for f in range(n):
                    last = V.scalar_tensor_tensor(src[:, f, :], TMP[:, f, :], col("mix", 4 * i + f), src[:, f, :], ALU.mult, ALU.add)
                link(last)
            V.memset(small[:, 200:201], 0.0).then_inc(S["low_in"], 1)

            for n, (h, tile) in enumerate(units):
                w = P * (tile + 1)
                b = 2 * (n % 2)
                i = n % 2
                dve.wait_ge(S["logit_ready"], n + 1)
                dve.wait_ge(S["bias_in"], 48)
                if n >= 2:
                    m = units[n - 2]
                    dve.wait_ge(S["pt_ready"], (n // 2 - 1) * 3 + (2 if n % 2 == 0 else 3))
                src = psum[:, b:b + 2, :].rearrange("p a b -> p (a b)")[:, 0:NG * w].rearrange("p (g u) -> p g u", g=NG)
                dst = LG[:, i, 0:NG * w]
                link(V.tensor_tensor(dst.rearrange("p (g u) -> p g u", g=NG), src, bias[:, h, :, 0:w], ALU.add))
                V.tensor_reduce(small[:, 8 + i:9 + i], dst, AX.X, ALU.max, negate=True).then_inc(S["neg_max"], 1)
                dve.wait_ge(S["expd"], n + 1)
                link(V.reciprocal(small[:, 12 + i:13 + i], small[:, 10 + i:11 + i]))
                V.tensor_scalar(dst, dst, small[:, 12 + i:13 + i], None, ALU.mult).then_inc(S["prob_ready"], 1)
                for half in range(tile + 1):
                    q = (n // 2) * 3 + (n % 2) * 2 + half
                    dve.wait_ge(S["pt_ready"], q + 1)
                    V.tensor_copy(PT[:, q % 2, 0, :, :], psum[:, 4 + q % 2, 0:NG * P].rearrange("p (g u) -> p g u", g=NG)).then_inc(S["pt_done"], 1)
                if tile == 0 and h == 0:
                    dve.wait_ge(S["za_exp"], 1)
                    link(V.tensor_scalar(oaT, oaT, 1.0, None, ALU.add))
                    link(V.reciprocal(oaT, oaT))
                    link(V.tensor_tensor(zaT, zaT, oaT, ALU.mult))
                if tile == 0:
                    r = 64 * (h % 2)
                    dve.wait_ge(S["o_ready"], h + 1)
                    V.tensor_tensor(oaT[r:r + 64, h // 2, :], psum[r:r + 64, 6 + h % 2, 0:T], zaT[r:r + 64, h // 2, :], ALU.mult).then_inc(S["o_done"], 1)

            r4, k4 = prT[:, 0:4, :], prT[:, 4:8, :]
            for f in range(FT):
                last = V.tensor_scalar(KK[:, f, :], k4[:, f, :], col("k_k", f), None, ALU.mult)
            link(last)
            V.tensor_tensor(TMP, KK, KK, ALU.mult).then_inc(S["sq_ready"], 1)
            dve.wait_ge(S["lowexp"], 1)
            link(V.tensor_scalar(LD, LD, 1.0, None, ALU.add))
            link(V.reciprocal(LD, LD))
            link(V.tensor_scalar(LD, LD, -E_HALF, None, ALU.mult))
            link(V.tensor_scalar(AA, AA, 1.0, None, ALU.add))
            link(V.reciprocal(AA, AA))
            for f in range(FT):
                last = V.tensor_tensor_scan(CS[:, f, :], CSTART, LD[:, f, :], 0.0, ALU.mult, ALU.add)
            link(last)
            V.tensor_tensor(LD, CS, LD, ALU.subtract).then_inc(S["cs_ready"], 1)
            dve.wait_ge(S["cs_ready"], 1)
            V.memset(small[:, 203:204], 0.0).then_inc(S["cs_ready"], 1)
            dve.wait_ge(S["norm_sqrt"], 1)
            link(V.tensor_scalar(TMP, TMP, 1e-12, None, ALU.max))
            link(V.reciprocal(TMP, TMP))
            link(V.tensor_tensor(KK, KK, TMP, ALU.mult))
            for f in range(FT):
                last = V.tensor_scalar(TMP[:, f, :], AA[:, f, :], 1.0, col("k_a", f), ALU.subtract, ALU.mult)
            link(last)
            link(V.scalar_tensor_tensor(k4, TMP, 1.0, k4, ALU.add, ALU.mult))
            dve.wait_ge(S["exps"], 3)
            arv = AR.rearrange("p f c a t -> p (f c) a t")
            def chunks(x):
                return x.rearrange("p f (c t) -> p (f c) t", c=NCH)
            V.scalar_tensor_tensor(arv[:, :, 0, :], chunks(KK), -1.0, chunks(CS), ALU.mult, ALU.mult)
            V.tensor_tensor(arv[:, :, 1, :], chunks(r4), chunks(EX1), ALU.mult)
            link(V.tensor_tensor(AA, KK, AA, ALU.mult))
            V.tensor_tensor(BT, AA, EX2, ALU.mult)
            V.tensor_tensor(KT, k4, EX2, ALU.mult)
            PC = small[:, 32:48].rearrange("p (f c) -> p f c", f=FT)
            link(V.tensor_copy(PC, EX1.rearrange("p f (c t) -> p f c t", c=NCH)[:, :, :, CH - 1]))
            V.tensor_tensor(CS, r4, k4, ALU.mult).then_inc(S["sq_ready"], 1)
            dve.wait_ge(S["sq_ready"], 2)
            V.memset(small[:, 204:205], 0.0).then_inc(S["ab_ready"], 1)
            dve.wait_ge(S["bonus_mm"], 1)
            link(V.tensor_copy(small[:, 48:64], psum[:, 6, 0:16]))

            def masked(dst, cp, bank, off, step, mask):
                src = psum[:, bank:bank + 2, :].rearrange("p b (q w) -> p b q w", w=step)[:, :, 0:4, off:off + CH]
                return V.tensor_tensor(dst[:, cp, :, :].rearrange("p (b q) w -> p b q w", b=2), src, spread(spread(mask, 1, 4), 1, 2), ALU.mult)
            for cp in range(2):
                dve.wait_ge(S["gram_mm"], 2 * cp + 1)
                masked(mN, cp, 0, 0, 128, US).then_inc(S["gram_done"], 1)
                masked(mRb, cp, 0, 64, 128, UI).then_inc(S["gram_done"], 1)
                masked(mAk, cp, 2, 0, 128, US).then_inc(S["gram_done"], 1)
                masked(mRk, cp, 2, 64, 128, UI).then_inc(S["gram_done"], 1)
                dve.wait_ge(S["gram_mm"], 2 * cp + 2)
                masked(mA, cp, 4, 0, 64, LS).then_inc(S["gram_done"], 1)
            dve.wait_ge(S["gram_done"], 10)
            def flat(x):
                return x.rearrange("p a h t -> p (a h) t")
            def over(mask):
                return spread(mask, 1, 16)
            link(V.tensor_tensor(flat(mMT), flat(mN), over(US2), ALU.mult))
            link(V.tensor_tensor(flat(mM), flat(mA), over(LS2), ALU.mult))
            V.tensor_tensor(flat(mMT), flat(mMT), over(I64), ALU.add).then_inc(S["MM_done"], 1)
            V.tensor_tensor(flat(mM), flat(mM), over(I64), ALU.add).then_inc(S["MM_done"], 1)
            V.tensor_tensor(flat(mOff), flat(mA), over(OFFB[0]), ALU.mult).then_inc(S["MM_done"], 1)
            for lev in range(5):
                dve.wait_ge(S["T1_mm"], lev + 1)
                V.tensor_copy(mT1.rearrange("p a h t -> p a (h t)"), psum[:, 0:2, :]).then_inc(S["T1_done"], 1)
                if lev < 4:
                    link(V.tensor_tensor(flat(mOff), flat(mA), over(OFFB[lev + 1]), ALU.mult))
                dve.wait_ge(S["MM_mm"], 2 * lev + 2)
                V.tensor_tensor(mMT.rearrange("p a h t -> p a (h t)"), psum[:, 2:4, :], mMT.rearrange("p a h t -> p a (h t)"), ALU.add).then_inc(S["MM_done"], 1)
                V.tensor_tensor(mM.rearrange("p a h t -> p a (h t)"), psum[:, 4:6, :], mM.rearrange("p a h t -> p a (h t)"), ALU.add).then_inc(S["MM_done"], 1)
            dve.wait_ge(S["xv_mm"], 1)
            V.tensor_copy(XV.rearrange("p a h t -> p a (h t)"), psum[:, 6:8, :]).then_inc(S["xv_done"], 1)
            for c in range(NCH):
                cp, p0 = c // 2, 64 * (c % 2)
                if c:
                    dve.wait_ge(S["x_mm"], c)
                    V.tensor_tensor(XS[p0:p0 + 64, :, :].rearrange("p (b q) w -> p b (q w)", b=2), psum[p0:p0 + 64, 0:2, 0:256],
                                    XV[p0:p0 + 64, cp, :, :].rearrange("p (b q) w -> p b (q w)", b=2), ALU.add).then_inc(S["x_done"], 1)
                dve.wait_ge(S["u_mm"], c + 1)
                V.tensor_copy(USB[p0:p0 + 64, :, :].rearrange("p h t -> p (h t)"), psum[p0:p0 + 64, 4, :]).then_inc(S["u_done"], 1)
                dve.wait_ge(S["s_mm"], c + 1)
                dS = psum[:, 5, 0:256].rearrange("p (f v) -> p f v", f=FT)
                if c:
                    link(V.tensor_tensor(ST, dS, ST, ALU.add))
                else:
                    link(V.tensor_copy(ST, dS))
                V.tensor_tensor(ST, ST, spread(PC[:, :, c], 2, CH), ALU.mult).then_inc(S["s_done"], 1)
                dve.wait_ge(S["y_mm"], 2 * c + 2)
                yd = Y[p0:p0 + 64, cp, :].rearrange("p (q r v) -> p r q v", q=4, r=2)
                ys = psum[p0:p0 + 64, 6 + cp, :].rearrange("p (r q v) -> p r q v", r=2, q=4)
                if c:
                    dve.wait_ge(S["y1_done"], c)
                    y1 = Y1[p0:p0 + 64, cp, :].rearrange("p (q r v) -> p r q v", q=4, r=2)
                    link(V.tensor_tensor(yd, ys, y1, ALU.add))
                else:
                    link(V.tensor_copy(yd, ys))
            Y3 = Y.rearrange("p a (h v) -> p (a h) v", h=NH)
            T3 = YT.rearrange("p a (h v) -> p (a h) v", h=NH)
            mu, var, rs = small[:, 80:96], small[:, 64:80], small[:, 112:128]
            link(V.tensor_reduce(mu, Y3, AX.X, ALU.add))
            link(V.tensor_scalar(mu, mu, 1.0 / HD, None, ALU.mult))
            link(V.tensor_tensor(Y3, Y3, spread(mu, 2, HD), ALU.subtract))
            link(V.tensor_tensor(T3, Y3, Y3, ALU.mult))
            link(V.tensor_reduce(var, T3, AX.X, ALU.add))
            V.tensor_scalar(var, var, 1.0 / HD, 64e-5, ALU.mult, ALU.add).then_inc(S["mean_in"], 1)
            dve.wait_ge(S["root_in"], 2)
            link(V.reciprocal(rs, var))
            link(V.tensor_tensor(Y3, Y3, spread(rs, 2, HD), ALU.mult))
            dve.wait_ge(S["rows_in"], 16)
            link(V.tensor_tensor(Y, Y, spread(rows[:, 0:AW], 1, TT), ALU.mult))
            link(V.tensor_tensor(Y, Y, spread(rows[:, AW:2 * AW], 1, TT), ALU.add))
            link(V.tensor_tensor(T3, TV.rearrange("p a (h v) -> p (a h) v", h=NH), spread(small[:, 48:64], 2, HD), ALU.mult))
            V.tensor_tensor(Y, Y, YT, ALU.add).then_inc(S["gn_done"], 1)
            dve.wait_ge(S["zr_exp"], 1)
            link(V.tensor_scalar(KK, KK, 1.0, None, ALU.add))
            link(V.reciprocal(KK, KK))
            link(V.tensor_tensor(zrT, zrT, KK, ALU.mult))
            for a in range(TT):
                dve.wait_ge(S["or_mm"], a + 1)
                V.tensor_tensor(orT[:, :, a * P:a * P + P], psum[:, a, :].rearrange("p (f t) -> p f t", f=FT), zrT[:, :, a * P:a * P + P],
                                ALU.mult).then_inc(S["or_done"], 1)
            for j in range(16):
                dve.wait_ge(S["g_exp"], j + 1)
                e = EG[:, j % 8, :]
                link(V.tensor_scalar(e, e, 1.0, None, ALU.add))
                link(V.reciprocal(e, e))
                if j < 8:
                    dve.wait_ge(S["up_done"], 8)
                    V.tensor_tensor(MG[:, j, :], e, YA[:, j, :], ALU.mult).then_inc(S["g_done"], 1)
                else:
                    dve.wait_ge(S["up_done"], 16)
                    link(V.tensor_tensor(e, e, YR[:, j % 8, :], ALU.mult))
                    V.tensor_tensor(MG[:, j % 8, :], MG[:, j % 8, :], e, ALU.add).then_inc(S["g_done"], 1)
            dve.wait_ge(S["sq_sum"], 4)
            V.tensor_scalar(small[:, 98:100], small[:, 96:98], 1.0 / D, 1e-6, ALU.mult, ALU.add).then_inc(S["mean_in"], 1)
            dve.wait_ge(S["root_in"], 3)
            link(V.reciprocal(small[:, 100:102], small[:, 98:100]))
            dve.wait_ge(S["postg_in"], 16)
            for a in range(TT):
                link(V.scalar_tensor_tensor(OUT1[:, a, :], OUT1[:, a, :], small[:, 100 + a:101 + a], postg, ALU.mult, ALU.mult))
            V.tensor_tensor(xres, xres, OUT1, ALU.add).then_inc(S["x1_ready"], 1)
            dve.wait_ge(S["sq_sum"], 6)
            V.tensor_scalar(small[:, 130:132], small[:, 128:130], 1.0 / D, 1e-6, ALU.mult, ALU.add).then_inc(S["mean_in"], 1)
            dve.wait_ge(S["root_in"], 4)
            link(V.reciprocal(small[:, 132:134], small[:, 130:132]))
            for a in range(TT):
                last = V.tensor_scalar(hn2[:, a, :], xres[:, a, :], small[:, 132 + a:133 + a], None, ALU.mult)
            last.then_inc(S["hn_ready"], 1)

            dve.wait_ge(S["f_in"], 160)
            link(V.tensor_tensor(lamr[:, 0, :], lamr[:, 0, :], lamr[:, 1, :], ALU.mult))
            link(V.tensor_tensor(lamr[:, 2, :], lamr[:, 2, :], lamr[:, 3, :], ALU.mult))
            V.tensor_reduce(small[:, 138:139], lamr[:, 0, :], AX.X, ALU.add)
            V.tensor_reduce(small[:, 139:140], lamr[:, 2, :], AX.X, ALU.add).then_inc(S["lam_sum"], 1)
            dve.wait_ge(S["lam_sum"], 1)
            for i in range(2):
                bcol = col("filt_b1" if i == 0 else "filt_b2")
                dve.wait_ge(S["f_mm"], i + 1)
                x, q = harg[0:64, :], hrnd[0:64, :]
                link(V.tensor_scalar(x, psum[0:64, 7, 0:T], bcol[0:64, :], col("filt_freq")[0:64, :], ALU.add, ALU.mult))
                link(V.tensor_scalar(q, x, INV_2PI, MAGIC, ALU.mult, ALU.add))
                link(V.tensor_scalar(q, q, -MAGIC, None, ALU.add))
                link(V.scalar_tensor_tensor(x, q, -PI2_HI, x, ALU.mult, ALU.add))
                link(V.scalar_tensor_tensor(x, q, -PI2_LO, x, ALU.mult, ALU.add))
                V.tensor_scalar(x, x, 3.1415925, -3.1415925, ALU.min, ALU.max).then_inc(S["f_arg"], 1)
            for k in range(4, KC):
                dve.wait_ge(S["n2_tr"], k // 2 + 1)
                V.tensor_scalar(h2T[:, k, :], psum[:, k // 2, (k % 2) * T:(k % 2) * T + T], col("attn_g", k), None, ALU.mult).then_inc(S["n2_evac2"], 1)
            for i in range(4):
                a, o = i // 2, i % 2
                dve.wait_ge(S["f_w3mm"], i + 1)
                if i:
                    dve.wait_ge(S["f_abs"], 2 * i)
                link(V.tensor_tensor(fF, psum[:, 4, :], decay[:, a, :], ALU.mult))
                if a == 0:
                    V.scalar_tensor_tensor(fB, psum[:, 5, :], first, decay[:, a, :], ALU.mult, ALU.mult).then_inc(S["f_abs_in"], 1)
                else:
                    V.tensor_tensor(fB, psum[:, 5, :], decay[:, a, :], ALU.mult).then_inc(S["f_abs_in"], 1)
                dve.wait_ge(S["f_abs_in"], i + 1)
                V.tensor_tensor(fS[:, a, o, :], fF, fB, ALU.add)
                link(V.tensor_tensor(fD[:, a, o, :], fF, fB, ALU.subtract))
                V.memset(small[:, 249:250], 0.0).then_inc(S["f_sd"], 1)
            dve.wait_ge(S["f_norm"], 4)
            link(V.reciprocal(rnorm, psum[:, 6:8, :]))
            for i, dst in enumerate((Kr[:, 0], Kr[:, 1], Ki[:, 0], Ki[:, 1], KrP)):
                dve.wait_ge(S["f_kmm"], i + 1)
                V.tensor_tensor(dst, psum[:, 2 * (i % 2):2 * (i % 2) + 2, :], rnorm, ALU.mult).then_inc(S["f_kdone"], 1)
            link(V.memset(UPR[:, :, 0:1], 0.0))
            link(V.memset(UPR[:, :, T + 1:T + 2], 0.0))
            for g in range(3):
                dve.wait_ge(S["p2_evac"], 4 * g + 4)
                for f in range(4 * g, 4 * g + 4):
                    last = V.tensor_scalar(UC[:, f, :], UPR[:, f, 1:T + 1], col("conv_w", 12 + f), col("conv_b", f), ALU.mult, ALU.add)
                link(last)
                for f in range(4 * g, 4 * g + 4):
                    last = V.scalar_tensor_tensor(UC[:, f, :], UPR[:, f, 0:T], col("conv_w", f), UC[:, f, :], ALU.mult, ALU.add)
                link(last)
                for f in range(4 * g, 4 * g + 4):
                    last = V.scalar_tensor_tensor(UC[:, f, :], UPR[:, f, 2:T + 2], col("conv_w", 24 + f), UC[:, f, :], ALU.mult, ALU.add)
                last.then_inc(S["u_conv"], 1)
            dve.wait_ge(S["f_in"], 160)
            for n in range(2):
                z = XU[:, 2, :, :]
                dve.wait_ge(S["z_mm"], n + 1)
                zr, zi = psum[:, 0:2, :], psum[:, 2:4, :]
                V.tensor_tensor(M1, zr, Kr[:, :, n, :], ALU.mult)
                link(V.tensor_tensor(M2, zi, Ki[:, :, n, :], ALU.mult))
                link(V.tensor_tensor(SPY[:, 0, :, :], M1, M2, ALU.subtract))
                V.tensor_tensor(M1, zr, Ki[:, :, n, :], ALU.mult)
                V.tensor_tensor(M2[:, 0, :], psum[:, 2, :], KrP[:, n, :], ALU.mult)
                link(V.tensor_tensor(M2[:, 1, :], psum[:, 3, :], Kr[:, 1, n, :], ALU.mult))
                V.tensor_tensor(SPY[:, 1, :, :], M1, M2, ALU.add).then_inc(S["spec"], 1)
                dve.wait_ge(S["spec"], n + 1)
                link(V.tensor_tensor(M1, z, spread(skip[:, n, :], 1, TT), ALU.mult))
                dve.wait_ge(S["i_mm"], n + 1)
                link(V.tensor_tensor(M1, psum[:, 4:6, :], M1, ALU.add))
                V.tensor_tensor(z, M1, XU[:, n, :, :], ALU.mult).then_inc(S["z_done"], 1)
            dve.wait_ge(S["z_done"], 2)
            z = XU[:, 2, :, :]
            g3 = lambda x: x.rearrange("p a (h v) -> p (a h) v", v=64)
            link(V.tensor_tensor(M1, z, z, ALU.mult))
            link(V.tensor_reduce(small[:, 160:176], g3(M1), AX.X, ALU.add))
            V.tensor_scalar(small[:, 144:160], small[:, 160:176], 1.0 / 64, 1e-6, ALU.mult, ALU.add).then_inc(S["mean_in"], 1)
            dve.wait_ge(S["root_in"], 5)
            link(V.reciprocal(small[:, 160:176], small[:, 144:160]))
            V.tensor_tensor(g3(ZN), g3(z), spread(small[:, 160:176], 2, 64), ALU.mult).then_inc(S["hy_norm"], 1)
            for f in range(4):
                dve.wait_ge(S["m_tr"], f // 2 + 1)
                V.tensor_scalar(mixT[:, f, :], psum[:, 4 + f // 2, (f % 2) * T:(f % 2) * T + T], col("hy_g", f), None, ALU.mult).then_inc(S["m_evac"], 1)
            dve.wait_ge(S["lam_exp"], 1)
            link(V.tensor_tensor(small[:, 142:143], small[:, 140:141], small[:, 141:142], ALU.subtract))
            link(V.tensor_scalar(small[:, 142:143], small[:, 142:143], 0.2, None, ALU.add))
            link(V.tensor_scalar(small[:, 143:144], col("subln"), 0.8, None, ALU.mult))
            for n in range(8):
                h, tile, i = n // 2, n % 2, n % 2
                dve.wait_ge(S["l2_mm"], n + 1)
                if n >= 2:
                    dve.wait_ge(S["l2_tr"], n - 1)
                L = LG2[:, i, :, :]
                link(V.scalar_tensor_tensor(L, spread(dist[:, tile * T:tile * T + T], 1, 2), -(2.0 ** (-2.0 * (h + 1))), psum[:, 2 * i:2 * i + 2, 0:T], ALU.mult, ALU.add))
                V.tensor_reduce(small[:, 176 + 2 * i:178 + 2 * i], L, AX.X, ALU.max, negate=True).then_inc(S["l2_neg"], 1)
                dve.wait_ge(S["l2_exp"], 2 * n + 2)
                link(V.reciprocal(small[:, 184:186], small[:, 180 + 2 * i:182 + 2 * i]))
                link(V.tensor_tensor(small[:, 185:186], small[:, 185:186], small[:, 142:143], ALU.mult))
                link(V.tensor_scalar(L[:, 1, :], L[:, 1, :], small[:, 185:186], None, ALU.mult))
                V.scalar_tensor_tensor(L[:, 0, :], L[:, 0, :], small[:, 184:185], L[:, 1, :], ALU.mult, ALU.subtract).then_inc(S["l2_prob"], 1)
                dve.wait_ge(S["l2_tr"], n + 1)
                V.tensor_copy(PT2[:, i, :, :], psum[:, 4 + i, 0:T].rearrange("p (s t) -> p s t", s=TT)).then_inc(S["l2_turned"], 1)
            dve.wait_ge(S["o2_sq"], 1)
            o3 = lambda x: x.rearrange("p a h v -> p (a h) v")
            link(V.tensor_reduce(small[:, 192:200], o3(OSQ), AX.X, ALU.add))
            V.tensor_scalar(small[:, 192:200], small[:, 192:200], 1.0 / P, 1e-6, ALU.mult, ALU.add).then_inc(S["mean_in"], 1)
            dve.wait_ge(S["root_in"], 6)
            link(V.reciprocal(small[:, 208:216], small[:, 192:200]))
            V.tensor_tensor(o3(OA), o3(OA), spread(small[:, 208:216], 2, P), ALU.mult).then_inc(S["o2_norm"], 1)
            for f in range(4):
                dve.wait_ge(S["m2_tr"], f // 2 + 1)
                V.tensor_scalar(mixT[:, 4 + f, :], psum[:, f // 2, (f % 2) * T:(f % 2) * T + T], small[:, 143:144], None, ALU.mult).then_inc(S["m2_evac"], 1)
            for n in range(2):
                for a in range(TT):
                    dve.wait_ge(S["x2_mm"], 2 * n + a + 1)
                    x = xres[:, a, 512 * n:512 * n + 512]
                    V.tensor_tensor(x, psum[:, 2 + 2 * n + a, :], x, ALU.add).then_inc(S["x2_ready"], 1)
            dve.wait_ge(S["sq_sum"], 8)
            V.tensor_scalar(stat[:, 2:4], stat[:, 0:2], 1.0 / D, 1e-6, ALU.mult, ALU.add).then_inc(S["mean_in"], 1)
            dve.wait_ge(S["root_in"], 7)
            link(V.reciprocal(stat[:, 4:6], stat[:, 2:4]))
            for a in range(TT):
                last = V.tensor_scalar(hf[:, a, :], xres[:, a, :], stat[:, 4 + a:5 + a], None, ALU.mult)
            last.then_inc(S["hn_ready"], 1)
            dve.wait_ge(S["r_mm"], 1)
            V.tensor_reduce(stat[:, 6:8], psum[:, 4, 0:TT * E].rearrange("p (a e) -> p a e", a=TT), AX.X, ALU.max, negate=True).then_inc(S["r_neg"], 1)
            dve.wait_ge(S["r_exp"], 2)
            link(V.reciprocal(stat[:, 10:12], stat[:, 8:10]))
            V.tensor_tensor(aff, aff, spread(stat[:, 10:12], 2, E), ALU.mult).then_inc(S["aff_ready"], 1)
            dve.wait_ge(S["aff_tr"], 1)
            link(V.tensor_copy(affT[0:E, :], psum[0:E, 5, 0:T]))
            src = affT[0:E, :]
            for i in range(CAP // 8):
                link(V.max(top8[0:E, :], src))
                dst = work[i % 2][0:E, :]
                link(V.match_replace(dst, top8[0:E, :], src, -1.0))
                src = dst
            dve.wait_ge(S["ones_set"], 2)
            sel, run = work[0][0:E, :], affT[0:E, :]
            link(V.tensor_scalar(sel, src, 0.0, None, ALU.is_lt))
            link(V.tensor_tensor_scan(run, onesT[0:E, :], sel, 0.0, ALU.mult, ALU.add))
            V.tensor_tensor(sel, sel, run, ALU.mult).then_inc(S["rank_ready"], 1)
            dve.wait_ge(S["rank_tr"], 1)
            link(V.tensor_copy(rank.rearrange("p a e -> p (a e)"), psum[:, 6, 0:TT * E]))
            dve.wait_ge(S["r_in"], 32)
            oe = lambda x: x.rearrange("p a e c -> p (a e) c")
            V.tensor_tensor(oe(ohot), spread(rank.rearrange("p a e -> p (a e)"), 2, CAP), spread(slotsr, 1, TT * E), ALU.is_equal).then_inc(S["ohot_ready"], 1)
            dve.wait_ge(S["ohot_ready"], 1)
            over4 = lambda x: bass.AP(x.tensor, x.offset, [list(x.ap[0]), [0, 4], [0, CAP]])
            for q in range(8):
                if q >= 2:
                    dve.wait_ge(S["o_tr"], q - 1)
                for a in range(TT):
                    for e in range(2):
                        last = V.tensor_tensor(og4[:, 2 * (q % 2) + a, e, :].rearrange("p (r c) -> p r c", r=4), spread(ohot[:, a, 2 * q + e, :], 1, 4),
                                               over4(aff[:, a, 2 * q + e:2 * q + e + 1]), ALU.mult)
                last.then_inc(S["og_ready"], 1)
                dve.wait_ge(S["o_tr"], q + 1)
                V.tensor_copy(OT[:, 512 * q:512 * q + 512], psum[:, 4 + q % 4, :]).then_inc(S["o_evac"], 1)
            V.memset(small[:, 247:248], 0.0).then_inc(S["h_ready"], 1)
            V.memset(small[:, 246:247], 0.0).then_inc(S["acc_done"], 1)
            with dve.Fori(0, E) as e:
                step = 6
                dve.wait_ge(S["g_expd"], e + 1)
                V.tensor_scalar(GE, GE, 1.0, None, ALU.add).then_inc(S["dve_loop"], 1)
                dve.wait_ge(S["dve_loop"], e * step + 1)
                V.reciprocal(GE, GE).then_inc(S["dve_loop"], 1)
                dve.wait_ge(S["dve_loop"], e * step + 2)
                ge = GE.rearrange("p (n x) -> p n x", n=2)
                V.tensor_tensor(ge, psum[:, 0:2, 0:HALFQ], ge, ALU.mult).then_inc(S["dve_loop"], 1)
                dve.wait_ge(S["dve_loop"], e * step + 3)
                dve.wait_ge(S["piece_used"], e * 24 + 16)
                V.tensor_tensor(ge, psum[:, 2:4, 0:HALFQ], ge, ALU.mult).then_inc(S["dve_loop"], 1)
                dve.wait_ge(S["dve_loop"], e * step + 4)
                V.tensor_copy(HP, GE.rearrange("p (q i) -> p i q", i=FPP)).then_inc(S["dve_loop"], 1)
                dve.wait_ge(S["dve_loop"], e * step + 5)
                V.transpose(HT.rearrange("p i c -> p (i c)"), HP.rearrange("p i c -> p (i c)")).then_inc(S["h_ready"], 1)
                for a in range(TT):
                    dve.wait_ge(S["sc_mm"], e * 2 + (a + 1))
                    x = xres[:, a, :].rearrange("p (n x) -> p n x", n=2)
                    b = 6 if a == 0 else 4
                    V.tensor_tensor(x, psum[:, b:b + 2, :], x, ALU.add).then_inc(S["acc_done"], 1)
                V.memset(small[:, 248:249], 0.0).then_inc(S["dve_loop"], 1)
                dve.wait_ge(S["h_ready"], e + 2)
                dve.wait_ge(S["acc_done"], e * 2 + 3)
            dve.wait_ge(S["sq_sum"], 10)
            V.tensor_scalar(small[:, 226:228], small[:, 224:226], 1.0 / D, 1e-6, ALU.mult, ALU.add).then_inc(S["mean_in"], 1)
            dve.wait_ge(S["root_in"], 8)
            link(V.reciprocal(small[:, 228:230], small[:, 226:228]))
            dve.wait_ge(S["fg_in"], 16)
            for a in range(TT):
                V.scalar_tensor_tensor(xres[:, a, :], xres[:, a, :], small[:, 228 + a:229 + a], finalg, ALU.mult, ALU.mult).then_inc(S["out_ready"], 1)


def kernel(**inputs):
    import numpy as _np
    import concourse.bacc as _bacc
    from concourse import mybir as _mybir
    from concourse.bass_utils import run_bass_kernel_spmd as _run

    i = {k: _np.asarray(v) for k, v in inputs.items()}
    pc = lambda a: a.reshape(-1, 128).T
    half = lambda a: _np.concatenate([a.reshape(-1, 1), _np.zeros((64, 1), _np.float32)])
    cols = _np.concatenate([pc(i["pre_norm_gain"]), pc(i["rwkv_shift_mix"]), pc(i["rwkv_w0"]), pc(i["rwkv_a0"]), pc(i["rwkv_k_k"]),
                            pc(i["rwkv_k_a"]), pc(i["rwkv_r_k"]), pc(i["attn_norm_g_2"]), pc(i["conv_w_2"]), pc(i["conv_b_2"]),
                            pc(i["subln_g_2"]), pc(i["ffn_norm_g_2"]), pc(i["hyena_norm_g_2"]), half(i["filt_b1_2"]),
                            half(i["filt_b2_2"]), half(i["filt_freq_2"])], axis=1)
    rows = _np.concatenate([i[n].reshape(-1) for n in ("post_norm_gain", "rwkv_ln_w", "rwkv_ln_b", "hyena_skip_2", "final_norm_g_2",
                                                       "lambda_q1_2", "lambda_k1_2", "lambda_q2_2", "lambda_k2_2")])
    arrays = {"x": i["x"][0], "cols": cols, "rows": rows, "low_up": _np.concatenate([i["rwkv_w_up"][0], i["rwkv_a_up"][0]]),
              "rel_bias": i["rel_bias"], "w_in": i["w_in"][0], "w_up_attn": i["w_up_attn"][0], "w_up_rwkv": i["w_up_rwkv"][0],
              "w_out": i["w_out"][0], "w_in_2": i["w_in_2"][0], "w_out_2": i["w_out_2"][0], "filt_w1": i["filt_w1_2"][0],
              "filt_w2": i["filt_w2_2"][0], "filt_w3": i["filt_w3_2"][0], "w_router": i["w_router_2"][0],
              "w_gate": i["w_gate_2"][0], "w_up": i["w_up_2"][0], "w_down": i["w_down_2"][0]}
    arrays.update(constants())
    nc = _bacc.Bacc("TRN2", target_bir_lowering=False, num_devices=1)
    A, feed = {}, {}
    for name, a in arrays.items():
        a = _np.ascontiguousarray(a)
        feed["in_" + name] = a
        A[name] = nc.dram_tensor("in_" + name, a.shape, _mybir.dt.from_np(a.dtype), kind="ExternalInput").ap()
    out = nc.dram_tensor("out_0", (T, D), F32, kind="ExternalOutput").ap()
    program(nc, A, out)
    r = _run(nc, [feed], core_ids=[0])
    return r.results[0]["out_0"].reshape(1, T, D)
```

```python
from contextlib import ExitStack

import concourse.bass as bass
from concourse import mybir

F32 = mybir.dt.float32
ALU = mybir.AluOpType
ACT = mybir.ActivationFunctionType
AX = mybir.AxisListType

P = 128
T = 256
TT = T // P
D = 1024
KC = D // P
HD = 64
NG, NH = 3, 8
CH = 64
NCH = T // CH
AW = NH * HD
FT = AW // P
OFF_GATE = 3 * NG * AW
OFF_RWKV = OFF_GATE + AW
OFF_LOW = OFF_RWKV + 3 * AW
OFF_RGATE = OFF_LOW + P
OFF_MERGE = OFF_RGATE + AW
NEG = -1.0e30
E_HALF = 0.6065306597126334

COLS = {}
def _cols():
    at = 0
    for name, n in [("pre_g", 8), ("mix", 13), ("w0", 4), ("a0", 4), ("k_k", 4), ("k_a", 4), ("r_k", 4),
                    ("attn_g", 8), ("conv_w", 36), ("conv_b", 12), ("subln", 1), ("ffn_g", 8),
                    ("hy_g", 4), ("filt_b1", 1), ("filt_b2", 1), ("filt_freq", 1)]:
        COLS[name] = (at, at + n)
        at += n
    return at
NCOLS = _cols()
ROWS = {}
def _rows():
    at = 0
    for name, n in [("post_g", 1024), ("ln_w", 512), ("ln_b", 512), ("skip", 1024), ("final_g", 1024), ("lam", 256)]:
        ROWS[name] = (at, at + n)
        at += n
    return at
NROWS = _rows()


def spread(x, axis, n):
    dims = [list(d) for d in x.ap]
    dims.insert(axis, [0, n])
    return bass.AP(x.tensor, x.offset, dims)


MAGIC = 12582912.0
INV_2PI = 0.15915494309189535
PI2_HI = 6.28125
PI2_LO = 0.0019353071795864769


def constants():
    import numpy as np
    import math
    c = {}
    i = np.arange(128)
    eye = np.eye(128, dtype=np.float32)
    half = np.arange(64)
    par = i % 64
    us = (par[:, None] < half[None, :]).astype(np.float32)
    ui = (par[:, None] <= half[None, :]).astype(np.float32)
    ls = (half[None, :] < par[:, None]).astype(np.float32)
    same2 = (par[:, None] // 2 == half[None, :] // 2).astype(np.float32)
    i64 = (par[:, None] == half[None, :]).astype(np.float32)
    offs = []
    for b in (2, 4, 8, 16, 32):
        offs.append(((par[:, None] // (2 * b) == half[None, :] // (2 * b)) & (par[:, None] % (2 * b) >= b)
                     & (half[None, :] % (2 * b) < b)).astype(np.float32))
    blockones = (i[:, None] // 64 == i[None, :] // 64).astype(np.float32)
    two = (i[:, None] // 64 == np.arange(2)[None, :]).astype(np.float32)
    chunkstart = np.tile((np.arange(256) % 64 != 0).astype(np.float32)[None], (128, 1))
    c["c_square"] = np.concatenate([eye, eye[:, ::-1], us, ui, ls, us * same2, ls * same2, i64] + offs
                                   + [blockones, two, chunkstart], axis=1).astype(np.float32)
    j = np.arange(384) - 127
    d = np.maximum(j, 0)
    ratio = np.log(np.maximum(d, 1).astype(np.float32) / 16) / np.float32(math.log(2048 / 16))
    large = np.minimum(16 + (ratio * 16).astype(np.int32), 31)
    bucket = np.where(d < 16, d, large).astype(np.int32)
    c["c_bucket"] = (np.arange(32)[:, None] == bucket[None]).astype(np.float32)
    rows = []
    for window, dil in ((128, 1), (512, 4), (2048, 16)):
        ok = (j >= 0) & (j % dil == 0) & (j // dil <= window // dil) & (j <= 255)
        rows += [np.where(ok, 0.0, -1.0e30)] * 8
    c["c_mask"] = np.stack(rows).astype(np.float32)
    t = np.arange(256)
    f = np.arange(256)
    ang = 2 * np.pi * ((t[:, None] * f[None]) % 512) / 512
    alt = np.where(t % 2 == 0, 1.0, -1.0)
    cos, sin = np.cos(ang), np.sin(ang)
    cosp = cos[:, 0:128].copy()
    cosp[:, 0] = alt
    sinp = -sin[:, 0:128]
    sinp[:, 0] = alt
    fwd = np.concatenate([cos, -sin, cosp, sinp], axis=1)
    c["c_fwd"] = fwd.reshape(2, 128, 768).transpose(1, 0, 2).reshape(128, 1536)
    wt = np.where(f == 0, 1.0, 2.0) / 512
    re = wt[:, None] * cos.T
    im = -wt[:, None] * sin.T
    im[0] = alt / 512
    inv = np.concatenate([re, im], axis=0).reshape(4, 128, 256)
    c["c_inv"] = inv.transpose(1, 0, 2).reshape(128, 1024)
    ts = np.linspace(0.0, 1.0, 256, dtype=np.float32)
    lo, hi = math.log(1e-2) / 1.5, math.log(1e-2) / 0.3
    deltas = np.abs(np.linspace(lo, hi, 512, dtype=np.float32))
    dec = np.exp(-ts[:, None] * deltas)
    c["c_decay"] = dec.reshape(2, 128, 512).transpose(1, 0, 2).reshape(128, 1024)
    w = np.float32(2 * math.pi) * np.arange(256, dtype=np.float32)[:, None] / np.float32(256)
    bands = np.linspace(1e-4, 15, 16, dtype=np.float32)[None]
    z = np.concatenate([ts[:, None], np.cos(bands * w), -np.sin(bands * w)], axis=-1)
    c["c_emb"] = z.T
    dist = np.abs(t[:, None] - t[None]).astype(np.float32)
    first = (np.arange(128) > 0).astype(np.float32)[:, None]
    c["c_dist"] = np.concatenate([dist.reshape(2, 128, 256).transpose(1, 0, 2).reshape(128, 512), first], axis=1)
    c["c_slots"] = np.tile(np.arange(1, 33)[None], (128, 1))
    return {k: np.ascontiguousarray(v, dtype=np.float32) for k, v in c.items()}


def program(nc, A, out):
    ctx = ExitStack()
    with ctx:
        def sem(name):
            return ctx.enter_context(nc.semaphore(name))

        ARENA = 52992
        arena = ctx.enter_context(nc.sbuf_tensor("arena", [P, ARENA], F32))
        psum = ctx.enter_context(nc.psum_tensor("psum", [P, 8, 512], F32))
        bias_rows = nc.dram_tensor("bias_rows", (NG * NH, 384), F32, kind="Internal").ap()

        def region(off, *shape):
            n = 1
            for s in shape:
                n *= s
            x = arena[:, off:off + n]
            if len(shape) == 2:
                x = x.rearrange("p (a b) -> p a b", a=shape[0])
            elif len(shape) == 3:
                x = x.rearrange("p (a b c) -> p a b c", a=shape[0], b=shape[1])
            elif len(shape) == 4:
                x = x.rearrange("p (a b c d) -> p a b c d", a=shape[0], b=shape[1], c=shape[2])
            return x

        RING = 12 * 2816
        NB = 3
        wb = [region(4096 * i, 8, 512) for i in range(NB)]
        wb_up = [region(4096 * i, 4, 1024) for i in range(NB)]
        EG = region(4096 * NB, 16, T)
        S0 = 16896
        qT = region(S0, 12, T)
        kT = region(S0 + 3072, 12, T)
        vR = region(S0 + 6144, TT, 1536)
        bias = region(S0 + 9216, NH, NG, T)
        F0 = RING
        xres = region(F0, TT, D)
        hT = region(F0 + 2048, KC, T)
        hR = region(F0 + 4096, KC, T)
        hn = region(F0 + 12000, TT, D)
        prT = region(F0 + 6144, 13, T)
        oaT = region(F0 + 9472, FT, T)
        zaT = region(F0 + 10496, FT, T)
        zrT = region(F0 + 11520, FT, T)
        LG = region(F0 + 12544, 2, NG * T)
        PT = region(F0 + 14080, 2, 3, P)
        C0 = F0 + 15616
        cols = region(C0, NCOLS)
        csq = region(C0 + 128, 1346)
        small = region(C0 + 128 + 1346, 256)
        bucketT = region(S0, 384)
        maskT = region(S0 + 384, 384)
        relb = region(S0 + 768, 32)
        brow = region(S0 + 800, 384)
        lowW = region(C0 + 1730, 512)
        rows = region(C0 + 1730 + 512, 1024)
        assert C0 + 1730 + 512 + 1024 <= ARENA and NCOLS <= 128

        ident, anti = csq[:, 0:128], csq[:, 128:256]
        US, UI, LS = csq[:, 256:320], csq[:, 320:384], csq[:, 384:448]
        US2, LS2, I64 = csq[:, 448:512], csq[:, 512:576], csq[:, 576:640]
        OFFB = [csq[:, 640 + 64 * i:704 + 64 * i] for i in range(5)]
        BLK1, TWO, CSTART = csq[:, 960:1088], csq[:, 1088:1090], csq[:, 1090:1346]

        def col(name, i=0, n=1):
            a = COLS[name][0] + i
            return cols[:, a:a + n]

        AR = region(S0, FT, NCH, 2, CH)
        BT = region(S0 + 2048, FT, T)
        KT = region(S0 + 3072, FT, T)
        TB, TK, TV = (region(S0 + 4096 + 1024 * i, TT, AW) for i in range(3))
        MATS = [region(S0 + 7168 + 1024 * i, 2, NH, CH) for i in range(9)]
        mN, mA, mMT, mM, mT1, mAk, mRb, mRk, mOff = MATS
        ST = region(S0 + 16384, FT, CH)
        LD = region(F0 + 2048 + 2048, FT, T)
        CS = region(F0 + 2048 + 3072, FT, T)
        KK = region(F0 + 12544, FT, T)
        AA = region(F0 + 13568, FT, T)
        TMP = region(F0 + 14592, FT, T)
        EX1 = region(S0 + 7168, FT, T)
        EX2 = region(S0 + 8192, FT, T)
        XV = region(S0 + 2048, 2, NH, CH)
        XS = region(S0 + 3072, NH, CH)
        USB = region(S0 + 3584, NH, CH)
        Y = region(F0 + 4096, TT, AW)
        Y1 = region(F0 + 5120, TT, AW)
        YT = region(F0 + 13568, TT, AW)
        orT = region(F0 + 12544, FT, T)
        ZE = region(F0 + 4096, FT, T)
        SHIFT = region(F0 + 4096, FT, T)
        MG = region(S0, KC, T)
        YR = region(S0 + 2048, KC, T)
        SQ = region(S0 + 10752, TT, D)
        OUT1 = region(S0 + 12800, TT, D)
        postg = region(S0 + 9728, D)

        h2T = region(F0 + 2048, KC, T)
        Kr = region(S0, 2, 2, 512)
        Ki = region(S0 + 2048, 2, 2, 512)
        KrP = region(S0 + 4096, 2, 512)
        fwd = region(S0 + 5120, TT, 768)
        inv = region(S0 + 6656, 4, T)
        decay = region(S0 + 7680, TT, 512)
        skip = region(S0 + 8704, 2, 512)
        XU = region(S0 + 9728, 3, TT, 512)
        SPY = region(S0 + 12800, 2, 2, 512)
        M1 = region(S0 + 14848, 2, 512)
        M2 = region(S0 + 15872, 2, 512)
        UPR = region(F0 + 4096, 12, T + 2)
        UC = region(F0 + 7200, 12, T)
        q2T = region(F0 + 10272, 4, T)
        k2T = region(F0 + 11296, 4, T)
        v2 = region(F0 + 12320, TT, 512)
        LG2 = region(F0 + 13344, 2, 2, T)
        PT2 = region(F0 + 14368, 2, TT, P)
        dist = region(F0 + 14880, 513)
        first = region(F0 + 14880 + 512, 1)
        fS = region(F0 + 4096, TT, 2, 512)
        fD = region(F0 + 6144, TT, 2, 512)
        w3 = region(S0 + 14848, 2048)
        emb = region(F0 + 8192, T)
        fw1 = region(F0 + 8448, 64)
        fw2 = region(F0 + 8512, 64)
        hid = region(F0 + 8576, T)
        harg = region(F0 + 8832, T)
        hrnd = region(F0 + 9088, T)
        fF, fB, fFa, fBa = (region(F0 + 9472 + 512 * i, 512) for i in range(4))
        rnorm = region(F0 + 13568, 2, 512)
        lamr = region(F0 + 14624, 4, 64)
        ones = region(C0 + 1730, 128)
        hn2 = region(S0 + 12800, TT, D)
        OA = region(F0 + 7200, TT, 4, P)
        OSQ = region(F0 + 8224, TT, 4, P)
        mixT = region(F0 + 4096, KC, T)
        ZN = region(S0 + 14848, TT, 512)
        E, CAP, FF = 16, 32, 2816
        SLOTS = 12
        PIECE = 2816
        FPP = FF // P
        QUARTER = FF // 4
        HALFQ = QUARTER // 2

        def slot(n):
            return region(PIECE * n, PIECE)
        XE = region(F0 + 2048, E * KC * CAP)
        OT = region(F0 + 6144, E * TT * P)
        XC = region(F0 + 10240, KC, CAP)
        OC = region(F0 + 10496, TT, P)
        GE = region(F0 + 10752, QUARTER)
        HP = region(F0 + 11456, FPP, CAP)
        HT = region(F0 + 12160, FPP, CAP)
        YS = region(F0 + 12864, 2, 512)
        finalg = region(F0 + 13888, D)
        hf = region(F0 + 2048 + 8192, TT, D)
        hfT = region(F0 + 6144, KC, T)
        ohot = region(F0 + 12288, TT, E, CAP)
        og4 = region(F0 + 13312, 4, 2, 4 * CAP)
        wr = region(C0 + 1858, KC, 16)
        affT = region(F0 + 8320, T)
        work = [region(F0 + 8576 + 256 * i, T) for i in range(2)]
        slotsr = region(C0 + 1986, CAP)
        onesT = region(C0 + 2018, T)
        top8 = region(F0 + 14944, 8)
        aff = region(F0 + 14952, TT, E)
        rank = region(F0 + 14984, TT, E)
        stat = region(F0 + 15016, 16)
        S = {}
        for name in ["params", "xin", "brow_out", "bias_in", "rows_in", "postg_in",
                     "proj_ready", "proj_evac", "hn_ready", "sq_sum", "mean_in", "root_in", "hT_ready", "hT_evac", "hR_evac", "low_in", "bias_mm", "bias_row", "logit_ready", "prob_ready", "pt_ready", "pt_done",
                     "o_ready", "o_done", "neg_max", "expd",
                     "low_t", "low_mm", "lowexp", "sq_ready", "norm_mm", "norm_sqrt", "cs_ready", "exps",
                     "ab_ready", "tok_tr", "tok_done", "gram_mm", "gram_done", "T1_mm", "T1_done", "MM_mm", "MM_done", "xv_mm", "xv_done",
                     "x_mm", "x_done", "u_mm", "u_done", "s_mm", "s_done", "y_mm", "y1_done", "bonus_mm", "gn_done", "or_mm", "or_done", "za_exp", "zr_exp", "oa_gated", "up_mm", "up_done", "g_done",
                     "out1_mm", "out1_sb", "x1_ready", "store",
                     "dve_line"]:
            S[name] = sem(name)
        for name in ["f_in", "f_mm", "lam_sum", "ones_set", "n2_evac2", "f_hid", "f_arg", "f_w3mm", "f_abs_in", "f_abs", "f_norm", "f_sd", "f_kmm", "f_kdone",
                     "n2_tr", "n2_evac", "p2_ready", "p2_evac", "u_conv", "u_tr", "u_evac",
                     "z_mm", "spec", "i_mm", "z_done", "hy_norm", "m_tr", "m_evac",
                     "l2_mm", "l2_neg", "l2_exp", "l2_prob", "l2_tr", "l2_turned", "o2_mm", "o2_sb", "o2_sq", "o2_norm",
                     "lam_exp", "m2_tr", "m2_evac", "x2_mm", "x2_ready"]:
            S[name] = sem(name)
        for name in ["r_in", "n3_tr", "n3_evac", "n3_evac2", "r_mm", "r_neg", "r_exp", "aff_ready", "aff_tr", "rank_ready",
                     "rank_tr", "ohot_ready", "og_ready", "x_gather", "x_evac", "o_tr", "o_evac", "xc_ready", "oc_ready", "piece_used", 
                     "g_expd", "h_ready", "y3_sb", "sc_mm", "acc_done", "out_ready", "fg_in",
                     "dve_loop"]:
            S[name] = sem(name)
        arrived = [sem(f"piece{i}_in") for i in range(SLOTS)]
        wload = [sem(f"wload{i}") for i in range(NB)]

        class Line:
            def __init__(self, eng, s):
                self.eng, self.s, self.n = eng, s, 0

            def __call__(self, ins):
                self.n += 1
                ins.then_inc(self.s, 1)
                self.eng.wait_ge(self.s, self.n)

        def in_cols(w, c0, n=512):
            return w[:, c0:c0 + n].rearrange("(k p) n -> p k n", p=P)
        w_in = A["w_in"]
        blocks = [(f"q{i}", in_cols(w_in, 512 * i)) for i in range(3)]
        blocks += [(f"k{i}", in_cols(w_in, 1536 + 512 * i)) for i in range(3)]
        blocks += [(f"v{i}", in_cols(w_in, 3072 + 512 * i)) for i in range(3)]
        blocks += [("low", in_cols(w_in, OFF_LOW, P))]
        blocks += [(f"rkv{i}", in_cols(w_in, OFF_RWKV + 512 * i)) for i in range(3)]
        blocks += [("rgate", in_cols(w_in, OFF_RGATE)), ("agate", in_cols(w_in, OFF_GATE))]
        blocks += [(f"g{i}", in_cols(w_in, OFF_MERGE + 512 * i)) for i in range(4)]
        blocks += [("upa", A["w_up_attn"].rearrange("(k p) n -> p k n", p=P)),
                   ("upr", A["w_up_rwkv"].rearrange("(k p) n -> p k n", p=P))]
        blocks += [(f"out{i}", in_cols(A["w_out"], 512 * i)) for i in range(2)]
        blocks += [(f"hy{i}", in_cols(A["w_in_2"], 512 * i)) for i in range(3)]
        blocks += [(f"at{i}", in_cols(A["w_in_2"], 1536 + 512 * i)) for i in range(3)]
        blocks += [(f"out2_{i}", in_cols(A["w_out_2"], 512 * i)) for i in range(2)]
        number = {name: n for n, (name, _) in enumerate(blocks)}

        def block_of(name):
            return wb[number[name] % NB]

        def weights_in(pe, name):
            n = number[name]
            pe.wait_ge(wload[n % NB], 16 * (n // NB + 1))

        wg, wu = A["w_gate"], A["w_up"]
        wd = A["w_down"].rearrange("e (p i) n -> (e p) (i n)", p=P)

        def piece(e, i):
            if i < 16:
                w = (wg if i < 8 else wu).rearrange("e k n -> (e k) n")
                return w[bass.ds(e * D + (i % 8) * P, P), :]
            return wd[bass.ds(e * P, P), (i - 16) * PIECE:(i - 15) * PIECE]

        tiles = [(f"q{i}", c, hT, qT[:, 4 * i + c, :], 0.125) for i in range(3) for c in range(4)]
        tiles += [(f"k{i}", c, hR, kT[:, 4 * i + c, :], 1.0) for i in range(3) for c in range(4)]
        tiles += [(f"v{i}", u, None, vR[:, u, 512 * i:512 * i + 512], 1.0) for i in range(3) for u in range(TT)]
        ATT_TILES = len(tiles)
        tiles += [("low", 0, hT, prT[:, 12, :], 1.0)]
        tiles += [(f"rkv{i}", c, hT, prT[:, 4 * i + c, :], 1.0) for i in range(3) for c in range(4)]
        tiles += [("rgate", c, hT, zrT[:, c, :], 1.0) for c in range(4)]
        tiles += [("agate", c, hT, zaT[:, c, :], 1.0) for c in range(4)]
        GATE_TILE = len(tiles)
        tiles += [(f"g{c // 4}", c % 4, hT, EG[:, c, :], 1.0) for c in range(16)]
        NT = len(tiles)
        RKV_TILE = ATT_TILES + 1
        PREP_TILE = ATT_TILES + 2 + 16
        GRAM_TILE = PREP_TILE + 10
        LEVEL_TILE = GRAM_TILE + 2
        NORM_TILE = LEVEL_TILE + 5
        assert NORM_TILE + 2 == NT

        def bank_of(j):
            if j < ATT_TILES:
                return j % 4
            return 6 if PREP_TILE <= j < NORM_TILE and (j - PREP_TILE) % 2 else 7

        def bank2_of(j):
            return j % 4 if j < 14 else 6 + j % 2

        released = {name: (S["proj_ready"], 1 + max(j for j, t in enumerate(tiles) if t[0] == name)) for name in {t[0] for t in tiles}}
        released.update({"upa": (S["up_mm"], 8), "upr": (S["up_mm"], 16), "out0": (S["out1_mm"], 2), "out1": (S["out1_mm"], 4)})
        released.update({f"hy{i}": (S["p2_ready"], 4 * i + 4) for i in range(3)})
        released.update({"at0": (S["p2_ready"], 16), "at1": (S["p2_ready"], 20), "at2": (S["p2_ready"], 22)})
        released.update({"out2_0": (S["x2_mm"], 3), "out2_1": (S["x2_mm"], 4)})
        units = [(h, tile) for h in range(NH) for tile in (1, 0)]
        NU = len(units)

        def hh(h):
            return (h % 2) * 4 + h // 2

        block = ctx.enter_context(nc.Block())

        @block.sync
        def _(sp):
            sp.dma_start(xres, A["x"].rearrange("(a p) d -> p a d", p=P)).then_inc(S["xin"], 16)
            sp.wait_ge(S["params"], 96)
            for n, (name, src) in enumerate(blocks):
                if n >= NB:
                    count, value = released[blocks[n - NB][0]]
                    sp.wait_ge(count, value)
                if name[0:2] == "up":
                    dst = wb_up[n % NB]
                else:
                    dst = wb[n % NB][:, :, 0:src.shape[2]]
                sp.dma_start(dst, src).then_inc(wload[n % NB], 16)
            used = S["x2_mm"]
            for i, count, value in ((5, S["z_done"], 1), (6, S["spec"], 2), (7, S["spec"], 2), (8, S["i_mm"], 2),
                                    (9, S["z_done"], 2), (10, S["hy_norm"], 1), (11, S["m_tr"], 2),
                                    (3, used, 3), (4, used, 3), (0, used, 4), (1, used, 4), (2, used, 4)):
                sp.wait_ge(count, value)
                sp.dma_start(slot(i), piece(0, i)).then_inc(arrived[i], 16)
            with sp.Fori(0, E - 1) as e:
                for i in range(SLOTS, 24):
                    sp.wait_ge(S["piece_used"], e * 24 + (i - 11))
                    sp.dma_start(slot(i - SLOTS), piece(e, i)).then_inc(arrived[i - SLOTS], 16)
                for i in range(SLOTS):
                    sp.wait_ge(S["piece_used"], e * 24 + (i + 13))
                    sp.dma_start(slot(i), piece(e + 1, i)).then_inc(arrived[i], 16)
            for i in range(SLOTS, 24):
                sp.wait_ge(S["piece_used"], (E - 1) * 24 + (i - 11))
                sp.dma_start(slot(i - SLOTS), piece(E - 1, i)).then_inc(arrived[i - SLOTS], 16)
            sp.wait_ge(S["out_ready"], 2)
            sp.dma_start(out.rearrange("(a p) d -> p a d", p=P), xres).then_inc(S["store"], 16)
            sp.wait_ge(S["store"], 16)

        @block.gpsimd
        def _(pool):
            pool.wait_ge(S["bias_row"], 1)
            pool.dma_start(bias_rows, brow[0:24, :]).then_inc(S["brow_out"], 16)
            pool.wait_ge(S["brow_out"], 16)
            for g in range(NG):
                src = bass.AP(bias_rows.tensor, g * NH * 384, [[1, P], [384, NH], [1, T]])
                pool.dma_start(bias[:, :, g, :], src).then_inc(S["bias_in"], 16)
            a, b = ROWS["ln_w"][0], ROWS["ln_b"][1]
            pool.dma_start(rows, A["rows"][a:b].partition_broadcast(P)).then_inc(S["rows_in"], 16)
            pool.wait_ge(S["gn_done"], 1)
            nc.gpsimd.memset(ones, 1.0).then_inc(S["ones_set"], 1)
            pool.dma_start(emb[0:33, :], A["c_emb"]).then_inc(S["f_in"], 16)
            pool.dma_start(fw1[0:33, :], A["filt_w1"]).then_inc(S["f_in"], 16)
            pool.dma_start(fw2[0:64, :], A["filt_w2"]).then_inc(S["f_in"], 16)
            for dst, name in ((fwd, "c_fwd"), (inv, "c_inv"), (decay, "c_decay"), (dist, "c_dist")):
                src = A[name]
                if name == "c_fwd" or name == "c_decay":
                    src = src.rearrange("p (a n) -> p a n", a=2)
                elif name == "c_inv":
                    src = src.rearrange("p (a n) -> p a n", a=4)
                pool.dma_start(dst, src).then_inc(S["f_in"], 16)
            pool.dma_start(w3[0:64, :], A["filt_w3"]).then_inc(S["f_in"], 16)
            a, b = ROWS["lam"]
            pool.dma_start(lamr, A["rows"][a:b].rearrange("(q d) -> q d", q=4).partition_broadcast(P)).then_inc(S["f_in"], 16)
            a, b = ROWS["skip"]
            pool.dma_start(skip, A["rows"][a:b].rearrange("(q d) -> q d", q=2).partition_broadcast(P)).then_inc(S["f_in"], 16)
            a, b = ROWS["post_g"]
            pool.dma_start(postg, A["rows"][a:b].partition_broadcast(P)).then_inc(S["postg_in"], 16)
            pool.dma_start(wr, A["w_router"].rearrange("(k p) e -> p k e", p=P)).then_inc(S["r_in"], 16)
            pool.dma_start(slotsr, A["c_slots"]).then_inc(S["r_in"], 16)
            nc.gpsimd.memset(onesT[0:16, :], 1.0).then_inc(S["ones_set"], 1)
            pool.wait_ge(S["x_evac"], KC)
            pool.wait_ge(S["o_evac"], 8)
            a, b = ROWS["final_g"]
            pool.dma_start(finalg, A["rows"][a:b].partition_broadcast(P)).then_inc(S["fg_in"], 16)
            nc.gpsimd.tensor_copy(XC.rearrange("p k c -> p (k c)"), XE[:, 0:KC * CAP]).then_inc(S["xc_ready"], 1)
            nc.gpsimd.tensor_copy(OC.rearrange("p a t -> p (a t)"), OT[:, 0:T]).then_inc(S["oc_ready"], 1)
            with pool.Fori(1, E) as e:
                pool.wait_ge(S["piece_used"], e * 24 - 8)
                nc.gpsimd.tensor_copy(XC.rearrange("p k c -> p (k c)"), XE[:, bass.ds(e * KC * CAP, KC * CAP)]).then_inc(S["xc_ready"], 1)
                pool.wait_ge(S["sc_mm"], e * 2)
                nc.gpsimd.tensor_copy(OC.rearrange("p a t -> p (a t)"), OT[:, bass.ds(e * T, T)]).then_inc(S["oc_ready"], 1)

        @block.scalar
        def _(act):
            act.dma_start(cols, A["cols"]).then_inc(S["params"], 16)
            act.dma_start(csq, A["c_square"]).then_inc(S["params"], 16)
            act.dma_start(bucketT[0:32, :], A["c_bucket"]).then_inc(S["params"], 16)
            act.dma_start(maskT[0:24, :], A["c_mask"]).then_inc(S["params"], 16)
            act.dma_start(relb[0:32, 0:24], A["rel_bias"]).then_inc(S["params"], 16)
            act.dma_start(lowW, A["low_up"]).then_inc(S["params"], 16)
            act.wait_ge(S["xin"], 16)
            for a in range(TT):
                act.activation(hn[:, a, :], xres[:, a, :], ACT.Square, accum_out=small[:, a:a + 1]).then_inc(S["sq_sum"], 1)
            act.wait_ge(S["mean_in"], 1)
            act.activation(small[:, 2:4], small[:, 2:4], ACT.Sqrt).then_inc(S["root_in"], 1)
            for k in range(KC):
                act.wait_ge(S["hT_ready"], k // 2 + 1)
                act.wait_ge(S["params"], 96)
                act.activation(hT[:, k, :], psum[:, k // 2, (k % 2) * T:(k % 2) * T + T], ACT.Copy, scale=col("pre_g", k)).then_inc(S["hT_evac"], 1)

            def evac(j):
                act.wait_ge(S["proj_ready"], j + 1)
                blk, c, rhs, dst, scale = tiles[j]
                n = T if rhs is not None else 512
                if j == 0:
                    act.wait_ge(S["bias_row"], 1)
                    act.wait_ge(S["brow_out"], 16)
                src = psum[:, bank_of(j), 0:n]
                if j < GATE_TILE:
                    act.activation(dst, src, ACT.Copy, scale=scale).then_inc(S["proj_evac"], 1)
                else:
                    act.activation(dst, src, ACT.Exp, scale=-1.0).then_inc(S["proj_evac"], 1)

            for j in range(ATT_TILES + 1):
                evac(j)
            def exponents(n):
                h, tile = units[n]
                w = NG * P * (tile + 1)
                act.wait_ge(S["neg_max"], n + 1)
                act.activation(LG[:, n % 2, 0:w], LG[:, n % 2, 0:w], ACT.Exp, bias=small[:, 8 + n % 2:9 + n % 2],
                               accum_out=small[:, 10 + n % 2:11 + n % 2]).then_inc(S["expd"], 1)

            def head_out(h):
                r = 64 * (h % 2)
                act.wait_ge(S["o_ready"], h + 1)
                act.activation(oaT[r:r + 64, h // 2, :], psum[r:r + 64, 6, 0:T], ACT.Copy).then_inc(S["o_done"], 1)

            exponents(0)
            evac(ATT_TILES + 1)
            for n in range(NU):
                if n + 1 < NU:
                    exponents(n + 1)
                if n % 2 == 0 and n:
                    head_out(n // 2 - 1)
                evac(ATT_TILES + 2 + n)
            head_out(NH - 1)
            act.wait_ge(S["low_in"], 1)
            act.activation(prT[0:64, 12, :], prT[0:64, 12, :], ACT.Tanh).then_inc(S["low_t"], 1)
            act.wait_ge(S["low_mm"], 1)
            for f in range(FT):
                act.activation(LD[:, f, :], psum[:, f // 2, (f % 2) * T:(f % 2) * T + T], ACT.Exp, scale=-1.0,
                               bias=small[:, 16 + f:17 + f])
                last = act.activation(AA[:, f, :], psum[:, 2 + f // 2, (f % 2) * T:(f % 2) * T + T], ACT.Exp, scale=-1.0,
                                      bias=small[:, 20 + f:21 + f])
            last.then_inc(S["lowexp"], 1)
            evac(PREP_TILE)
            act.wait_ge(S["norm_mm"], 1)
            act.activation(TMP, psum[:, 4:6, :].rearrange("p a (b c) -> p (a b) c", b=2), ACT.Sqrt).then_inc(S["norm_sqrt"], 1)
            evac(PREP_TILE + 1)
            evac(PREP_TILE + 2)
            evac(PREP_TILE + 3)
            evac(PREP_TILE + 4)
            act.wait_ge(S["cs_ready"], 1)
            act.activation(EX1, CS, ACT.Exp).then_inc(S["exps"], 1)
            act.activation(EX2, CS, ACT.Exp, scale=-1.0).then_inc(S["exps"], 1)
            act.wait_ge(S["cs_ready"], 2)
            act.wait_ge(S["exps"], 2)
            act.activation(CS, LD, ACT.Exp).then_inc(S["exps"], 1)
            for j in range(PREP_TILE + 5, GRAM_TILE):
                evac(j)
            act.wait_ge(S["exps"], 3)
            act.wait_ge(S["proj_evac"], GATE_TILE)
            act.activation(ZE, zaT, ACT.Exp, scale=-1.0).then_inc(S["za_exp"], 1)
            act.wait_ge(S["ab_ready"], 1)
            act.activation(KK, zrT, ACT.Exp, scale=-1.0).then_inc(S["zr_exp"], 1)
            for w, dst in enumerate((TB, TK, TV)):
                for a in range(TT):
                    act.wait_ge(S["tok_tr"], 2 * w + a + 1)
                    act.activation(dst[:, a, :], psum[:, 2 * w + a, :], ACT.Copy).then_inc(S["tok_done"], 1)
            evac(GRAM_TILE)
            evac(GRAM_TILE + 1)
            for lev in range(5):
                evac(LEVEL_TILE + lev)
            for c in range(1, NCH):
                act.wait_ge(S["y_mm"], 2 * c + 1)
                a, p0 = c // 2, 64 * (c % 2)
                act.activation(Y1[p0:p0 + 64, a, :].rearrange("p (q r v) -> p r q v", q=4, r=2),
                               psum[p0:p0 + 64, 2:4, 0:256].rearrange("p a (b c) -> p a b c", b=4), ACT.Copy).then_inc(S["y1_done"], 1)
            evac(NORM_TILE)
            evac(NORM_TILE + 1)
            act.wait_ge(S["y_mm"], 2 * NCH)
            act.wait_ge(S["x_done"], NCH - 1)
            for j in range(8):
                act.wait_ge(S["up_mm"], j + 1)
                act.activation(MG[:, j, :], psum[:, j % 4, 0:T], ACT.Copy).then_inc(S["up_done"], 1)
            act.wait_ge(S["mean_in"], 2)
            act.activation(small[:, 64:80], small[:, 64:80], ACT.Sqrt).then_inc(S["root_in"], 1)
            def out1_part(i):
                act.wait_ge(S["out1_mm"], i + 1)
                act.activation(OUT1[:, i % 2, 512 * (i // 2):512 * (i // 2) + 512], psum[:, i, :], ACT.Copy).then_inc(S["out1_sb"], 1)

            def hidden(i):
                act.wait_ge(S["f_arg"], i + 1)
                act.activation(hid[0:64, :], harg[0:64, :], ACT.Sin).then_inc(S["f_hid"], 1)

            def magnitudes(i):
                act.wait_ge(S["f_abs_in"], i + 1)
                if i:
                    act.wait_ge(S["f_norm"], i)
                act.activation(fFa, fF, ACT.Abs).then_inc(S["f_abs"], 1)
                act.activation(fBa, fB, ACT.Abs).then_inc(S["f_abs"], 1)

            hidden(0)
            out1_part(0)
            hidden(1)
            out1_part(1)
            magnitudes(0)
            magnitudes(1)
            out1_part(2)
            magnitudes(2)
            magnitudes(3)
            out1_part(3)
            act.wait_ge(S["out1_sb"], 4)
            for a in range(TT):
                act.activation(SQ[:, a, :], OUT1[:, a, :], ACT.Square, accum_out=small[:, 96 + a:97 + a]).then_inc(S["sq_sum"], 1)
            act.wait_ge(S["mean_in"], 3)
            act.activation(small[:, 98:100], small[:, 98:100], ACT.Sqrt).then_inc(S["root_in"], 1)
            act.wait_ge(S["x1_ready"], 1)
            for a in range(TT):
                act.activation(hn2[:, a, :], xres[:, a, :], ACT.Square, accum_out=small[:, 128 + a:129 + a]).then_inc(S["sq_sum"], 1)
            act.wait_ge(S["mean_in"], 4)
            act.activation(small[:, 130:132], small[:, 130:132], ACT.Sqrt).then_inc(S["root_in"], 1)
            for k in range(4):
                act.wait_ge(S["n2_tr"], k // 2 + 1)
                act.activation(h2T[:, k, :], psum[:, 4 + k // 2, (k % 2) * T:(k % 2) * T + T], ACT.Copy, scale=col("attn_g", k)).then_inc(S["n2_evac"], 1)

            def evac2(j):
                act.wait_ge(S["p2_ready"], j + 1)
                if j == 0:
                    act.wait_ge(S["f_kdone"], 5)
                b = bank2_of(j)
                if j < 12:
                    act.activation(UPR[:, j, 1:T + 1], psum[:, b, 0:T], ACT.Copy).then_inc(S["p2_evac"], 1)
                elif j < 20:
                    dst = (q2T if j < 16 else k2T)[:, j % 4, :]
                    act.activation(dst, psum[:, b, 0:T], ACT.Copy, scale=0.125 if j < 16 else 1.0).then_inc(S["p2_evac"], 1)
                else:
                    act.activation(v2[:, j - 20, :], psum[:, b, :], ACT.Copy).then_inc(S["p2_evac"], 1)

            for j in range(13):
                evac2(j)
            for i in range(6):
                act.wait_ge(S["u_tr"], i + 1)
                act.activation(XU[:, i // 2, i % 2, :], psum[:, 4 + i % 4, :], ACT.Copy).then_inc(S["u_evac"], 1)
            for j in range(13, 20):
                evac2(j)
            act.wait_ge(S["lam_sum"], 1)
            act.activation(small[:, 140:142], small[:, 138:140], ACT.Exp).then_inc(S["lam_exp"], 1)
            act.wait_ge(S["mean_in"], 5)
            act.activation(small[:, 144:160], small[:, 144:160], ACT.Sqrt).then_inc(S["root_in"], 1)
            evac2(20)
            evac2(21)
            for n in range(8):
                act.wait_ge(S["l2_neg"], n + 1)
                for c in range(2):
                    act.activation(LG2[:, n % 2, c, :], LG2[:, n % 2, c, :], ACT.Exp, bias=small[:, 176 + 2 * (n % 2) + c:177 + 2 * (n % 2) + c],
                                   accum_out=small[:, 180 + 2 * (n % 2) + c:181 + 2 * (n % 2) + c]).then_inc(S["l2_exp"], 1)
            act.wait_ge(S["o2_mm"], 8)
            act.activation(OA.rearrange("p a h v -> p a (h v)"), psum[:, 6:8, :], ACT.Copy).then_inc(S["o2_sb"], 1)
            act.wait_ge(S["o2_sb"], 1)
            act.activation(OSQ, OA, ACT.Square).then_inc(S["o2_sq"], 1)
            act.wait_ge(S["mean_in"], 6)
            act.activation(small[:, 192:200], small[:, 192:200], ACT.Sqrt).then_inc(S["root_in"], 1)
            for a in range(TT):
                act.wait_ge(S["x2_ready"], 2 * a + 2)
                act.activation(hf[:, a, :], xres[:, a, :], ACT.Square, accum_out=stat[:, a:a + 1]).then_inc(S["sq_sum"], 1)
            act.wait_ge(S["mean_in"], 7)
            act.activation(stat[:, 2:4], stat[:, 2:4], ACT.Sqrt).then_inc(S["root_in"], 1)
            for k in range(4):
                act.wait_ge(S["n3_tr"], k // 2 + 1)
                act.activation(hfT[:, k, :], psum[:, k // 2, (k % 2) * T:(k % 2) * T + T], ACT.Copy, scale=col("ffn_g", k)).then_inc(S["n3_evac"], 1)
            for a in range(TT):
                act.wait_ge(S["r_neg"], 1)
                act.activation(aff[:, a, :], psum[:, 4, a * E:a * E + E], ACT.Exp, bias=stat[:, 6 + a:7 + a], accum_out=stat[:, 8 + a:9 + a]).then_inc(S["r_exp"], 1)
            for k in range(KC):
                act.wait_ge(S["x_gather"], k + 1)
                dst = XE.rearrange("p (e k c) -> p e k c", e=E, k=KC)[:, :, k, :]
                act.activation(dst, psum[:, k % 4, :].rearrange("p (e c) -> p e c", e=E), ACT.Copy, scale=col("ffn_g", k)).then_inc(S["x_evac"], 1)
            with act.Fori(0, E) as e:
                act.wait_ge(S["piece_used"], e * 24 + 8)
                act.wait_ge(S["h_ready"], e + 1)
                act.activation(GE.rearrange("p (n x) -> p n x", n=2), psum[:, 0:2, 0:HALFQ], ACT.Exp, scale=-1.0).then_inc(S["g_expd"], 1)
                act.wait_ge(S["piece_used"], e * 24 + 24)
                act.wait_ge(S["acc_done"], e * 2 + 1)
                act.activation(YS, psum[:, 4:6, :], ACT.Copy).then_inc(S["y3_sb"], 1)
            act.wait_ge(S["acc_done"], 2 * E + 1)
            for a in range(TT):
                act.activation(hfT.rearrange("p k t -> p (k t)")[:, a * D:a * D + D], xres[:, a, :], ACT.Square, accum_out=small[:, 224 + a:225 + a]).then_inc(S["sq_sum"], 1)
            act.wait_ge(S["mean_in"], 8)
            act.activation(small[:, 226:228], small[:, 226:228], ACT.Sqrt).then_inc(S["root_in"], 1)

        @block.tensor
        def _(pe):
            mm = nc.tensor.matmul
            pe.wait_ge(S["params"], 96)
            mm(psum[0:24, 7, 0:384], relb[0:32, 0:24], bucketT[0:32, :], start=True, stop=True).then_inc(S["bias_mm"], 1)
            pe.wait_ge(S["hn_ready"], 1)
            for k in range(KC):
                for a in range(TT):
                    o = (k % 2) * T + a * P
                    last = nc.tensor.transpose(psum[:, k // 2, o:o + P], hn[:, a, k * P:k * P + P], ident)
                if k % 2:
                    last.then_inc(S["hT_ready"], 1)
            pe.wait_ge(S["bias_row"], 1)
            for k in range(KC):
                for a in range(TT):
                    o = (k % 2) * T + (1 - a) * P
                    last = nc.tensor.transpose(psum[:, 4 + k // 2, o:o + P], hn[:, a, k * P:k * P + P], anti)
                if k % 2:
                    last.then_inc(S["hT_ready"], 1)

            pe.wait_ge(S["hT_evac"], KC)

            def project(j, k0=0, k1=KC):
                blk, c, rhs, dst, scale = tiles[j]
                if k0 == 0:
                    weights_in(pe, blk)
                    if rhs is hR or rhs is None:
                        pe.wait_ge(S["hR_evac"], KC)
                    before = [i for i in range(j) if bank_of(i) == bank_of(j)]
                    if before:
                        pe.wait_ge(S["proj_evac"], before[-1] + 1)
                o = psum[:, bank_of(j), 0:T]
                for k in range(k0, k1):
                    if rhs is not None:
                        last = mm(o, block_of(blk)[:, k, c * P:c * P + P], rhs[:, k, :], start=(k == 0), stop=(k == KC - 1))
                    else:
                        last = mm(psum[:, j % 4, :], hR[:, k, c * P:c * P + P], block_of(blk)[:, k, :], start=(k == 0), stop=(k == KC - 1))
                if k1 == KC:
                    last.then_inc(S["proj_ready"], 1)

            for j in range(ATT_TILES + 1):
                project(j)

            def logits(n):
                h, tile = units[n]
                b = 2 * (n % 2)
                w = P * (tile + 1)
                if n >= 2:
                    pe.wait_ge(S["neg_max"], n - 1)
                r = 64 * (h % 2)
                for g in range(NG):
                    t = 4 * g + h // 2
                    last = mm(psum[:, b + g * w // 512, (g * w) % 512:(g * w) % 512 + w],
                              qT[r:r + 64, t, tile * P:tile * P + P], kT[r:r + 64, t, T - w:T] if tile == 0 else kT[r:r + 64, t, :],
                              start=True, stop=True)
                last.then_inc(S["logit_ready"], 1)

            def turned(n):
                h, tile = units[n]
                pe.wait_ge(S["prob_ready"], n + 1)
                for half in range(tile + 1):
                    i = (n // 2) * 3 + (n % 2) * 2 + half
                    if i >= 2:
                        pe.wait_ge(S["pt_done"], i - 1)
                    for g in range(NG):
                        o = (g * (tile + 1) + half) * P
                        last = nc.tensor.transpose(psum[:, 4 + i % 2, g * P:g * P + P], LG[:, n % 2, o:o + P], ident)
                    last.then_inc(S["pt_ready"], 1)

            def values(n):
                h, tile = units[n]
                r, o = 64 * (h % 2), tile * P
                if tile == 1 and h >= 2:
                    pe.wait_ge(S["o_done"], h - 1)
                for half in range(tile + 1):
                    i = (n // 2) * 3 + (n % 2) * 2 + half
                    pe.wait_ge(S["pt_done"], i + 1)
                    for g in range(NG):
                        u = half if tile else 1
                        last = mm(psum[r:r + 64, 6, o:o + P], vR[:, u, g * AW + h * HD:g * AW + h * HD + HD],
                                  PT[:, i % 2, g, :], start=(g == 0 and half == 0), stop=(g == NG - 1 and half == tile))
                if tile == 0:
                    last.then_inc(S["o_ready"], 1)

            pe.wait_ge(S["proj_evac"], ATT_TILES)
            logits(0)
            logits(1)
            project(ATT_TILES + 1)
            for n in range(NU):
                turned(n)
                if n + 2 < NU:
                    logits(n + 2)
                project(ATT_TILES + 2 + n)
                values(n)

            pe.wait_ge(S["low_t"], 1)
            for f in range(FT):
                mm(psum[:, f // 2, (f % 2) * T:(f % 2) * T + T], lowW[0:64, f * P:f * P + P], prT[0:64, 12, :], start=True, stop=True)
            for f in range(FT):
                last = mm(psum[:, 2 + f // 2, (f % 2) * T:(f % 2) * T + T], lowW[64:128, f * P:f * P + P], prT[64:128, 12, :], start=True, stop=True)
            last.then_inc(S["low_mm"], 1)
            project(PREP_TILE)
            pe.wait_ge(S["sq_ready"], 1)
            pe.wait_ge(S["pt_done"], 24)
            for f in range(FT):
                last = mm(psum[:, 4 + f // 2, (f % 2) * T:(f % 2) * T + T], BLK1, TMP[:, f, :], start=True, stop=True)
            last.then_inc(S["norm_mm"], 1)
            pe.wait_ge(S["o_done"], NH)
            for j in range(PREP_TILE + 1, GRAM_TILE):
                project(j)
            pe.wait_ge(S["proj_evac"], GRAM_TILE)
            pe.wait_ge(S["sq_ready"], 2)
            pe.wait_ge(S["o_done"], NH)
            for a in range(TT):
                for f in range(FT):
                    last = mm(psum[:, 6, a * 8 + 2 * f:a * 8 + 2 * f + 2], CS[:, f, a * P:a * P + P], small[:, 24 + 2 * f:26 + 2 * f], start=True, stop=True)
            last.then_inc(S["bonus_mm"], 1)
            pe.wait_ge(S["ab_ready"], 1)
            pe.wait_ge(S["norm_sqrt"], 1)
            for w, src in enumerate((BT, KT, prT[:, 8:12, :])):
                for a in range(TT):
                    if w == 2:
                        pe.wait_ge(S["tok_done"], 1)
                    for f in range(FT):
                        last = nc.tensor.transpose(psum[:, 2 * w + a, f * P:f * P + P], src[:, f, a * P:a * P + P], ident)
                    last.then_inc(S["tok_tr"], 1)
            pe.wait_ge(S["tok_done"], 6)
            for cp in range(2):
                if cp:
                    project(GRAM_TILE)
                    pe.wait_ge(S["gram_done"], 5)
                for h in range(NH):
                    r, f = 64 * (h % 2), h // 2
                    for c in (2 * cp, 2 * cp + 1):
                        o = 64 * (c % 2)
                        ar = AR[r:r + 64, f, c, :, :].rearrange("p a b -> p (a b)")
                        q = (h // 2) * 128
                        mm(psum[o:o + 64, h % 2, q:q + 128], BT[r:r + 64, f, c * CH:c * CH + CH], ar, start=True, stop=True)
                        last = mm(psum[o:o + 64, 2 + h % 2, q:q + 128], KT[r:r + 64, f, c * CH:c * CH + CH], ar, start=True, stop=True)
                last.then_inc(S["gram_mm"], 1)
                for h in range(NH):
                    r, f = 64 * (h % 2), h // 2
                    for c in (2 * cp, 2 * cp + 1):
                        o = 64 * (c % 2)
                        last = mm(psum[o:o + 64, 4 + h % 2, (h // 2) * 64:(h // 2) * 64 + 64], AR[r:r + 64, f, c, 0, :],
                                  BT[r:r + 64, f, c * CH:c * CH + CH], start=True, stop=True)
                last.then_inc(S["gram_mm"], 1)

            def pairs(bank, lhs, rhs):
                for cp in range(2):
                    for i in range(NH):
                        for p0 in (0, 64):
                            last = mm(psum[p0:p0 + 64, bank + cp, i * CH:i * CH + CH], lhs[p0:p0 + 64, cp, i, :], rhs[p0:p0 + 64, cp, i, :],
                                      start=True, stop=True)
                return last

            project(GRAM_TILE + 1, 0, 4)
            pe.wait_ge(S["gram_done"], 10)
            for cp in range(2):
                for h in range(NH):
                    for p0 in (0, 64):
                        last = mm(psum[p0:p0 + 64, cp, hh(h) * CH:hh(h) * CH + CH], mAk[p0:p0 + 64, cp, hh(h), :],
                                  TV[p0:p0 + 64, cp, h * CH:h * CH + CH], start=True, stop=True)
            last.then_inc(S["xv_mm"], 1)
            project(GRAM_TILE + 1, 4, 8)
            pe.wait_ge(S["xv_done"], 1)
            for lev in range(5):
                pe.wait_ge(S["MM_done"], 2 * lev + 2 if lev else 3)
                pairs(0, mOff, mMT).then_inc(S["T1_mm"], 1)
                project(LEVEL_TILE + lev, 0, 4)
                pe.wait_ge(S["T1_done"], lev + 1)
                pe.wait_ge(S["MM_done"], 2 * lev + 3)
                pairs(2, mM, mT1).then_inc(S["MM_mm"], 1)
                pairs(4, mT1, mM).then_inc(S["MM_mm"], 1)
                project(LEVEL_TILE + lev, 4, 8)
            pe.wait_ge(S["MM_done"], 13)
            pe.wait_ge(S["proj_evac"], NORM_TILE)
            for c in range(NCH):
                cp, p0 = c // 2, 64 * (c % 2)
                if c:
                    pe.wait_ge(S["s_done"], c)
                    for h in range(NH):
                        r, f = 64 * (h % 2), h // 2
                        last = mm(psum[p0:p0 + 64, h % 2, f * CH:f * CH + CH], AR[r:r + 64, f, c, 0, :], ST[r:r + 64, f, :], start=True, stop=True)
                    last.then_inc(S["x_mm"], 1)
                    if c >= 2:
                        pe.wait_ge(S["y1_done"], c - 1)
                    for h in range(NH):
                        r, f = 64 * (h % 2), h // 2
                        last = mm(psum[p0:p0 + 64, 2 + h % 2, f * CH:f * CH + CH], AR[r:r + 64, f, c, 1, :], ST[r:r + 64, f, :], start=True, stop=True)
                    last.then_inc(S["y_mm"], 1)
                    pe.wait_ge(S["x_done"], c)
                else:
                    pe.nop().then_inc(S["y_mm"], 1)
                for h in range(NH):
                    rhs = XS[p0:p0 + 64, hh(h), :] if c else XV[p0:p0 + 64, 0, hh(h), :]
                    last = mm(psum[p0:p0 + 64, 4, hh(h) * CH:hh(h) * CH + CH], mMT[p0:p0 + 64, cp, hh(h), :], rhs, start=True, stop=True)
                last.then_inc(S["u_mm"], 1)
                pe.wait_ge(S["u_done"], c + 1)
                for h in range(NH):
                    r, f = 64 * (h % 2), h // 2
                    mm(psum[r:r + 64, 5, f * CH:f * CH + CH], TB[p0:p0 + 64, cp, h * CH:h * CH + CH], USB[p0:p0 + 64, hh(h), :], start=True, stop=False)
                    last = mm(psum[r:r + 64, 5, f * CH:f * CH + CH], TK[p0:p0 + 64, cp, h * CH:h * CH + CH], TV[p0:p0 + 64, cp, h * CH:h * CH + CH],
                              start=False, stop=True)
                last.then_inc(S["s_mm"], 1)
                for h in range(NH):
                    o = psum[p0:p0 + 64, 6, hh(h) * CH:hh(h) * CH + CH]
                    mm(o, mRb[p0:p0 + 64, cp, hh(h), :], USB[p0:p0 + 64, hh(h), :], start=True, stop=False)
                    last = mm(o, mRk[p0:p0 + 64, cp, hh(h), :], TV[p0:p0 + 64, cp, h * CH:h * CH + CH], start=False, stop=True)
                last.then_inc(S["y_mm"], 1)
            project(NORM_TILE)
            project(NORM_TILE + 1)
            weights_in(pe, "upa")
            pe.wait_ge(S["oa_gated"], 1)
            pe.wait_ge(S["x_done"], NCH - 1)
            pe.wait_ge(S["y1_done"], NCH - 1)
            for j in range(8):
                if j >= 4:
                    pe.wait_ge(S["up_done"], j - 3)
                for f in range(FT):
                    last = mm(psum[:, j % 4, 0:T], wb_up[number["upa"] % NB][:, f, j * P:j * P + P], oaT[:, f, :], start=(f == 0), stop=(f == FT - 1))
                last.then_inc(S["up_mm"], 1)
            pe.wait_ge(S["gn_done"], 1)
            for a in range(TT):
                for f in range(FT):
                    last = nc.tensor.transpose(psum[:, 4 + a, f * P:f * P + P], Y[:, a, f * P:f * P + P], ident)
                last.then_inc(S["or_mm"], 1)
            weights_in(pe, "upr")
            pe.wait_ge(S["or_done"], 2)
            pe.wait_ge(S["up_done"], 8)
            for j in range(8):
                if j >= 4:
                    pe.wait_ge(S["g_done"], j - 3)
                for f in range(FT):
                    last = mm(psum[:, j % 4, 0:T], wb_up[number["upr"] % NB][:, f, j * P:j * P + P], orT[:, f, :], start=(f == 0), stop=(f == FT - 1))
                last.then_inc(S["up_mm"], 1)
            def out1(i, k0=0, k1=KC):
                name = f"out{i // 2}"
                a = i % 2
                if k0 == 0:
                    weights_in(pe, name)
                for k in range(k0, k1):
                    last = mm(psum[:, i, :], MG[:, k, a * P:a * P + P], block_of(name)[:, k, :], start=(k == 0), stop=(k == KC - 1))
                if k1 == KC:
                    last.then_inc(S["out1_mm"], 1)

            def taps(i):
                a, o = i // 2, i % 2
                if i:
                    pe.wait_ge(S["f_abs_in"], i)
                for w in range(2):
                    c0 = (2 * w + o) * 512
                    last = mm(psum[:, 4 + w, :], hid[0:64, a * P:a * P + P], w3[0:64, c0:c0 + 512], start=True, stop=True)
                last.then_inc(S["f_w3mm"], 1)

            def norms(i):
                a, o = i // 2, i % 2
                pe.wait_ge(S["f_abs"], 2 * i + 2)
                mm(psum[:, 6 + o, :], ones, fFa, start=(a == 0), stop=False)
                mm(psum[:, 6 + o, :], ones, fBa, start=False, stop=(a == 1)).then_inc(S["f_norm"], 1)

            pe.wait_ge(S["f_in"], 160)
            pe.wait_ge(S["proj_evac"], NT)
            mm(psum[0:64, 7, 0:T], fw1[0:33, :], emb[0:33, :], start=True, stop=True).then_inc(S["f_mm"], 1)
            pe.wait_ge(S["g_done"], 9)
            out1(0)
            pe.wait_ge(S["f_hid"], 1)
            mm(psum[0:64, 7, 0:T], fw2[0:64, :], hid[0:64, :], start=True, stop=True).then_inc(S["f_mm"], 1)
            out1(1)
            pe.wait_ge(S["f_hid"], 2)
            pe.wait_ge(S["ones_set"], 1)
            taps(0)
            out1(2, 0, 4)
            norms(0)
            taps(1)
            out1(2, 4, 8)
            norms(1)
            taps(2)
            out1(3, 0, 4)
            norms(2)
            taps(3)
            out1(3, 4, 8)
            norms(3)
            pe.wait_ge(S["f_sd"], 4)
            pe.wait_ge(S["out1_sb"], 4)
            for i, (c0, src) in enumerate(((0, fS), (P, fS), (2 * P, fD), (3 * P, fD), (4 * P, fS))):
                if i >= 2:
                    pe.wait_ge(S["f_kdone"], i - 1)
                for o in range(2):
                    for a in range(TT):
                        last = mm(psum[:, 2 * (i % 2) + o, :], fwd[:, a, c0:c0 + P], src[:, a, o, :], start=(a == 0), stop=(a == 1))
                last.then_inc(S["f_kmm"], 1)
            pe.wait_ge(S["hn_ready"], 2)
            for k in range(KC):
                for a in range(TT):
                    o = (k % 2) * T + a * P
                    last = nc.tensor.transpose(psum[:, 4 + k // 2, o:o + P], hn2[:, a, k * P:k * P + P], ident)
                if k % 2:
                    last.then_inc(S["n2_tr"], 1)
            pe.wait_ge(S["f_kdone"], 5)
            pe.wait_ge(S["n2_evac"], 4)
            pe.wait_ge(S["n2_evac2"], 4)

            def project2(j, k0=0, k1=KC):
                b = j // 4 if j < 20 else 5
                name = f"hy{b}" if b < 3 else f"at{b - 3}"
                if k0 == 0:
                    weights_in(pe, name)
                    before = [i for i in range(j) if bank2_of(i) == bank2_of(j)]
                    if before:
                        pe.wait_ge(S["p2_evac"], before[-1] + 1)
                for k in range(k0, k1):
                    if j < 20:
                        last = mm(psum[:, bank2_of(j), 0:T], block_of(name)[:, k, (j % 4) * P:(j % 4) * P + P], h2T[:, k, :], start=(k == 0), stop=(k == KC - 1))
                    else:
                        last = mm(psum[:, bank2_of(j), :], h2T[:, k, (j - 20) * P:(j - 20) * P + P], block_of(name)[:, k, :], start=(k == 0), stop=(k == KC - 1))
                if k1 == KC:
                    last.then_inc(S["p2_ready"], 1)

            for j in range(13):
                project2(j)
            for i in range(6):
                pe.wait_ge(S["u_conv"], i // 2 + 1)
                if i >= 4:
                    pe.wait_ge(S["u_evac"], i - 3)
                for f in range(4):
                    last = nc.tensor.transpose(psum[:, 4 + i % 4, f * P:f * P + P], UC[:, 4 * (i // 2) + f, (i % 2) * P:(i % 2) * P + P], ident)
                last.then_inc(S["u_tr"], 1)
            project2(13)
            for n in range(2):
                z = XU[:, 2, :, :]
                if n == 0:
                    pe.wait_ge(S["u_evac"], 6)
                    pe.wait_ge(S["p2_evac"], 14)
                else:
                    pe.wait_ge(S["z_done"], 1)
                for j, c0 in enumerate((0, P, 5 * P, 3 * P)):
                    for a in range(TT):
                        last = mm(psum[:, j, :], fwd[:, a, c0:c0 + P], z[:, a, :], start=(a == 0), stop=(a == 1))
                last.then_inc(S["z_mm"], 1)
                project2(14 + 3 * n)
                project2(15 + 3 * n)
                pe.wait_ge(S["spec"], n + 1)
                for a in range(TT):
                    for j in range(4):
                        last = mm(psum[:, 4 + a, :], inv[:, j, a * P:a * P + P], SPY[:, j // 2, j % 2, :], start=(j == 0), stop=(j == 3))
                last.then_inc(S["i_mm"], 1)
                project2(16 + 3 * n)
            project2(20)
            pe.wait_ge(S["hy_norm"], 1)
            for f in range(4):
                for a in range(TT):
                    o = (f % 2) * T + a * P
                    last = nc.tensor.transpose(psum[:, 4 + f // 2, o:o + P], ZN[:, a, f * P:f * P + P], ident)
                if f % 2:
                    last.then_inc(S["m_tr"], 1)
            project2(21, 0, 4)
            def logits2(n):
                h, tile = n // 2, n % 2
                if n:
                    pe.wait_ge(S["l2_neg"], n)
                for c in range(2):
                    r = 64 * c
                    last = mm(psum[:, 4 + c, 0:T], q2T[r:r + 64, h, tile * P:tile * P + P], k2T[r:r + 64, h, :], start=True, stop=True)
                last.then_inc(S["l2_mm"], 1)

            def out2(i, k0, k1):
                name = f"out2_{i // 2}"
                a = i % 2
                if k0 == 0:
                    weights_in(pe, name)
                for k in range(k0, k1):
                    last = mm(psum[:, i, :], mixT[:, k, a * P:a * P + P], block_of(name)[:, k, :], start=(k == 0), stop=(k == KC - 1))
                if k1 == KC:
                    last.then_inc(S["x2_mm"], 1)

            pe.wait_ge(S["m_evac"], 4)
            logits2(0)
            project2(21, 4, 8)
            pe.wait_ge(S["p2_evac"], 22)
            for n in range(8):
                if n < 7:
                    logits2(n + 1)
                h, tile = n // 2, n % 2
                pe.wait_ge(S["l2_prob"], n + 1)
                if n:
                    pe.wait_ge(S["l2_turned"], n)
                for s in range(TT):
                    last = nc.tensor.transpose(psum[:, 3, s * P:s * P + P], LG2[:, n % 2, 0, s * P:s * P + P], ident)
                last.then_inc(S["l2_tr"], 1)
                if n < 4:
                    out2(n // 2, 2 * (n % 2), 2 * (n % 2) + 2)
                else:
                    out2(2, n - 4, n - 3)
                pe.wait_ge(S["l2_turned"], n + 1)
                for s in range(TT):
                    last = mm(psum[:, 6 + tile, h * P:h * P + P], PT2[:, n % 2, s, :], v2[:, s, h * P:h * P + P], start=(s == 0), stop=(s == 1))
                last.then_inc(S["o2_mm"], 1)
            out2(3, 0, 4)
            pe.wait_ge(S["o2_norm"], 1)
            for f in range(4):
                for a in range(TT):
                    o = (f % 2) * T + a * P
                    last = nc.tensor.transpose(psum[:, 4 + f // 2, o:o + P], OA[:, a, f, :], ident)
                if f % 2:
                    last.then_inc(S["m2_tr"], 1)
            pe.wait_ge(S["m2_evac"], 4)
            for i in (0, 2, 1, 3):
                out2(i, 4, 8)
            pe.wait_ge(S["hn_ready"], 3)
            for k in range(KC):
                for a in range(TT):
                    o = (k % 2) * T + a * P
                    last = nc.tensor.transpose(psum[:, k // 2, o:o + P], hf[:, a, k * P:k * P + P], ident)
                if k % 2:
                    last.then_inc(S["n3_tr"], 1)
            pe.wait_ge(S["r_in"], 32)
            for a in range(TT):
                for k in range(KC):
                    if k < 4:
                        pe.wait_ge(S["n3_evac"], k + 1)
                    else:
                        pe.wait_ge(S["n3_evac2"], k - 3)
                    last = mm(psum[:, 4, a * E:a * E + E], hfT[:, k, a * P:a * P + P], wr[:, k, :], start=(k == 0), stop=(k == KC - 1))
            last.then_inc(S["r_mm"], 1)
            pe.wait_ge(S["aff_ready"], 1)
            for a in range(TT):
                last = nc.tensor.transpose(psum[0:E, 5, a * P:a * P + P], aff[:, a, :], ident)
            last.then_inc(S["aff_tr"], 1)
            pe.wait_ge(S["rank_ready"], 1)
            for a in range(TT):
                last = nc.tensor.transpose(psum[:, 6, a * E:a * E + E], work[0][0:E, a * P:a * P + P], ident[0:E, 0:E])
            last.then_inc(S["rank_tr"], 1)
            pe.wait_ge(S["ohot_ready"], 1)
            for k in range(KC):
                if k >= 4:
                    pe.wait_ge(S["x_evac"], k - 3)
                for a in range(TT):
                    last = mm(psum[:, k % 4, :], hf[:, a, k * P:k * P + P], ohot[:, a, :, :].rearrange("p e c -> p (e c)"), start=(a == 0), stop=(a == 1))
                last.then_inc(S["x_gather"], 1)
                q = k
                pe.wait_ge(S["og_ready"], q + 1)
                if q >= 4:
                    pe.wait_ge(S["o_evac"], q - 3)
                for i in range(4):
                    e, a = (4 * q + i) // 2, i % 2
                    last = nc.tensor.transpose(psum[:, 4 + q % 4, i * P:i * P + P], og4[:, 2 * (q % 2) + a, e % 2, :], ident)
                last.then_inc(S["o_tr"], 1)
            with pe.Fori(0, E) as e:
                pe.wait_ge(S["xc_ready"], e + 1)
                pe.wait_ge(S["x_evac"], KC)
                pe.wait_ge(S["h_ready"], e + 1)
                for i in range(16):
                    pe.wait_ge(arrived[i % SLOTS], e * 32 + 16 * (i // SLOTS + 1))
                    w = slot(i % SLOTS)
                    k, b = i % 8, 2 * (i // 8)
                    for n in range(2):
                        for j in range(4):
                            c0 = j * QUARTER + n * HALFQ
                            last = mm(psum[32 * j:32 * j + CAP, b + n, 0:HALFQ], XC[:, k, :], w[:, c0:c0 + HALFQ], start=(k == 0), stop=(k == KC - 1))
                    last.then_inc(S["piece_used"], 1)
                pe.wait_ge(S["h_ready"], e + 2)
                pe.wait_ge(S["acc_done"], e * 2 + 1)
                seen = 0
                for i in range(FPP):
                    need = -(-(i + 1) * D // PIECE)
                    while seen < need:
                        pe.wait_ge(arrived[4 + seen], e * 32 + 32)
                        seen += 1
                    g = i % 4
                    for n in range(2):
                        o = 4 * PIECE + i * D + n * 512
                        last = mm(psum[32 * g:32 * g + CAP, 4 + n, :], HT[:, i, :], region(o, 512), start=(i < 4), stop=(i >= FPP - 4))
                    if (i + 1) * D // PIECE > i * D // PIECE:
                        last.then_inc(S["piece_used"], 1)
                pe.wait_ge(S["y3_sb"], e + 1)
                pe.wait_ge(S["oc_ready"], e + 1)
                for a in range(TT):
                    for n in range(2):
                        last = mm(psum[:, (6 if a == 0 else 4) + n, :], OC[:, a, :], YS[:, n, :], start=True, stop=True)
                    last.then_inc(S["sc_mm"], 1)

        @block.vector
        def _(dve):
            V = nc.vector
            link = Line(dve, S["dve_line"])
            dve.wait_ge(S["sq_sum"], 2)
            V.tensor_scalar(small[:, 2:4], small[:, 0:2], 1.0 / D, 1e-6, ALU.mult, ALU.add).then_inc(S["mean_in"], 1)
            dve.wait_ge(S["root_in"], 1)
            link(V.reciprocal(small[:, 4:6], small[:, 2:4]))
            for a in range(TT):
                last = V.tensor_scalar(hn[:, a, :], xres[:, a, :], small[:, 4 + a:5 + a], None, ALU.mult)
            last.then_inc(S["hn_ready"], 1)
            dve.wait_ge(S["params"], 96)
            dve.wait_ge(S["bias_mm"], 1)
            V.tensor_tensor(brow[0:24, :], psum[0:24, 7, 0:384], maskT[0:24, :], ALU.add).then_inc(S["bias_row"], 1)
            V.tensor_scalar(small[:, 16:24], cols[:, COLS["w0"][0]:COLS["a0"][1]], -1.0, None, ALU.mult)
            dve.wait_ge(S["params"], 96)
            for f in range(FT):
                V.tensor_scalar(small[:, 24 + 2 * f:26 + 2 * f], TWO, col("r_k", f), None, ALU.mult)
            for k in range(KC):
                dve.wait_ge(S["hT_ready"], 5 + k // 2)
                V.tensor_scalar(hR[:, k, :], psum[:, 4 + k // 2, (k % 2) * T:(k % 2) * T + T], col("pre_g", k), None, ALU.mult).then_inc(S["hR_evac"], 1)

            def token_shift(i):
                n, t0 = (4, RKV_TILE + 4 * i) if i < 3 else (1, ATT_TILES)
                dve.wait_ge(S["proj_evac"], t0 + n)
                src = prT[:, 4 * i:4 * i + n, :]
                V.tensor_scalar(SHIFT[:, 0:n, 0:1], src[:, :, 0:1], -1.0, None, ALU.mult)
                link(V.tensor_tensor(SHIFT[:, 0:n, 1:T], src[:, :, 0:T - 1], src[:, :, 1:T], ALU.subtract))
                for f in range(n):
                    last = V.scalar_tensor_tensor(src[:, f, :], SHIFT[:, f, :], col("mix", 4 * i + f), src[:, f, :], ALU.mult, ALU.add)
                return last

            def biased(n):
                h, tile = units[n]
                w = P * (tile + 1)
                b = 2 * (n % 2)
                i = n % 2
                dve.wait_ge(S["logit_ready"], n + 1)
                if n >= 2:
                    dve.wait_ge(S["pt_ready"], (n // 2 - 1) * 3 + (2 if n % 2 == 0 else 3))
                src = psum[:, b:b + 2, :].rearrange("p a b -> p (a b)")[:, 0:NG * w].rearrange("p (g u) -> p g u", g=NG)
                dst = LG[:, i, 0:NG * w]
                link(V.tensor_tensor(dst.rearrange("p (g u) -> p g u", g=NG), src, bias[:, h, :, 0:w], ALU.add))
                V.tensor_reduce(small[:, 8 + i:9 + i], dst, AX.X, ALU.max, negate=True).then_inc(S["neg_max"], 1)

            dve.wait_ge(S["bias_in"], 48)
            biased(0)
            for n, (h, tile) in enumerate(units):
                i = n % 2
                dst = LG[:, i, 0:NG * P * (tile + 1)]
                dve.wait_ge(S["expd"], n + 1)
                link(V.reciprocal(small[:, 12 + i:13 + i], small[:, 10 + i:11 + i]))
                V.tensor_scalar(dst, dst, small[:, 12 + i:13 + i], None, ALU.mult).then_inc(S["prob_ready"], 1)
                if n + 1 < NU:
                    biased(n + 1)
                for half in range(tile + 1):
                    q = (n // 2) * 3 + (n % 2) * 2 + half
                    dve.wait_ge(S["pt_ready"], q + 1)
                    V.tensor_copy(PT[:, q % 2, :, :], psum[:, 4 + q % 2, 0:NG * P].rearrange("p (g u) -> p g u", g=NG)).then_inc(S["pt_done"], 1)
                if n == 1:
                    token_shift(3).then_inc(S["low_in"], 1)
                    dve.wait_ge(S["low_in"], 1)
                elif n in (5, 9, 13):
                    link(token_shift(n // 4 - 1))

            r4, k4 = prT[:, 0:4, :], prT[:, 4:8, :]
            for f in range(FT):
                last = V.tensor_scalar(KK[:, f, :], k4[:, f, :], col("k_k", f), None, ALU.mult)
            link(last)
            dve.wait_ge(S["o_ready"], NH)
            V.tensor_tensor(TMP, KK, KK, ALU.mult).then_inc(S["sq_ready"], 1)
            dve.wait_ge(S["lowexp"], 1)
            link(V.tensor_scalar(LD, LD, 1.0, None, ALU.add))
            link(V.reciprocal(LD, LD))
            link(V.tensor_scalar(LD, LD, -E_HALF, None, ALU.mult))
            link(V.tensor_scalar(AA, AA, 1.0, None, ALU.add))
            link(V.reciprocal(AA, AA))
            for f in range(FT):
                last = V.tensor_tensor_scan(CS[:, f, :], CSTART, LD[:, f, :], 0.0, ALU.mult, ALU.add)
            link(last)
            V.tensor_tensor(LD, CS, LD, ALU.subtract).then_inc(S["cs_ready"], 1)
            dve.wait_ge(S["cs_ready"], 1)
            V.memset(small[:, 203:204], 0.0).then_inc(S["cs_ready"], 1)
            dve.wait_ge(S["norm_sqrt"], 1)
            link(V.tensor_scalar(TMP, TMP, 1e-12, None, ALU.max))
            link(V.reciprocal(TMP, TMP))
            link(V.tensor_tensor(KK, KK, TMP, ALU.mult))
            for f in range(FT):
                last = V.tensor_scalar(TMP[:, f, :], AA[:, f, :], 1.0, col("k_a", f), ALU.subtract, ALU.mult)
            link(last)
            link(V.scalar_tensor_tensor(k4, TMP, 1.0, k4, ALU.add, ALU.mult))
            dve.wait_ge(S["exps"], 3)
            arv = AR.rearrange("p f c a t -> p (f c) a t")
            def chunks(x):
                return x.rearrange("p f (c t) -> p (f c) t", c=NCH)
            V.scalar_tensor_tensor(arv[:, :, 0, :], chunks(KK), -1.0, chunks(CS), ALU.mult, ALU.mult)
            V.tensor_tensor(arv[:, :, 1, :], chunks(r4), chunks(EX1), ALU.mult)
            link(V.tensor_tensor(AA, KK, AA, ALU.mult))
            V.tensor_tensor(BT, AA, EX2, ALU.mult)
            V.tensor_tensor(KT, k4, EX2, ALU.mult)
            PC = small[:, 32:48].rearrange("p (f c) -> p f c", f=FT)
            link(V.tensor_copy(PC, EX1.rearrange("p f (c t) -> p f c t", c=NCH)[:, :, :, CH - 1]))
            V.tensor_tensor(CS, r4, k4, ALU.mult).then_inc(S["sq_ready"], 1)
            dve.wait_ge(S["sq_ready"], 2)
            V.memset(small[:, 204:205], 0.0).then_inc(S["ab_ready"], 1)
            dve.wait_ge(S["bonus_mm"], 1)
            link(V.tensor_copy(small[:, 48:64], psum[:, 6, 0:16]))

            def masked(dst, cp, bank, off, step, mask):
                src = psum[:, bank:bank + 2, :].rearrange("p b (q w) -> p b q w", w=step)[:, :, 0:4, off:off + CH]
                return V.tensor_tensor(dst[:, cp, :, :].rearrange("p (b q) w -> p b q w", b=2), src, spread(spread(mask, 1, 4), 1, 2), ALU.mult)
            for cp in range(2):
                dve.wait_ge(S["gram_mm"], 2 * cp + 1)
                masked(mN, cp, 0, 0, 128, US).then_inc(S["gram_done"], 1)
                masked(mRb, cp, 0, 64, 128, UI).then_inc(S["gram_done"], 1)
                masked(mAk, cp, 2, 0, 128, US).then_inc(S["gram_done"], 1)
                masked(mRk, cp, 2, 64, 128, UI).then_inc(S["gram_done"], 1)
                dve.wait_ge(S["gram_mm"], 2 * cp + 2)
                masked(mA, cp, 4, 0, 64, LS).then_inc(S["gram_done"], 1)
            dve.wait_ge(S["gram_done"], 10)

            def gate_group(g):
                e = EG[:, 4 * g:4 * g + 4, :]
                dve.wait_ge(S["proj_evac"], GATE_TILE + 4 * g + 4)
                link(V.tensor_scalar(e, e, 1.0, None, ALU.add))
                link(V.reciprocal(e, e))

            def flat(x):
                return x.rearrange("p a h t -> p (a h) t")
            def over(mask):
                return spread(mask, 1, 16)
            link(V.tensor_tensor(flat(mMT), flat(mN), over(US2), ALU.mult))
            link(V.tensor_tensor(flat(mM), flat(mA), over(LS2), ALU.mult))
            V.tensor_tensor(flat(mMT), flat(mMT), over(I64), ALU.add).then_inc(S["MM_done"], 1)
            V.tensor_tensor(flat(mM), flat(mM), over(I64), ALU.add).then_inc(S["MM_done"], 1)
            V.tensor_tensor(flat(mOff), flat(mA), over(OFFB[0]), ALU.mult).then_inc(S["MM_done"], 1)
            dve.wait_ge(S["xv_mm"], 1)
            V.tensor_copy(XV.rearrange("p a h t -> p a (h t)"), psum[:, 0:2, :]).then_inc(S["xv_done"], 1)
            for lev in range(5):
                dve.wait_ge(S["T1_mm"], lev + 1)
                V.tensor_copy(mT1.rearrange("p a h t -> p a (h t)"), psum[:, 0:2, :]).then_inc(S["T1_done"], 1)
                if lev < 4:
                    link(V.tensor_tensor(flat(mOff), flat(mA), over(OFFB[lev + 1]), ALU.mult))
                if lev == 0:
                    gate_group(0)
                elif lev == 1:
                    gate_group(1)
                elif lev == 2:
                    dve.wait_ge(S["za_exp"], 1)
                    link(V.tensor_scalar(ZE, ZE, 1.0, None, ALU.add))
                    link(V.reciprocal(ZE, ZE))
                elif lev == 3:
                    gate_group(2)
                elif lev == 4:
                    dve.wait_ge(S["o_done"], NH)
                    link(V.tensor_tensor(ZE, zaT, ZE, ALU.mult))
                    V.tensor_tensor(oaT, oaT, ZE, ALU.mult).then_inc(S["oa_gated"], 1)
                dve.wait_ge(S["MM_mm"], 2 * lev + 1)
                V.tensor_tensor(mMT.rearrange("p a h t -> p a (h t)"), psum[:, 2:4, :], mMT.rearrange("p a h t -> p a (h t)"), ALU.add).then_inc(S["MM_done"], 1)
                dve.wait_ge(S["MM_mm"], 2 * lev + 2)
                V.tensor_tensor(mM.rearrange("p a h t -> p a (h t)"), psum[:, 4:6, :], mM.rearrange("p a h t -> p a (h t)"), ALU.add).then_inc(S["MM_done"], 1)
            for c in range(NCH):
                cp, p0 = c // 2, 64 * (c % 2)
                if c:
                    dve.wait_ge(S["x_mm"], c)
                    V.tensor_tensor(XS[p0:p0 + 64, :, :].rearrange("p (b q) w -> p b (q w)", b=2), psum[p0:p0 + 64, 0:2, 0:256],
                                    XV[p0:p0 + 64, cp, :, :].rearrange("p (b q) w -> p b (q w)", b=2), ALU.add).then_inc(S["x_done"], 1)
                dve.wait_ge(S["u_mm"], c + 1)
                V.tensor_copy(USB[p0:p0 + 64, :, :].rearrange("p h t -> p (h t)"), psum[p0:p0 + 64, 4, :]).then_inc(S["u_done"], 1)
                if c == 0:
                    dve.wait_ge(S["zr_exp"], 1)
                    link(V.tensor_scalar(KK, KK, 1.0, None, ALU.add))
                    link(V.reciprocal(KK, KK))
                elif c == 1:
                    link(V.tensor_tensor(zrT, zrT, KK, ALU.mult))
                dve.wait_ge(S["s_mm"], c + 1)
                dS = psum[:, 5, 0:256].rearrange("p (f v) -> p f v", f=FT)
                if c:
                    link(V.tensor_tensor(ST, dS, ST, ALU.add))
                else:
                    link(V.tensor_copy(ST, dS))
                V.tensor_tensor(ST, ST, spread(PC[:, :, c], 2, CH), ALU.mult).then_inc(S["s_done"], 1)
                dve.wait_ge(S["y_mm"], 2 * c + 2)
                yd = Y[p0:p0 + 64, cp, :].rearrange("p (q r v) -> p r q v", q=4, r=2)
                ys = psum[p0:p0 + 64, 6, :].rearrange("p (r q v) -> p r q v", r=2, q=4)
                if c:
                    dve.wait_ge(S["y1_done"], c)
                    y1 = Y1[p0:p0 + 64, cp, :].rearrange("p (q r v) -> p r q v", q=4, r=2)
                    link(V.tensor_tensor(yd, ys, y1, ALU.add))
                else:
                    link(V.tensor_copy(yd, ys))
            Y3 = Y.rearrange("p a (h v) -> p (a h) v", h=NH)
            T3 = YT.rearrange("p a (h v) -> p (a h) v", h=NH)
            mu, var, rs = small[:, 80:96], small[:, 64:80], small[:, 112:128]
            link(V.tensor_reduce(mu, Y3, AX.X, ALU.add))
            link(V.tensor_scalar(mu, mu, 1.0 / HD, None, ALU.mult))
            link(V.tensor_tensor(Y3, Y3, spread(mu, 2, HD), ALU.subtract))
            link(V.tensor_tensor(T3, Y3, Y3, ALU.mult))
            link(V.tensor_reduce(var, T3, AX.X, ALU.add))
            V.tensor_scalar(var, var, 1.0 / HD, 64e-5, ALU.mult, ALU.add).then_inc(S["mean_in"], 1)
            gate_group(3)
            dve.wait_ge(S["root_in"], 2)
            link(V.reciprocal(rs, var))
            link(V.tensor_tensor(Y3, Y3, spread(rs, 2, HD), ALU.mult))
            dve.wait_ge(S["rows_in"], 16)
            link(V.tensor_tensor(Y, Y, spread(rows[:, 0:AW], 1, TT), ALU.mult))
            link(V.tensor_tensor(Y, Y, spread(rows[:, AW:2 * AW], 1, TT), ALU.add))
            link(V.tensor_tensor(T3, TV.rearrange("p a (h v) -> p (a h) v", h=NH), spread(small[:, 48:64], 2, HD), ALU.mult))
            V.tensor_tensor(Y, Y, YT, ALU.add).then_inc(S["gn_done"], 1)
            for a in range(TT):
                dve.wait_ge(S["or_mm"], a + 1)
                V.tensor_tensor(orT[:, :, a * P:a * P + P], psum[:, 4 + a, :].rearrange("p (f t) -> p f t", f=FT), zrT[:, :, a * P:a * P + P],
                                ALU.mult).then_inc(S["or_done"], 1)
            dve.wait_ge(S["up_done"], 8)
            link(V.tensor_tensor(MG, MG, EG[:, 0:8, :], ALU.mult))
            for j in range(8):
                dve.wait_ge(S["up_mm"], j + 9)
                V.tensor_tensor(YR[:, j, :], psum[:, j % 4, 0:T], EG[:, 8 + j, :], ALU.mult).then_inc(S["g_done"], 1)
                if j % 4 == 3:
                    dve.wait_ge(S["g_done"], j + 1)
                    last = V.tensor_tensor(MG[:, j - 3:j + 1, :], MG[:, j - 3:j + 1, :], YR[:, j - 3:j + 1, :], ALU.add)
            last.then_inc(S["g_done"], 1)
            dve.wait_ge(S["f_in"], 160)
            link(V.tensor_tensor(lamr[:, 0, :], lamr[:, 0, :], lamr[:, 1, :], ALU.mult))
            link(V.tensor_tensor(lamr[:, 2, :], lamr[:, 2, :], lamr[:, 3, :], ALU.mult))
            V.tensor_reduce(small[:, 138:139], lamr[:, 0, :], AX.X, ALU.add)
            V.tensor_reduce(small[:, 139:140], lamr[:, 2, :], AX.X, ALU.add).then_inc(S["lam_sum"], 1)
            dve.wait_ge(S["lam_sum"], 1)
            for i in range(2):
                bcol = col("filt_b1" if i == 0 else "filt_b2")
                dve.wait_ge(S["f_mm"], i + 1)
                x, q = harg[0:64, :], hrnd[0:64, :]
                link(V.tensor_scalar(x, psum[0:64, 7, 0:T], bcol[0:64, :], col("filt_freq")[0:64, :], ALU.add, ALU.mult))
                link(V.tensor_scalar(q, x, INV_2PI, MAGIC, ALU.mult, ALU.add))
                link(V.tensor_scalar(q, q, -MAGIC, None, ALU.add))
                link(V.scalar_tensor_tensor(x, q, -PI2_HI, x, ALU.mult, ALU.add))
                link(V.scalar_tensor_tensor(x, q, -PI2_LO, x, ALU.mult, ALU.add))
                V.tensor_scalar(x, x, 3.1415925, -3.1415925, ALU.min, ALU.max).then_inc(S["f_arg"], 1)
            for i in range(4):
                a, o = i // 2, i % 2
                dve.wait_ge(S["f_w3mm"], i + 1)
                if i:
                    dve.wait_ge(S["f_abs"], 2 * i)
                link(V.tensor_tensor(fF, psum[:, 4, :], decay[:, a, :], ALU.mult))
                if a == 0:
                    V.scalar_tensor_tensor(fB, psum[:, 5, :], first, decay[:, a, :], ALU.mult, ALU.mult).then_inc(S["f_abs_in"], 1)
                else:
                    V.tensor_tensor(fB, psum[:, 5, :], decay[:, a, :], ALU.mult).then_inc(S["f_abs_in"], 1)
                dve.wait_ge(S["f_abs_in"], i + 1)
                V.tensor_tensor(fS[:, a, o, :], fF, fB, ALU.add)
                link(V.tensor_tensor(fD[:, a, o, :], fF, fB, ALU.subtract))
                V.memset(small[:, 249:250], 0.0).then_inc(S["f_sd"], 1)
            dve.wait_ge(S["f_norm"], 4)
            link(V.reciprocal(rnorm, psum[:, 6:8, :]))

            def spectrum(i):
                dve.wait_ge(S["f_kmm"], i + 1)
                dst = (Kr[:, 0], Kr[:, 1], Ki[:, 0], Ki[:, 1], KrP)[i]
                V.tensor_tensor(dst, psum[:, 2 * (i % 2):2 * (i % 2) + 2, :], rnorm, ALU.mult).then_inc(S["f_kdone"], 1)

            spectrum(0)
            dve.wait_ge(S["sq_sum"], 4)
            V.tensor_scalar(small[:, 98:100], small[:, 96:98], 1.0 / D, 1e-6, ALU.mult, ALU.add).then_inc(S["mean_in"], 1)
            spectrum(1)
            dve.wait_ge(S["root_in"], 3)
            link(V.reciprocal(small[:, 100:102], small[:, 98:100]))
            dve.wait_ge(S["postg_in"], 16)
            for a in range(TT):
                last = V.scalar_tensor_tensor(OUT1[:, a, :], OUT1[:, a, :], small[:, 100 + a:101 + a], postg, ALU.mult, ALU.mult)
            link(last)
            V.tensor_tensor(xres, xres, OUT1, ALU.add).then_inc(S["x1_ready"], 1)
            spectrum(2)
            dve.wait_ge(S["sq_sum"], 6)
            V.tensor_scalar(small[:, 130:132], small[:, 128:130], 1.0 / D, 1e-6, ALU.mult, ALU.add).then_inc(S["mean_in"], 1)
            spectrum(3)
            dve.wait_ge(S["root_in"], 4)
            link(V.reciprocal(small[:, 132:134], small[:, 130:132]))
            for a in range(TT):
                last = V.tensor_scalar(hn2[:, a, :], xres[:, a, :], small[:, 132 + a:133 + a], None, ALU.mult)
            last.then_inc(S["hn_ready"], 1)
            spectrum(4)
            for k in range(4, KC):
                dve.wait_ge(S["n2_tr"], k // 2 + 1)
                V.tensor_scalar(h2T[:, k, :], psum[:, 4 + k // 2, (k % 2) * T:(k % 2) * T + T], col("attn_g", k), None, ALU.mult).then_inc(S["n2_evac2"], 1)
            link(V.memset(UPR[:, :, 0:1], 0.0))
            link(V.memset(UPR[:, :, T + 1:T + 2], 0.0))
            for g in range(3):
                dve.wait_ge(S["p2_evac"], 4 * g + 4)
                for f in range(4 * g, 4 * g + 4):
                    last = V.tensor_scalar(UC[:, f, :], UPR[:, f, 1:T + 1], col("conv_w", 12 + f), col("conv_b", f), ALU.mult, ALU.add)
                link(last)
                for f in range(4 * g, 4 * g + 4):
                    last = V.scalar_tensor_tensor(UC[:, f, :], UPR[:, f, 0:T], col("conv_w", f), UC[:, f, :], ALU.mult, ALU.add)
                link(last)
                for f in range(4 * g, 4 * g + 4):
                    last = V.scalar_tensor_tensor(UC[:, f, :], UPR[:, f, 2:T + 2], col("conv_w", 24 + f), UC[:, f, :], ALU.mult, ALU.add)
                last.then_inc(S["u_conv"], 1)
            dve.wait_ge(S["f_in"], 160)
            for n in range(2):
                z = XU[:, 2, :, :]
                dve.wait_ge(S["z_mm"], n + 1)
                zr, zi = psum[:, 0:2, :], psum[:, 2:4, :]
                V.tensor_tensor(M1, zr, Kr[:, :, n, :], ALU.mult)
                link(V.tensor_tensor(M2, zi, Ki[:, :, n, :], ALU.mult))
                link(V.tensor_tensor(SPY[:, 0, :, :], M1, M2, ALU.subtract))
                V.tensor_tensor(M1, zr, Ki[:, :, n, :], ALU.mult)
                V.tensor_tensor(M2[:, 0, :], psum[:, 2, :], KrP[:, n, :], ALU.mult)
                link(V.tensor_tensor(M2[:, 1, :], psum[:, 3, :], Kr[:, 1, n, :], ALU.mult))
                V.tensor_tensor(SPY[:, 1, :, :], M1, M2, ALU.add).then_inc(S["spec"], 1)
                dve.wait_ge(S["spec"], n + 1)
                link(V.tensor_tensor(M1, z, spread(skip[:, n, :], 1, TT), ALU.mult))
                dve.wait_ge(S["i_mm"], n + 1)
                link(V.tensor_tensor(M1, psum[:, 4:6, :], M1, ALU.add))
                V.tensor_tensor(z, M1, XU[:, n, :, :], ALU.mult).then_inc(S["z_done"], 1)
            dve.wait_ge(S["z_done"], 2)
            z = XU[:, 2, :, :]
            g3 = lambda x: x.rearrange("p a (h v) -> p (a h) v", v=64)
            link(V.tensor_tensor(M1, z, z, ALU.mult))
            link(V.tensor_reduce(small[:, 160:176], g3(M1), AX.X, ALU.add))
            V.tensor_scalar(small[:, 144:160], small[:, 160:176], 1.0 / 64, 1e-6, ALU.mult, ALU.add).then_inc(S["mean_in"], 1)
            dve.wait_ge(S["root_in"], 5)
            link(V.reciprocal(small[:, 160:176], small[:, 144:160]))
            V.tensor_tensor(g3(ZN), g3(z), spread(small[:, 160:176], 2, 64), ALU.mult).then_inc(S["hy_norm"], 1)
            for f in range(4):
                dve.wait_ge(S["m_tr"], f // 2 + 1)
                V.tensor_scalar(mixT[:, f, :], psum[:, 4 + f // 2, (f % 2) * T:(f % 2) * T + T], col("hy_g", f), None, ALU.mult).then_inc(S["m_evac"], 1)
            dve.wait_ge(S["lam_exp"], 1)
            link(V.tensor_tensor(small[:, 142:143], small[:, 140:141], small[:, 141:142], ALU.subtract))
            link(V.tensor_scalar(small[:, 142:143], small[:, 142:143], 0.2, None, ALU.add))
            link(V.tensor_scalar(small[:, 143:144], col("subln"), 0.8, None, ALU.mult))

            def biased2(n):
                h, tile, i = n // 2, n % 2, n % 2
                dve.wait_ge(S["l2_mm"], n + 1)
                if n >= 2:
                    dve.wait_ge(S["l2_tr"], n - 1)
                L = LG2[:, i, :, :]
                link(V.scalar_tensor_tensor(L, spread(dist[:, tile * T:tile * T + T], 1, 2), -(2.0 ** (-2.0 * (h + 1))),
                                            psum[:, 4:6, 0:T], ALU.mult, ALU.add))
                V.tensor_reduce(small[:, 176 + 2 * i:178 + 2 * i], L, AX.X, ALU.max, negate=True).then_inc(S["l2_neg"], 1)

            biased2(0)
            for n in range(8):
                i = n % 2
                L = LG2[:, i, :, :]
                dve.wait_ge(S["l2_exp"], 2 * n + 2)
                link(V.reciprocal(small[:, 184:186], small[:, 180 + 2 * i:182 + 2 * i]))
                link(V.tensor_tensor(small[:, 185:186], small[:, 185:186], small[:, 142:143], ALU.mult))
                link(V.tensor_scalar(L[:, 1, :], L[:, 1, :], small[:, 185:186], None, ALU.mult))
                V.scalar_tensor_tensor(L[:, 0, :], L[:, 0, :], small[:, 184:185], L[:, 1, :], ALU.mult, ALU.subtract).then_inc(S["l2_prob"], 1)
                if n < 7:
                    biased2(n + 1)
                dve.wait_ge(S["l2_tr"], n + 1)
                V.tensor_copy(PT2[:, i, :, :], psum[:, 3, 0:T].rearrange("p (s t) -> p s t", s=TT)).then_inc(S["l2_turned"], 1)
            dve.wait_ge(S["o2_sq"], 1)
            o3 = lambda x: x.rearrange("p a h v -> p (a h) v")
            link(V.tensor_reduce(small[:, 192:200], o3(OSQ), AX.X, ALU.add))
            V.tensor_scalar(small[:, 192:200], small[:, 192:200], 1.0 / P, 1e-6, ALU.mult, ALU.add).then_inc(S["mean_in"], 1)
            dve.wait_ge(S["root_in"], 6)
            link(V.reciprocal(small[:, 208:216], small[:, 192:200]))
            V.tensor_tensor(o3(OA), o3(OA), spread(small[:, 208:216], 2, P), ALU.mult).then_inc(S["o2_norm"], 1)
            for f in range(4):
                dve.wait_ge(S["m2_tr"], f // 2 + 1)
                V.tensor_scalar(mixT[:, 4 + f, :], psum[:, 4 + f // 2, (f % 2) * T:(f % 2) * T + T], small[:, 143:144], None, ALU.mult).then_inc(S["m2_evac"], 1)
            for count, i in enumerate((0, 2, 1, 3)):
                dve.wait_ge(S["x2_mm"], count + 1)
                x = xres[:, i % 2, 512 * (i // 2):512 * (i // 2) + 512]
                V.tensor_tensor(x, psum[:, i, :], x, ALU.add).then_inc(S["x2_ready"], 1)
            dve.wait_ge(S["sq_sum"], 8)
            V.tensor_scalar(stat[:, 2:4], stat[:, 0:2], 1.0 / D, 1e-6, ALU.mult, ALU.add).then_inc(S["mean_in"], 1)
            dve.wait_ge(S["root_in"], 7)
            link(V.reciprocal(stat[:, 4:6], stat[:, 2:4]))
            for a in range(TT):
                last = V.tensor_scalar(hf[:, a, :], xres[:, a, :], stat[:, 4 + a:5 + a], None, ALU.mult)
            last.then_inc(S["hn_ready"], 1)
            for k in range(4, KC):
                dve.wait_ge(S["n3_tr"], k // 2 + 1)
                V.tensor_scalar(hfT[:, k, :], psum[:, k // 2, (k % 2) * T:(k % 2) * T + T], col("ffn_g", k), None, ALU.mult).then_inc(S["n3_evac2"], 1)
            dve.wait_ge(S["r_mm"], 1)
            V.tensor_reduce(stat[:, 6:8], psum[:, 4, 0:TT * E].rearrange("p (a e) -> p a e", a=TT), AX.X, ALU.max, negate=True).then_inc(S["r_neg"], 1)
            dve.wait_ge(S["r_exp"], 2)
            link(V.reciprocal(stat[:, 10:12], stat[:, 8:10]))
            V.tensor_tensor(aff, aff, spread(stat[:, 10:12], 2, E), ALU.mult).then_inc(S["aff_ready"], 1)
            dve.wait_ge(S["aff_tr"], 1)
            link(V.tensor_copy(affT[0:E, :], psum[0:E, 5, 0:T]))
            src = affT[0:E, :]
            for i in range(CAP // 8):
                link(V.max(top8[0:E, :], src))
                dst = work[i % 2][0:E, :]
                link(V.match_replace(dst, top8[0:E, :], src, -1.0))
                src = dst
            dve.wait_ge(S["ones_set"], 2)
            sel, run = work[0][0:E, :], affT[0:E, :]
            link(V.tensor_scalar(sel, src, 0.0, None, ALU.is_lt))
            link(V.tensor_tensor_scan(run, onesT[0:E, :], sel, 0.0, ALU.mult, ALU.add))
            V.tensor_tensor(sel, sel, run, ALU.mult).then_inc(S["rank_ready"], 1)
            dve.wait_ge(S["rank_tr"], 1)
            link(V.tensor_copy(rank.rearrange("p a e -> p (a e)"), psum[:, 6, 0:TT * E]))
            dve.wait_ge(S["r_in"], 32)
            oe = lambda x: x.rearrange("p a e c -> p (a e) c")
            V.tensor_tensor(oe(ohot), spread(rank.rearrange("p a e -> p (a e)"), 2, CAP), spread(slotsr, 1, TT * E), ALU.is_equal).then_inc(S["ohot_ready"], 1)
            dve.wait_ge(S["ohot_ready"], 1)
            over4 = lambda x: bass.AP(x.tensor, x.offset, [list(x.ap[0]), [0, 4], [0, CAP]])
            for q in range(9):
                if q < 8:
                    if q >= 2:
                        dve.wait_ge(S["o_tr"], q - 1)
                    for a in range(TT):
                        for e in range(2):
                            last = V.tensor_tensor(og4[:, 2 * (q % 2) + a, e, :].rearrange("p (r c) -> p r c", r=4), spread(ohot[:, a, 2 * q + e, :], 1, 4),
                                                   over4(aff[:, a, 2 * q + e:2 * q + e + 1]), ALU.mult)
                    last.then_inc(S["og_ready"], 1)
                if q:
                    dve.wait_ge(S["o_tr"], q)
                    V.tensor_copy(OT[:, 512 * (q - 1):512 * q], psum[:, 4 + (q - 1) % 4, :]).then_inc(S["o_evac"], 1)
            V.memset(small[:, 247:248], 0.0).then_inc(S["h_ready"], 1)
            V.memset(small[:, 246:247], 0.0).then_inc(S["acc_done"], 1)
            with dve.Fori(0, E) as e:
                step = 6
                dve.wait_ge(S["g_expd"], e + 1)
                V.tensor_scalar(GE, GE, 1.0, None, ALU.add).then_inc(S["dve_loop"], 1)
                dve.wait_ge(S["dve_loop"], e * step + 1)
                V.reciprocal(GE, GE).then_inc(S["dve_loop"], 1)
                dve.wait_ge(S["dve_loop"], e * step + 2)
                ge = GE.rearrange("p (n x) -> p n x", n=2)
                V.tensor_tensor(ge, psum[:, 0:2, 0:HALFQ], ge, ALU.mult).then_inc(S["dve_loop"], 1)
                dve.wait_ge(S["dve_loop"], e * step + 3)
                dve.wait_ge(S["piece_used"], e * 24 + 16)
                V.tensor_tensor(ge, psum[:, 2:4, 0:HALFQ], ge, ALU.mult).then_inc(S["dve_loop"], 1)
                dve.wait_ge(S["dve_loop"], e * step + 4)
                V.tensor_copy(HP, GE.rearrange("p (q i) -> p i q", i=FPP)).then_inc(S["dve_loop"], 1)
                dve.wait_ge(S["dve_loop"], e * step + 5)
                V.transpose(HT.rearrange("p i c -> p (i c)"), HP.rearrange("p i c -> p (i c)")).then_inc(S["h_ready"], 1)
                for a in range(TT):
                    dve.wait_ge(S["sc_mm"], e * 2 + (a + 1))
                    x = xres[:, a, :].rearrange("p (n x) -> p n x", n=2)
                    b = 6 if a == 0 else 4
                    V.tensor_tensor(x, psum[:, b:b + 2, :], x, ALU.add).then_inc(S["acc_done"], 1)
                V.memset(small[:, 248:249], 0.0).then_inc(S["dve_loop"], 1)
                dve.wait_ge(S["h_ready"], e + 2)
                dve.wait_ge(S["acc_done"], e * 2 + 3)
            dve.wait_ge(S["sq_sum"], 10)
            V.tensor_scalar(small[:, 226:228], small[:, 224:226], 1.0 / D, 1e-6, ALU.mult, ALU.add).then_inc(S["mean_in"], 1)
            dve.wait_ge(S["root_in"], 8)
            link(V.reciprocal(small[:, 228:230], small[:, 226:228]))
            dve.wait_ge(S["fg_in"], 16)
            for a in range(TT):
                V.scalar_tensor_tensor(xres[:, a, :], xres[:, a, :], small[:, 228 + a:229 + a], finalg, ALU.mult, ALU.mult).then_inc(S["out_ready"], 1)


def kernel(**inputs):
    import numpy as _np
    import concourse.bacc as _bacc
    from concourse import mybir as _mybir
    from concourse.bass_utils import run_bass_kernel_spmd as _run

    i = {k: _np.asarray(v) for k, v in inputs.items()}
    pc = lambda a: a.reshape(-1, 128).T
    half = lambda a: _np.concatenate([a.reshape(-1, 1), _np.zeros((64, 1), _np.float32)])
    cols = _np.concatenate([pc(i["pre_norm_gain"]), pc(i["rwkv_shift_mix"]), pc(i["rwkv_w0"]), pc(i["rwkv_a0"]), pc(i["rwkv_k_k"]),
                            pc(i["rwkv_k_a"]), pc(i["rwkv_r_k"]), pc(i["attn_norm_g_2"]), pc(i["conv_w_2"]), pc(i["conv_b_2"]),
                            pc(i["subln_g_2"]), pc(i["ffn_norm_g_2"]), pc(i["hyena_norm_g_2"]), half(i["filt_b1_2"]),
                            half(i["filt_b2_2"]), half(i["filt_freq_2"])], axis=1)
    rows = _np.concatenate([i[n].reshape(-1) for n in ("post_norm_gain", "rwkv_ln_w", "rwkv_ln_b", "hyena_skip_2", "final_norm_g_2",
                                                       "lambda_q1_2", "lambda_k1_2", "lambda_q2_2", "lambda_k2_2")])
    arrays = {"x": i["x"][0], "cols": cols, "rows": rows, "low_up": _np.concatenate([i["rwkv_w_up"][0], i["rwkv_a_up"][0]]),
              "rel_bias": i["rel_bias"], "w_in": i["w_in"][0], "w_up_attn": i["w_up_attn"][0], "w_up_rwkv": i["w_up_rwkv"][0],
              "w_out": i["w_out"][0], "w_in_2": i["w_in_2"][0], "w_out_2": i["w_out_2"][0], "filt_w1": i["filt_w1_2"][0],
              "filt_w2": i["filt_w2_2"][0], "filt_w3": i["filt_w3_2"][0], "w_router": i["w_router_2"][0],
              "w_gate": i["w_gate_2"][0], "w_up": i["w_up_2"][0], "w_down": i["w_down_2"][0]}
    arrays.update(constants())
    nc = _bacc.Bacc("TRN2", target_bir_lowering=False, num_devices=1)
    A, feed = {}, {}
    for name, a in arrays.items():
        a = _np.ascontiguousarray(a)
        feed["in_" + name] = a
        A[name] = nc.dram_tensor("in_" + name, a.shape, _mybir.dt.from_np(a.dtype), kind="ExternalInput").ap()
    out = nc.dram_tensor("out_0", (T, D), F32, kind="ExternalOutput").ap()
    program(nc, A, out)
    r = _run(nc, [feed], core_ids=[0])
    return r.results[0]["out_0"].reshape(1, T, D)
```
